# Optimizing a Trainium2 kernel written in Bass

```python
import jax, jax.numpy as jnp
from jax import lax
import numpy as np

D_MODEL = 1024
BATCH = 1
SEQ = 1024
DEPTH = 1
DEC_BATCH = 1
DEC_SEQ = 64
PAST_LEN = 512

CHUNK = 64
D_MIX = D_MODEL
D_CONV = D_MIX // 4
D_ATT = D_MIX // 2
D_SC = D_MIX - D_CONV - D_ATT
N_HEADS_B = 8
HEAD_DIM_B = D_ATT // N_HEADS_B
CONV_A_WIDTH = 31
CONV_C_WIDTH = 3
BAND_CHUNKS = 8
BAND_PAST = BAND_CHUNKS * CHUNK
REL_CLIP = 128
N_REL = 2 * REL_CLIP + 1
N_MEM = 256
N_HEADS_X = 4
HEAD_DIM_X = D_MODEL // N_HEADS_X
D_FF = 4 * D_MODEL
EPS = 1e-6
NEG = -1e30
IN_COLS = 2 * D_CONV + 3 * D_ATT + 3 * D_SC
SPLITS = (D_CONV, 2 * D_CONV, 2 * D_CONV + D_ATT, 2 * D_CONV + 2 * D_ATT, 2 * D_CONV + 3 * D_ATT,
          2 * D_CONV + 3 * D_ATT + D_SC, 2 * D_CONV + 3 * D_ATT + 2 * D_SC)

kernel_name = 'hybrid_streaming_encoder_step'

def rmsnorm(x, g):
    xf = x.astype(jnp.float32)
    y = xf * lax.rsqrt(jnp.mean(xf * xf, axis=-1, keepdims=True) + EPS)
    return (y * g.astype(jnp.float32)).astype(x.dtype)

def layernorm(x, g, b):
    xf = x.astype(jnp.float32)
    mu = jnp.mean(xf, axis=-1, keepdims=True)
    var = jnp.mean(jnp.square(xf - mu), axis=-1, keepdims=True)
    y = (xf - mu) * lax.rsqrt(var + EPS) * g.astype(jnp.float32) + b.astype(jnp.float32)
    return y.astype(x.dtype)

def causal_dwconv(u_ext, w):
    return lax.conv_general_dilated(u_ext, w[:, None, :].astype(u_ext.dtype), window_strides=(1,),
                                    padding='VALID', dimension_numbers=('NWC', 'WIO', 'NWC'),
                                    feature_group_count=u_ext.shape[-1])

def chunk_band_attention(qc, kb, vb, key_valid, rel_bias, offset):
    nq, nk = qc.shape[2], kb.shape[2]
    rel = offset + jnp.arange(nq)[:, None] - jnp.arange(nk)[None, :]
    idx = jnp.clip(rel, -REL_CLIP, REL_CLIP) + REL_CLIP
    bias = rel_bias[:, idx].astype(jnp.float32)
    s = jnp.einsum('bnqhd,bnkhd->bnhqk', qc, kb).astype(jnp.float32) * (HEAD_DIM_B ** -0.5) + bias[None, None]
    s = jnp.where(key_valid[None, :, None, None, :], s, NEG)
    p = jax.nn.softmax(s, axis=-1).astype(vb.dtype)
    return jnp.einsum('bnhqk,bnkhd->bnqhd', p, vb)

def hybrid_mixer(xn, ctx_a, ctx_c, k_past, v_past, w_in, conv_a_w, conv_a_b, ln_a_g, ln_a_b,
                 q_norm, k_norm, rel_bias, conv_c_w, out_norm, w_out):
    bsz, t, _ = xn.shape
    z = xn @ w_in
    a_val, a_gate, q, k, v, g_b, g_c, h_c = jnp.split(z, SPLITS, axis=-1)
    u_a = a_val * jax.nn.sigmoid(a_gate)
    ua_ext = jnp.concatenate([ctx_a, u_a], axis=1)
    y_a = jax.nn.silu(layernorm(causal_dwconv(ua_ext, conv_a_w) + conv_a_b, ln_a_g, ln_a_b))
    new_a = ua_ext[:, -(CONV_A_WIDTH - 1):]
    uc_ext = jnp.concatenate([ctx_c, g_c * h_c], axis=1)
    y_c = g_b * causal_dwconv(uc_ext, conv_c_w)
    new_c = uc_ext[:, -(CONV_C_WIDTH - 1):]
    q = rmsnorm(q.reshape(bsz, t, N_HEADS_B, HEAD_DIM_B), q_norm)
    k = rmsnorm(k.reshape(bsz, t, N_HEADS_B, HEAD_DIM_B), k_norm)
    v = v.reshape(bsz, t, N_HEADS_B, HEAD_DIM_B)
    if k_past is None:
        nc = t // CHUNK
        qc = q.reshape(bsz, nc, CHUNK, N_HEADS_B, HEAD_DIM_B)
        pad = jnp.zeros((bsz, BAND_PAST, N_HEADS_B, HEAD_DIM_B), k.dtype)
        kp = jnp.concatenate([pad, k], axis=1).reshape(bsz, nc + BAND_CHUNKS, CHUNK, N_HEADS_B, HEAD_DIM_B)
        vp = jnp.concatenate([pad, v], axis=1).reshape(bsz, nc + BAND_CHUNKS, CHUNK, N_HEADS_B, HEAD_DIM_B)
        band_idx = jnp.arange(nc)[:, None] + jnp.arange(BAND_CHUNKS + 1)[None, :]
        kb = kp[:, band_idx].reshape(bsz, nc, (BAND_CHUNKS + 1) * CHUNK, N_HEADS_B, HEAD_DIM_B)
        vb = vp[:, band_idx].reshape(bsz, nc, (BAND_CHUNKS + 1) * CHUNK, N_HEADS_B, HEAD_DIM_B)
        valid = jnp.repeat(band_idx >= BAND_CHUNKS, CHUNK, axis=1)
        o = chunk_band_attention(qc, kb, vb, valid, rel_bias, BAND_PAST).reshape(bsz, t, D_ATT)
        keep = min(BAND_PAST, t)
        new_k, new_v = k[:, -keep:], v[:, -keep:]
    else:
        past = k_past.shape[1]
        kb = jnp.concatenate([k_past, k], axis=1)
        vb = jnp.concatenate([v_past, v], axis=1)
        valid = jnp.ones((1, past + t), dtype=bool)
        o = chunk_band_attention(q[:, None], kb[:, None], vb[:, None], valid, rel_bias, past).reshape(bsz, t, D_ATT)
        keep = min(BAND_PAST, past + t)
        new_k, new_v = kb[:, -keep:], vb[:, -keep:]
    y = jnp.concatenate([rmsnorm(y_a, out_norm[:D_CONV]),
                         rmsnorm(o, out_norm[D_CONV:D_CONV + D_ATT]),
                         rmsnorm(y_c, out_norm[D_CONV + D_ATT:])], axis=-1)
    return y @ w_out, new_a, new_k, new_v, new_c

def memory_kv(mem, norm_mem, w_xk, w_xv, xk_norm):
    bsz = mem.shape[0]
    mn = rmsnorm(mem, norm_mem)
    mk = rmsnorm((mn @ w_xk).reshape(bsz, N_MEM, N_HEADS_X, HEAD_DIM_X), xk_norm)
    mv = (mn @ w_xv).reshape(bsz, N_MEM, N_HEADS_X, HEAD_DIM_X)
    return mk, mv

def cross_attention(xn, mk, mv, w_xq, xq_norm, w_xo):
    bsz, t, _ = xn.shape
    q = rmsnorm((xn @ w_xq).reshape(bsz, t, N_HEADS_X, HEAD_DIM_X), xq_norm)
    s = jnp.einsum('bqhd,bkhd->bhqk', q, mk).astype(jnp.float32) * (HEAD_DIM_X ** -0.5)
    p = jax.nn.softmax(s, axis=-1).astype(mv.dtype)
    o = jnp.einsum('bhqk,bkhd->bqhd', p, mv).reshape(bsz, t, N_HEADS_X * HEAD_DIM_X)
    return o @ w_xo

def sq_relu_mlp(xn, w_up, w_down):
    return jnp.square(jax.nn.relu(xn @ w_up)) @ w_down

def setup_inputs(seed: int = 0) -> dict:
    key = jax.random.key(seed)
    keys = list(jax.random.split(key, 48))

    def nrm(shape, scale):
        return scale * jax.random.normal(keys.pop(), shape, jnp.float32)

    kv_len = min(BAND_PAST, PAST_LEN)
    d = D_MODEL
    return {
        'x_prompt': nrm((BATCH, SEQ, d), 1.0),
        'x_sample': nrm((DEC_BATCH, DEC_SEQ, d), 1.0),
        'cache_conv_a': nrm((DEPTH, DEC_BATCH, CONV_A_WIDTH - 1, D_CONV), 0.5),
        'cache_band_k': nrm((DEPTH, DEC_BATCH, kv_len, N_HEADS_B, HEAD_DIM_B), 1.0),
        'cache_band_v': nrm((DEPTH, DEC_BATCH, kv_len, N_HEADS_B, HEAD_DIM_B), 1.0),
        'cache_conv_c': nrm((DEPTH, DEC_BATCH, CONV_C_WIDTH - 1, D_SC), 1.0),
        'cache_mem_k': nrm((DEPTH, DEC_BATCH, N_MEM, N_HEADS_X, HEAD_DIM_X), 1.0),
        'cache_mem_v': nrm((DEPTH, DEC_BATCH, N_MEM, N_HEADS_X, HEAD_DIM_X), 1.0),
        'mem_prompt': nrm((BATCH, N_MEM, d), 1.0),
        'norm_mix': 1.0 + nrm((DEPTH, d), 0.02),
        'w_in': nrm((DEPTH, d, IN_COLS), d ** -0.5),
        'conv_a_w': nrm((DEPTH, CONV_A_WIDTH, D_CONV), CONV_A_WIDTH ** -0.5),
        'conv_a_b': nrm((DEPTH, D_CONV), 0.02),
        'ln_a_g': 1.0 + nrm((DEPTH, D_CONV), 0.02),
        'ln_a_b': nrm((DEPTH, D_CONV), 0.02),
        'q_norm': 1.0 + nrm((DEPTH, HEAD_DIM_B), 0.02),
        'k_norm': 1.0 + nrm((DEPTH, HEAD_DIM_B), 0.02),
        'rel_bias': nrm((DEPTH, N_HEADS_B, N_REL), 0.1),
        'conv_c_w': nrm((DEPTH, CONV_C_WIDTH, D_SC), CONV_C_WIDTH ** -0.5),
        'out_norm': 1.0 + nrm((DEPTH, D_MIX), 0.02),
        'w_out': nrm((DEPTH, D_MIX, d), D_MIX ** -0.5),
        'norm_x': 1.0 + nrm((DEPTH, d), 0.02),
        'norm_mem': 1.0 + nrm((DEPTH, d), 0.02),
        'w_xq': nrm((DEPTH, d, N_HEADS_X * HEAD_DIM_X), d ** -0.5),
        'w_xk': nrm((DEPTH, d, N_HEADS_X * HEAD_DIM_X), d ** -0.5),
        'w_xv': nrm((DEPTH, d, N_HEADS_X * HEAD_DIM_X), d ** -0.5),
        'xq_norm': 1.0 + nrm((DEPTH, HEAD_DIM_X), 0.02),
        'xk_norm': 1.0 + nrm((DEPTH, HEAD_DIM_X), 0.02),
        'w_xo': nrm((DEPTH, N_HEADS_X * HEAD_DIM_X, d), (N_HEADS_X * HEAD_DIM_X) ** -0.5),
        'norm_ff': 1.0 + nrm((DEPTH, d), 0.02),
        'w_up': nrm((DEPTH, d, D_FF), d ** -0.5),
        'w_down': nrm((DEPTH, D_FF, d), D_FF ** -0.5),
    }

def reference(x_prompt, x_sample, cache_conv_a, cache_band_k, cache_band_v, cache_conv_c,
              cache_mem_k, cache_mem_v, mem_prompt, norm_mix, w_in, conv_a_w, conv_a_b, ln_a_g, ln_a_b,
              q_norm, k_norm, rel_bias, conv_c_w, out_norm, w_out, norm_x, norm_mem, w_xq, w_xk, w_xv,
              xq_norm, xk_norm, w_xo, norm_ff, w_up, w_down):
    yp, ys = x_prompt, x_sample
    bp = x_prompt.shape[0]
    ca_p, kb_p, vb_p, cc_p, mk_p, mv_p = [], [], [], [], [], []
    ca_s, kb_s, vb_s, cc_s = [], [], [], []
    for l in range(DEPTH):
        mix_w = (w_in[l], conv_a_w[l], conv_a_b[l], ln_a_g[l], ln_a_b[l], q_norm[l], k_norm[l],
                 rel_bias[l], conv_c_w[l], out_norm[l], w_out[l])
        ctx_a0 = jnp.zeros((bp, CONV_A_WIDTH - 1, D_CONV), yp.dtype)
        ctx_c0 = jnp.zeros((bp, CONV_C_WIDTH - 1, D_SC), yp.dtype)
        h, sa, sk, sv, sc = hybrid_mixer(rmsnorm(yp, norm_mix[l]), ctx_a0, ctx_c0, None, None, *mix_w)
        yp = yp + h
        mk, mv = memory_kv(mem_prompt, norm_mem[l], w_xk[l], w_xv[l], xk_norm[l])
        yp = yp + cross_attention(rmsnorm(yp, norm_x[l]), mk, mv, w_xq[l], xq_norm[l], w_xo[l])
        yp = yp + sq_relu_mlp(rmsnorm(yp, norm_ff[l]), w_up[l], w_down[l])
        ca_p.append(sa); kb_p.append(sk); vb_p.append(sv); cc_p.append(sc); mk_p.append(mk); mv_p.append(mv)
        h, sa, sk, sv, sc = hybrid_mixer(rmsnorm(ys, norm_mix[l]), cache_conv_a[l], cache_conv_c[l],
                                         cache_band_k[l], cache_band_v[l], *mix_w)
        ys = ys + h
        ys = ys + cross_attention(rmsnorm(ys, norm_x[l]), cache_mem_k[l], cache_mem_v[l], w_xq[l], xq_norm[l], w_xo[l])
        ys = ys + sq_relu_mlp(rmsnorm(ys, norm_ff[l]), w_up[l], w_down[l])
        ca_s.append(sa); kb_s.append(sk); vb_s.append(sv); cc_s.append(sc)
    return (yp, ys,
            jnp.stack(ca_p), jnp.stack(kb_p), jnp.stack(vb_p), jnp.stack(cc_p), jnp.stack(mk_p), jnp.stack(mv_p),
            jnp.stack(ca_s), jnp.stack(kb_s), jnp.stack(vb_s), jnp.stack(cc_s))


_drawn_inputs = setup_inputs


def setup_inputs(seed=0):
    import zlib

    import numpy as np

    out = dict(_drawn_inputs(seed))
    spreads = {}
    factors = {'conv_a_b': 3.903,
     'ln_a_g': 6.466,
     'ln_a_b': 7.412,
     'q_norm': 5.458,
     'k_norm': 3.604,
     'out_norm': 3.603,
     'norm_x': 8.0,
     'norm_mem': 2.797,
     'xq_norm': 8.0,
     'xk_norm': 2.901,
     'norm_ff': 3.803}
    for name, (base, spread) in spreads.items():
        noise = np.random.default_rng([zlib.crc32(name.encode()), seed]).standard_normal(out[name].shape)
        drawn = base * np.exp(spread * noise) if base else spread * noise
        out[name] = __import__('jax').numpy.asarray(drawn.astype(out[name].dtype))
    for name, factor in factors.items():
        out[name] = (out[name] * factor).astype(out[name].dtype)
    return out
```

```python
from contextlib import ExitStack

import numpy as np

import concourse.bass as bass
from concourse import mybir

F32 = mybir.dt.float32
F32R = mybir.dt.float32r
ACT = mybir.ActivationFunctionType
ALU = mybir.AluOpType
AX = mybir.AxisListType

P = 128
D = 1024
KT = D // P
SEQ, DEC = 1024, 64
NCH = 3
CH = 364
T = NCH * CH
TOK = SEQ + DEC
NMEM = 256
CA = 30
CC = 2
EPS = 1e-6
BIG = 1e30
BLK = [128 * b for b in range(8)] + [T - 128]
BC = [(0, 384, (0, 1, 2)), (384, 768, (3, 4, 5)), (768, T, (6, 7, 8))]

_cols = {}
_n = 0
for _name, _w in (("norm_mix", 8), ("norm_x", 8), ("norm_ff", 8), ("norm_mem", 8), ("out_norm", 8),
                  ("ln_a_g", 2), ("ln_a_b", 2), ("conv_a_b", 2), ("conv_a_w", 62), ("conv_c_w", 6),
                  ("q_norm", 1), ("k_norm", 1), ("xq_norm", 2), ("xk_norm", 2)):
    _cols[_name] = _n
    _n += _w
NPAR = _n

S_MEM, S_IN, S_OUT, S_XQ, S_XO, S_UP = 0, 16, 38, 46, 54, 62
N_SLABS = 126
N_G = 8

IN_ORDER = [0, 2, 1, 3, 18, 20, 16, 19, 21, 17] + list(range(4, 16))
TAPS = {4: 4, 5: 3, 6: 3, 7: 5, 8: 3, 9: 3, 10: 6, 11: 5, 12: 4, 13: 5, 14: 6, 15: 5, 16: 5, 17: 5}


class Semaphores:

    def __init__(self, sem):
        self.params_in = sem("params_in")
        self.mem_in = sem("mem_in")
        self.x_in = sem("x_in")
        self.w_in0 = sem("w_in0")
        self.w_in1 = sem("w_in1")
        self.w_hi = sem("w_hi")
        self.w_lo = sem("w_lo")
        self.zero_ready = sem("zero_ready")
        self.const_ready = sem("const_ready")
        self.pad_ready = sem("pad_ready")
        self.tile_done = sem("tile_done")
        self.tile_read = sem("tile_read")
        self.stat_done = sem("stat_done")
        self.stat_read = sem("stat_read")
        self.rc_done = sem("rc_done")
        self.bc_done = sem("bc_done")
        self.bc_used = sem("bc_used")
        self.a_hi = sem("a_hi")
        self.a_lo = sem("a_lo")
        self.sq_done = sem("sq_done")
        self.acc_done = sem("acc_done")
        self.acc_zero = sem("acc_zero")
        self.q_hi = sem("q_hi")
        self.q_lo = sem("q_lo")
        self.mem_hi = sem("mem_hi")
        self.mem_lo = sem("mem_lo")
        self.mem_sq = sem("mem_sq")
        self.mem_sum = sem("mem_sum")
        self.mem_qhi = sem("mem_qhi")
        self.mem_qlo = sem("mem_qlo")
        self.kq_sq = sem("kq_sq")
        self.kq_hi = sem("kq_hi")
        self.kq_lo = sem("kq_lo")
        self.ck_rc = sem("ck_rc")
        self.mk_bc = sem("mk_bc")
        self.mk_norm = sem("mk_norm")
        self.mv_tr = sem("mv_tr")
        self.mv_cp = sem("mv_cp")
        self.mem_stored = sem("mem_stored")
        self.sig_done = sem("sig_done")
        self.ue_done = sem("ue_done")
        self.ctx_in = sem("ctx_in")
        self.state_out = sem("state_out")
        self.conv_step = sem("conv_step")
        self.uc_done = sem("uc_done")
        self.c3_done = sem("c3_done")
        self.yc_done = sem("yc_done")
        self.g_sq = sem("g_sq")
        self.g_sum = sem("g_sum")
        self.g_hi = sem("g_hi")
        self.g_lo = sem("g_lo")
        self.xa_hi = sem("xa_hi")
        self.xa_lo = sem("xa_lo")
        self.xa_sub = sem("xa_sub")
        self.xa_nrm = sem("xa_nrm")
        self.ya_sig = sem("ya_sig")
        self.ya_done = sem("ya_done")
        self.gn_done = sem("gn_done")
        self.qk_sq = sem("qk_sq")
        self.qk_hi = sem("qk_hi")
        self.qk_lo = sem("qk_lo")
        self.bx_in = sem("bx_in")
        self.bx_done = sem("bx_done")
        self.ext_out = sem("ext_out")
        self.rep_out = sem("rep_out")
        self.bias_in = sem("bias_in")
        self.bias_ready = sem("bias_ready")
        self.cache_in = sem("cache_in")
        self.cache_out = sem("cache_out")
        self.kv_out = sem("kv_out")
        self.cq_rc = sem("cq_rc")
        self.gq_ready = sem("gq_ready")
        self.rx_ready = sem("rx_ready")
        self.q_nrm = sem("q_nrm")
        self.k_nrm = sem("k_nrm")
        self.qk2_hi = sem("qk2_hi")
        self.qk2_lo = sem("qk2_lo")
        self.kc_hi = sem("kc_hi")
        self.kc_lo = sem("kc_lo")
        self.v_hi = sem("v_hi")
        self.v_lo = sem("v_lo")
        self.s_done = sem("s_done")
        self.ttr_done = sem("ttr_done")
        self.exp_done = sem("exp_done")
        self.rec_done = sem("rec_done")
        self.p_ready = sem("p_ready")
        self.t_done = sem("t_done")
        self.pt_hi = sem("pt_hi")
        self.pt_lo = sem("pt_lo")
        self.pv_done = sem("pv_done")
        self.o_used = sem("o_used")
        self.o_sq = sem("o_sq")
        self.o_sum = sem("o_sum")
        self.o_nrm = sem("o_nrm")
        self.b_hi = sem("b_hi")
        self.b_lo = sem("b_lo")
        self.x2_in = sem("x2_in")
        self.y1_out = sem("y1_out")
        self.xs_sq = sem("xs_sq")
        self.xs_sum = sem("xs_sum")
        self.xkv_in = sem("xkv_in")
        self.xkv_hi = sem("xkv_hi")
        self.xkv_lo = sem("xkv_lo")
        self.xq_hi = sem("xq_hi")
        self.xq_lo = sem("xq_lo")
        self.x_s = sem("x_s")
        self.x_min = sem("x_min")
        self.x_exp = sem("x_exp")
        self.x_rec = sem("x_rec")
        self.x_p = sem("x_p")
        self.x_t = sem("x_t")
        self.x_pthi = sem("x_pthi")
        self.x_ptlo = sem("x_ptlo")
        self.x_pv = sem("x_pv")
        self.x_ohi = sem("x_ohi")
        self.x_olo = sem("x_olo")
        self.o_pad = sem("o_pad")
        self.y1_in = sem("y1_in")
        self.h_sq = sem("h_sq")
        self.h_hi = sem("h_hi")
        self.h_lo = sem("h_lo")
        self.stored = sem("stored")


class BandOperands:

    def __init__(self, Q, K, V, KC, VC):
        self.Q, self.K, self.V, self.KC, self.VC = Q, K, V, KC, VC


class CrossOperands:

    def __init__(self, Q, KV):
        self.Q, self.KV = Q, KV


def build(nc, xT, memT, slabs, par, rbrev, ctxa, ctxc, kcT, vc, mkcT, mvc,
          o_y, o_ca, o_cc, o_k, o_v, o_kc, o_vc, o_mk, o_mv):
    ctx = ExitStack()
    with ctx:
        base = (nc.sbuf_base + 31) // 32 * 32
        TB = 4 * T
        A0, B0, Y0, W0 = base, base + 16 * TB, base + 32 * TB, base + 40 * TB
        R0 = W0 + 3 * 8192

        def at(name, shape, dt, off):
            return nc.alloc_sbuf_tensor_at(name, shape, dt, offset=off, align_bytes=16)

        def sem(name):
            return ctx.enter_context(nc.semaphore(name))

        A = [at("A_hi", [P, KT * T], F32R, A0), at("A_lo", [P, KT * T], F32R, A0 + 8 * TB)]
        B = [at("B_hi", [P, KT * T], F32R, B0), at("B_lo", [P, KT * T], F32R, B0 + 8 * TB)]
        Y = at("Y", [P, KT * T], F32, Y0)
        RAW = at("w_raw", [P, 2, D], F32, W0)
        WH = at("w_hi", [P, 2, D], F32R, W0 + 8192)
        WL = at("w_lo", [P, 2, D], F32R, W0 + 16384)
        TT = at("square", [P, T], F32, R0)
        TH = at("square_hi", [P, T], F32R, R0)
        RSTD = at("rstd", [P, T], F32, R0 + TB)
        ACC = RSTD
        RL = at("sum_lo", [P, T], F32R, R0 + TB)
        c0 = R0 + 2 * TB
        ID = at("ident", [P, P], F32, c0)
        ONE = at("ones", [P, 2], F32R, c0 + 512)
        SEL = at("half_sel", [P, 2], F32R, c0 + 544)
        PAR = at("params", [P, NPAR], F32, c0 + 576)
        c1 = c0 + 576 + (NPAR * 4 + 31) // 32 * 32
        CRT = at("c_root", [P, 9], F32, c1)
        CRC = at("c_rstd", [P, 9], F32, c1 + 64)
        CKR = at("ck_root", [P, 8], F32, c1 + 128)
        CKC = at("ck_rstd", [P, 8], F32, c1 + 160)
        CQR = at("cq_root", [P, 8, 9, 2], F32, c1 + 192)
        CQC = at("cq_rstd", [P, 8, 9, 2], F32, c1 + 192 + 576)
        EPSC = at("eps", [P, 1], F32, c1 + 192 + 1152)
        GQ = at("gq_scaled", [P, 3], F32, c1 + 192 + 1184)
        MIN = at("neg_max", [P, 4], F32, c1 + 192 + 1216)
        SUM = at("exp_sum", [P, 4], F32, c1 + 192 + 1248)
        REC = at("exp_rec", [P, 4], F32, c1 + 192 + 1280)
        assert c1 + 192 + 1312 <= nc.sbuf_usable_end

        MR = at("mem_raw", [P, 8, NMEM], F32, B0)
        MX = [at("mem_hi", [P, 8 * NMEM], F32R, B0 + 8192), at("mem_lo", [P, 8 * NMEM], F32R, B0 + 16384)]
        MSQ = at("mem_sq", [P, 8, NMEM], F32, B0 + 24576)
        KV = at("mem_kv", [P, 16, NMEM], F32, B0 + 32768)
        VMN = at("mem_v", [P, 2, D], F32, B0 + 49152)
        MSUM = at("mem_sum", [P, NMEM], F32, B0 + 57344)
        MQH = at("mem_sum_hi", [P, NMEM], F32R, B0 + 58368)
        MQL = at("mem_sum_lo", [P, NMEM], F32R, B0 + 59392)
        RM = at("mem_rstd", [P, NMEM], F32, B0 + 60416)
        KQH = at("memk_sq_hi", [P, 8, NMEM], F32R, B0)
        KQL = at("memk_sq_lo", [P, 8, NMEM], F32R, B0 + 24576)

        def slot(name, i, dt=F32):
            return at(name, [P, T], dt, B0 + i * TB)

        UEW = CA + SEQ + CA + DEC
        UE = at("ua_ext", [P, 2, UEW], F32, B0)
        CAW = UEW - CA
        CAV = at("conv_acc", [P, 2, CAW], F32, B0 + 9216)
        QKV = [slot(f"q_raw{j}", 12 + j) for j in range(4)] + [slot(f"k_raw{j}", 8 + j) for j in range(4)] \
            + [slot(f"v_raw{j}", 7 - j) for j in range(4)]
        XH = [slot("ln_hi0", 0, F32R), slot("ln_hi1", 1, F32R)]
        XL = [slot("ln_lo0", 2, F32R), slot("ln_lo1", 3, F32R)]
        BCC, BCM, BCV, BCN = slot("bc_c", 6), slot("bc_mean", 4), slot("bc_var", 0), slot("bc_a", 1)
        SGM = [slot("sig0", 2), slot("sig1", 3)]

        AT = []
        for r in range(2):
            o = A0 + 8 * r * TB
            AT.append(BandOperands(
                Q=[at(f"q_hi{r}", [P, T], F32R, o), at(f"q_lo{r}", [P, T], F32R, o + TB)],
                K=[at(f"k_hi{r}", [P, T], F32R, o + 2 * TB), at(f"k_lo{r}", [P, T], F32R, o + 3 * TB)],
                V=[at(f"v_hi{r}", [P, 9, P], F32R, o + 4 * TB), at(f"v_lo{r}", [P, 9, P], F32R, o + 4 * TB + 4608)],
                KC=[at(f"kc_hi{r}", [P, 512], F32R, o + 4 * TB + 9216),
                    at(f"kc_lo{r}", [P, 512], F32R, o + 4 * TB + 11264)],
                VC=[at(f"vc_hi{r}", [P, 4, P], F32R, o + 4 * TB + 13312),
                    at(f"vc_lo{r}", [P, 4, P], F32R, o + 4 * TB + 15360)]))
        SS = [at(f"scores{r}", [P, 2, 640], F32, B0 + 5120 * r) for r in range(2)]
        BIAS = [at("bias0", [P, 2, 640], F32, B0 + 10240), at("bias1", [P, 2, 640], F32, W0 + 18432)]
        PT = [at("pt_hi", [P, 5, 256], F32R, W0 + 8192), at("pt_lo", [P, 5, 256], F32R, W0 + 8192 + 5120)]
        RX = at("rstd_heads", [P, 9, 2, 64], F32, R0)
        RKC = at("kc_raw", [P, 512], F32, R0 + 4608)
        RVC = at("vc_raw", [P, 4, P], F32, R0 + 6656)
        BX = at("bias_ext", [8, 768], F32, B0 + 5 * TB)
        ext_d = nc.dram_tensor("bias_ext_d", [8, 768], F32, kind="Internal").ap()
        rep_d = nc.dram_tensor("bias_rep_d", [P, 8 * 768], F32, kind="Internal").ap()
        y1_d = nc.dram_tensor("y1_d", [KT, P, T], F32, kind="Internal").ap()
        OS = [at(f"o_sq{i}", [P, T], F32, A0 + i * TB) for i in range(4)]

        XSQ = [at(f"xq_sq{i}", [P, T], F32, B0 + (6 + i) * TB) for i in range(2)]
        XQH = at("xq_sum_hi", [P, T], F32R, B0 + 14 * TB)
        XQL = at("xq_sum_lo", [P, T], F32R, B0 + 15 * TB)
        CX = []
        for r in range(2):
            o = A0 + 8 * r * TB
            CX.append(CrossOperands(
                Q=[at(f"xq_hi{r}", [P, 2 * T], F32R, o), at(f"xq_lo{r}", [P, 2 * T], F32R, o + 2 * TB)],
                KV=[at(f"xkv_hi{r}", [P, 4, 512], F32R, o + 4 * TB),
                    at(f"xkv_lo{r}", [P, 4, 512], F32R, o + 4 * TB + 8192)]))
        XR = at("xkv_raw", [P, 4, 512], F32, R0)
        XPT = [at("xpt_hi", [P, 2, 512], F32R, W0 + 8192), at("xpt_lo", [P, 2, 512], F32R, W0 + 8192 + 4096)]
        XS = at("x_scores", [P, 2, 2, NMEM], F32, W0 + 16384)
        HID = TT

        def y(i):
            return Y[:, i * T:(i + 1) * T]
        Y5R = at("sum_hi", [P, T], F32R, Y0 + 5 * TB)
        Y4, Y5 = y(4), y(5)

        PS = ctx.enter_context(nc.psum_tensor("ps", [P, 8, 512], F32))

        s = Semaphores(sem)
        w_in = [s.w_in0, s.w_in1]

        def par_col(name, i=0):
            return PAR[:, _cols[name] + i:_cols[name] + i + 1]

        def ps_tile(par):
            return PS[:, 3 * par:3 * par + 3, 0:CH]

        def chunks(ap):
            return ap.rearrange("p (c n) -> p c n", n=CH)

        def act_split(e, sl, par, tile_needed):
            e.wait_ge(w_in[par], 16 * ((sl // 2) + 1) if isinstance(sl, int) else sl * 8 + 16 - 8 * par)
            if tile_needed is not None:
                e.wait_ge(s.tile_done, tile_needed)
            e.activation(WH[:, par], RAW[:, par], ACT.Copy).then_inc(s.w_hi, 1)

        def dve_split(e, sl, par):
            e.wait_ge(s.w_hi, sl + 1)
            e.tensor_tensor(WL[:, par], RAW[:, par], WH[:, par].bitcast(F32), ALU.subtract).then_inc(s.w_lo, 1)

        def pe_tile(e, par, wpar, X, nk=KT, k0=0, woff=0, order=None, kwait=None, wcol=P):
            order = order or list(range(nk))
            for n, k in enumerate(order):
                if kwait is not None:
                    kwait(k)
                w = slice(woff + k * P, woff + (k + 1) * P)
                for m, (wt, xt) in enumerate(((WH, X[0]), (WH, X[1]), (WL, X[0]))):
                    for c in range(NCH):
                        col = (k0 + k) * T + c * CH
                        ins = e.matmul(PS[:, 3 * par + c, 0:CH], wt[:, wpar, w], xt[:, col:col + CH],
                                       start=(n == 0 and m == 0), stop=(n == nk - 1 and m == 2))
            ins.then_inc(s.tile_done, 1)

        class Count:
            def __init__(self):
                self.stat = 0
                self.rc = 0
                self.bc = 0
                self.other = 0

            def used(self, n):
                return n - self.other

        def pe_stat(e, cnt, pairs, rhs, bc_seen):
            if cnt.stat:
                e.wait_ge(s.stat_read, cnt.stat)
            if bc_seen:
                e.wait_ge(s.bc_used, bc_seen)
            for b, t0 in enumerate(BLK):
                for n, src in enumerate(pairs):
                    ins = e.matmul(PS[:, 6, 2 * b:2 * b + 2], src[:, t0:t0 + P], rhs[:, :],
                                   start=(n == 0), stop=(n == len(pairs) - 1))
            ins.then_inc(s.stat_done, 1)
            cnt.stat += 1

        def pe_bcast(e, cnt, src, first_wait, used=None):
            used = used or (lambda n: e.wait_ge(s.bc_used, cnt.used(n)))
            first_wait()
            for c, (lo, hi, blocks) in enumerate(BC):
                n = cnt.bc
                if c == 0:
                    used(n)
                if c == 1:
                    e.wait_ge(s.stat_read, cnt.stat)
                if c == 2:
                    used(n - 1)
                bank = 6 if c == 1 else 7
                for b in blocks:
                    ins = e.transpose(PS[:, bank, BLK[b] - lo:BLK[b] - lo + P], src(b), ID[:, :])
                ins.then_inc(s.bc_done, 1)
                cnt.bc += 1

        def act_bcast(e, cnt, dst):
            for c, (lo, hi, blocks) in enumerate(BC):
                bank = 6 if c == 1 else 7
                e.wait_ge(s.bc_done, cnt.bc + 1)
                e.activation(dst[:, lo:hi], PS[:, bank, 0:hi - lo], ACT.Copy).then_inc(s.bc_used, 1)
                cnt.bc += 1

        def act_root(e, cnt, dim):
            e.wait_ge(s.stat_done, cnt.stat + 1)
            if cnt.rc:
                e.wait_ge(s.rc_done, cnt.rc)
            e.activation(CRT[:, :], PS[:, 6, 0:18:2], ACT.Sqrt, bias=EPSC[:, :], scale=1.0 / dim)\
                .then_inc(s.stat_read, 1)
            cnt.stat += 1
            cnt.rc += 1

        def dve_recip(e, cnt):
            e.wait_ge(s.stat_read, cnt.stat + 1)
            if cnt.bc:
                e.wait_ge(s.bc_done, cnt.bc)
            e.reciprocal(CRC[:, :], CRT[:, :]).then_inc(s.rc_done, 1)
            cnt.stat += 1
            cnt.rc += 1

        N_U = 36

        def keys(n):
            b = n % 9
            tiles = min(b + 1, 5)
            cols = 576 if b == 8 else 128 * tiles
            return tiles, cols, 640 - cols

        def pieces(n):
            return (keys(n)[0] + 1) // 2
        CUM = [0]
        for n in range(N_U):
            CUM.append(CUM[-1] + pieces(n))

        def piece(n, p):
            tiles = keys(n)[0]
            w = 256 * min(2, tiles - 2 * p)
            return (64 if n % 9 == 8 and p == 2 else P), w

        N_XU, N_XQ = 20, 12

        def xblocks(u):
            return 1 if u % 5 == 4 else 2

        def xexps(u):
            return 9 * (u // 5) + 2 * (u % 5)

        def xgroup(u):
            return 3 * (u // 5) + (u % 5) // 2, u % 5 in (1, 3, 4)

        def su(g):
            return g * 8 + (S_UP + 4)

        def sd(g):
            return g * 8 + (S_UP + (8 if not isinstance(g, int) or g < N_G - 1 else 4))

        def tu(g):
            return g * 12 + (S_UP + 4)

        def td(g):
            return g * 12 + (S_UP + (8 if not isinstance(g, int) or g < N_G - 1 else 4))

        KORD = [0, 1, 6, 7, 2, 3, 4, 5]

        block = ctx.enter_context(nc.Block())

        N_STAT_X = 17

        @block.sync
        def _(sp):
            for par in range(2):
                sp.dma_start(RAW[:, par], slabs[par]).then_inc(w_in[par], 16)
            with sp.Fori(1, N_SLABS // 2) as i:
                for par in range(2):
                    sp.wait_ge(s.w_lo, i * 2 + par - 1)
                    sp.dma_start(RAW[:, par], slabs[bass.ds(i * 2 + par, 1)].rearrange("o p c -> p (o c)"))\
                        .then_inc(w_in[par], 16)

        @block.gpsimd
        def _(g):
            g.dma_start(MR[:, :, :], memT.rearrange("k p n -> p k n")).then_inc(s.mem_in, 16)
            g.dma_start(PAR[:, :], par).then_inc(s.params_in, 16)
            for k in range(KT):
                if k:
                    g.wait_ge(s.x_in, 16 * k)
                g.dma_start(y(k), xT[k]).then_inc(s.x_in, 16)
                if k == 0:
                    g.memset(ID[:, :], 0.0).then_inc(s.zero_ready, 1)
                    g.wait_ge(s.zero_ready, 1)
                    g.affine_select(out=ID[:, :], in_=ID[:, :], compare_op=ALU.not_equal, fill=1.0, base=0,
                                    pattern=[[-1, P]], channel_multiplier=1).then_inc(s.const_ready, 1)
                    g.memset(SEL[:, :].bitcast(F32), 0.0).then_inc(s.zero_ready, 1)
                    g.wait_ge(s.zero_ready, 2)
                    for n, (ap, value) in enumerate((
                            (ONE[:, :].bitcast(F32), 1.0), (SEL[0:64, 0:1].bitcast(F32), 1.0),
                            (SEL[64:128, 1:2].bitcast(F32), 1.0), (EPSC[:, :], EPS), (ACC[:, :], 0.0))):
                        g.wait_ge(s.const_ready, n + 1)
                        g.memset(ap, value).then_inc(s.const_ready, 1)
            g.wait_ge(s.mk_norm, 8)
            g.dma_start(o_mk.rearrange("k p n -> p k n"), KV[:, 0:8]).then_inc(s.mem_stored, 16)
            g.wait_ge(s.mv_cp, 4)
            g.dma_start(o_mv.rearrange("a p n -> p a n"), VMN[:, :, :]).then_inc(s.mem_stored, 16)
            g.wait_ge(s.stat_done, 3)
            g.dma_start(UE[:, :, CA + SEQ:2 * CA + SEQ], ctxa.rearrange("i p n -> p i n")).then_inc(s.ctx_in, 16)
            for i in range(2):
                g.wait_ge(s.sq_done, 8)
                g.wait_ge(s.a_lo, 8)
                g.dma_start(y(i)[:, CC + SEQ:2 * CC + SEQ], ctxc[i]).then_inc(s.ctx_in, 16)
            g.dma_start(BX[:, 511:768], rbrev).then_inc(s.bx_in, 16)
            g.wait_ge(s.bx_in, 16)
            g.tensor_copy(BX[:, 0:511], BX[:, 511:512].to_broadcast([8, 511])).then_inc(s.bx_done, 1)
            g.wait_ge(s.bx_done, 1)
            g.tensor_scalar(BX[:, :], BX[:, :], -1.0, 0.0, ALU.mult, ALU.add).then_inc(s.bx_done, 1)
            g.wait_ge(s.bx_done, 2)
            g.dma_start(ext_d, BX[:, :]).then_inc(s.ext_out, 16)
            g.wait_ge(s.ext_out, 16)
            g.dma_start(rep_d, bass.AP(ext_d.tensor, 0, [[0, P], [1, 8 * 768]])).then_inc(s.rep_out, 16)
            g.dma_start(o_kc, kcT[:, :, 64:512]).then_inc(s.cache_out, 16)
            g.dma_start(o_vc, vc.rearrange("a p n -> (a p) n")[64:512, :]).then_inc(s.cache_out, 16)
            g.wait_ge(s.ue_done, 4)
            g.wait_ge(s.ctx_in, 48)
            g.dma_start(o_ca[0].rearrange("i p n -> p i n"), UE[:, :, SEQ:SEQ + CA]).then_inc(s.state_out, 16)
            g.dma_start(o_ca[1].rearrange("i p n -> p i n"), UE[:, :, UEW - CA:UEW]).then_inc(s.state_out, 16)
            for i in range(2):
                g.wait_ge(s.uc_done, 2 * i + 2)
                g.dma_start(o_cc[0, i], y(i)[:, SEQ:SEQ + CC]).then_inc(s.state_out, 16)
                g.dma_start(o_cc[1, i], y(i)[:, T - CC:T]).then_inc(s.state_out, 16)
            def load_bias(j):
                if j >= 2:
                    g.wait_ge(s.ttr_done, 18 * (j - 1))
                else:
                    g.wait_ge(s.gn_done, 4)
                    g.wait_ge(s.w_lo, S_OUT)
                    g.wait_ge(s.tile_done, S_OUT)
                if j >= 1:
                    g.wait_ge(s.bias_in, 16 * j)
                g.dma_start(BIAS[j % 2][:, :, :], bass.AP(rep_d.tensor, 2 * j * 768 + 127,
                                                          [[8 * 768 - 1, P], [768, 2], [1, 640]])).then_inc(s.bias_in, 16)
                g.wait_ge(s.bias_in, 16 * (j + 1))
                g.memset(BIAS[j % 2][0:64, :, 576:640], BIG).then_inc(s.bias_ready, 1)
                g.wait_ge(s.bias_ready, 2 * j + 1)
                g.memset(BIAS[j % 2][64:128, :, 0:64], BIG).then_inc(s.bias_ready, 1)

            def load_cache(j):
                if j == 0:
                    g.wait_ge(s.gn_done, 4)
                    g.wait_ge(s.stat_done, 14)
                else:
                    g.wait_ge(s.kc_lo, 2 * j)
                g.dma_start(RKC[:, :], kcT[j]).then_inc(s.cache_in, 16)
                g.dma_start(RVC[:, :, :], vc[:, :, j * P:(j + 1) * P].rearrange("a p n -> p a n")).then_inc(s.cache_in, 16)

            g.wait_ge(s.tile_read, S_IN + 22)
            for j in range(4):
                g.dma_start(o_v[j], QKV[8 + j][:, 512:TOK]).then_inc(s.kv_out, 16)
            g.wait_ge(s.rep_out, 16)
            for j in range(4):
                load_cache(j)
                load_bias(j)
                g.wait_ge(s.k_nrm, 3 * j + 3)
                g.dma_start(o_k[j], QKV[4 + j][:, 512:TOK]).then_inc(s.kv_out, 16)
            g.wait_ge(s.b_lo, 8)
            for k in range(KT):
                if k:
                    g.wait_ge(s.x2_in, 16 * k)
                g.dma_start(y(k), xT[k]).then_inc(s.x2_in, 16)
            for k in range(KT):
                g.wait_ge(s.tile_read, S_OUT + k + 1)
                if k:
                    g.wait_ge(s.y1_out, 16 * k)
                g.dma_start(y1_d[k], y(k)).then_inc(s.y1_out, 16)
            for h in range(4):
                if h == 0:
                    g.wait_ge(s.tile_read, S_XO)
                    g.wait_ge(s.stat_done, N_STAT_X)
                else:
                    g.wait_ge(s.xkv_lo, h)
                for n, src in enumerate((o_mk[2 * h:2 * h + 2].rearrange("k p n -> p k n"),
                                         o_mv[:, :, h * 256:(h + 1) * 256].rearrange("a p n -> p a n"),
                                         mkcT[2 * h:2 * h + 2].rearrange("k p n -> p k n"),
                                         mvc[:, :, h * 256:(h + 1) * 256].rearrange("a p n -> p a n"))):
                    g.dma_start(XR[:, n].rearrange("p (k n) -> p k n", k=2), src).then_inc(s.xkv_in, 16)
            g.wait_ge(s.xq_lo, 4)
            g.wait_ge(s.y1_out, 128)
            for k in range(KT):
                if k:
                    g.wait_ge(s.y1_in, 16 * k)
                g.dma_start(y(k), y1_d[k]).then_inc(s.y1_in, 16)
            for m in range(KT):
                g.wait_ge(s.tile_read, td(N_G - 1) + m + 1)
                g.dma_start(o_y[m], y(m)).then_inc(s.stored, 16)
            g.wait_ge(s.stored, 128)
            for q, v in ((s.state_out, 96), (s.mem_stored, 32), (s.cache_out, 32), (s.kv_out, 128)):
                g.wait_ge(q, v)

        @block.scalar
        def _(e):
            cnt = Count()
            act_split(e, 0, 0, None)
            act_split(e, 1, 1, None)
            e.wait_ge(s.mem_in, 16)
            e.wait_ge(s.params_in, 16)
            for k in range(KT):
                e.activation(MX[0][:, k * NMEM:(k + 1) * NMEM], MR[:, k], ACT.Copy,
                             scale=par_col("norm_mem", k)).then_inc(s.mem_hi, 1)
            e.activation(MSQ[:, :, :], MR[:, :, :], ACT.Square).then_inc(s.mem_sq, 1)
            e.wait_ge(s.mem_sum, 1)
            e.activation(MQH[:, :], MSUM[:, :], ACT.Copy).then_inc(s.mem_qhi, 1)

            def x_hi(k):
                e.wait_ge(s.x_in, k * 16 + 16)
                e.wait_ge(s.params_in, 16)
                e.activation(A[0][:, bass.ds(k * T, T)], Y[:, bass.ds(k * T, T)], ACT.Copy,
                             scale=PAR[:, bass.ds(k + _cols["norm_mix"], 1)]).then_inc(s.a_hi, 1)

            act_split(e, 2, 0, 1)
            e.wait_ge(s.stat_done, 1)
            e.wait_ge(s.const_ready, 6)
            e.activation(CKR[:, 0:2], PS[:, 6, 0:4:2], ACT.Sqrt, bias=EPSC[:, :], scale=1.0 / D)\
                .then_inc(s.stat_read, 1)
            cnt.stat += 1
            e.wait_ge(s.bc_done, 1)
            e.activation(RM[:, :], PS[:, 7, 0:NMEM], ACT.Copy).then_inc(s.bc_used, 1)
            cnt.bc += 1
            x_hi(0)
            act_split(e, 3, 1, 2)
            e.activation(TT[:, :], y(0), ACT.Square).then_inc(s.sq_done, 1)
            with e.Fori(1, 8) as i:
                act_split(e, i * 2 + 2, 0, i * 2 + 1)
                x_hi(i)
                e.wait_ge(s.acc_done, i)
                act_split(e, i * 2 + 3, 1, i * 2 + 2)
                e.activation(TT[:, :], Y[:, bass.ds(i * T, T)], ACT.Square).then_inc(s.sq_done, 1)
            e.wait_ge(s.acc_done, 8)
            e.activation(TH[:, :], ACC[:, :], ACT.Copy).then_inc(s.q_hi, 1)
            e.wait_ge(s.tile_read, 8)
            e.activation(MSQ[:, :, :], KV[:, 0:8], ACT.Square).then_inc(s.kq_sq, 1)
            e.wait_ge(s.kq_sq, 1)
            e.activation(KQH[:, :, :], MSQ[:, :, :], ACT.Copy).then_inc(s.kq_hi, 1)

            def win_split(i):
                if i < 20:
                    act_split(e, S_IN + i + 2, i % 2, S_IN + i + 1)

            act_root(e, cnt, D)
            act_bcast(e, cnt, RSTD)
            win_split(0)
            e.wait_ge(s.stat_done, cnt.stat + 1)
            e.activation(CKR[:, :], PS[:, 6, 0:16:2], ACT.Sqrt, bias=EPSC[:, :], scale=1.0 / 256)\
                .then_inc(s.stat_read, 1)
            cnt.stat += 1
            win_split(1)

            def sigmoid(i):
                e.wait_ge(s.tile_read, S_IN + 2 + 2 * i)
                e.activation(y(3), y(3), ACT.Sigmoid).then_inc(s.sig_done, 1)

            sigmoid(0)
            for n in range(4):
                e.wait_ge(s.mv_tr, n + 1)
                e.activation(VMN[:, n // 2, (n % 2) * 512:(n % 2) * 512 + 512], PS[:, 6 + n % 2, :], ACT.Copy)\
                    .then_inc(s.mv_cp, 1)
            win_split(2)
            win_split(3)
            sigmoid(1)
            def group_sq(n, tiles, ready, cnt_ready):
                e.wait_ge(ready, cnt_ready)
                e.wait_ge(s.stat_done, cnt.stat)
                e.activation(TT[:, :], tiles[0], ACT.Square).then_inc(s.g_sq, 1)
                e.activation(Y4, tiles[1], ACT.Square).then_inc(s.g_sq, 1)

            def group_hi(n):
                e.wait_ge(s.g_sum, n + 1)
                e.activation(Y5R[:, :], TT[:, :], ACT.Copy).then_inc(s.g_hi, 1)

            for i in range(4, 22):
                win_split(i)
                if i == 10:
                    group_sq(0, (y(6), y(7)), s.yc_done, 4)
                    group_hi(0)
                if i == 11:
                    act_root(e, cnt, 256)
                if i == 12:
                    act_bcast(e, cnt, BCC)
                if i == 18:
                    for h in range(2):
                        e.wait_ge(s.conv_step, 64)
                        e.activation(XH[h][:, :], y(h), ACT.Copy).then_inc(s.xa_hi, 1)
                if 11 <= i <= 18:
                    j = i - 11
                    e.wait_ge(s.tile_read, S_IN + 10 + j + 1)
                    e.wait_ge(s.stat_done, cnt.stat)
                    e.activation(TT[:, :], QKV[j][:, :], ACT.Square).then_inc(s.qk_sq, 1)
                    e.wait_ge(s.qk_sq, j + 1)
                    e.activation(Y5R[:, :], TT[:, :], ACT.Copy).then_inc(s.qk_hi, 1)
                    e.wait_ge(s.stat_done, cnt.stat + 1)
                    e.activation(CQR[:, j].rearrange("p b e -> p (b e)"), PS[:, 6, 0:18], ACT.Sqrt,
                                 bias=EPSC[:, :], scale=1.0 / 64).then_inc(s.stat_read, 1)
                    cnt.stat += 1
                if i == 19:
                    e.wait_ge(s.stat_done, cnt.stat + 1)
                    e.activation(CRT[:, :], PS[:, 6, 0:18:2], ACT.Copy, scale=1.0 / 256).then_inc(s.stat_read, 1)
                    cnt.stat += 1
                    act_bcast(e, cnt, BCM)
                    group_sq(1, (y(0), y(1)), s.xa_sub, 2)
                    group_hi(1)
                if i == 20:
                    act_root(e, cnt, 256)
                    act_bcast(e, cnt, BCV)
                    for h in range(2):
                        e.wait_ge(s.xa_nrm, h + 1)
                        e.activation(SGM[h][:, :], y(h), ACT.Sigmoid, bias=par_col("ln_a_b", h)).then_inc(s.ya_sig, 1)
                    group_sq(2, (y(0), y(1)), s.ya_done, 2)
                    group_hi(2)
                if i == 21:
                    act_root(e, cnt, 256)
                    act_bcast(e, cnt, BCN)

            def prep(j):
                r = AT[j % 2]
                qr, kr = QKV[j], QKV[4 + j]
                for which, src in ((0, j), (1, 4 + j)):
                    if j == 0 and which == 0:
                        e.wait_ge(s.cq_rc, 1)
                        e.wait_ge(s.gn_done, 4)
                    e.wait_ge(s.bc_done, cnt.bc)
                    e.activation(RX[:, :, :, :], CQC[:, src].unsqueeze(3).to_broadcast([P, 9, 2, 64]), ACT.Copy)\
                        .then_inc(s.rx_ready, 1)
                    cnt.bc += 3
                e.wait_ge(s.cache_in, 32 * (j + 1))
                if j >= 2:
                    e.wait_ge(s.pv_done, 9 * (j - 1))
                e.activation(r.KC[0][:, :], RKC[:, :], ACT.Copy).then_inc(s.kc_hi, 1)
                e.activation(r.VC[0][:, :, :], RVC[:, :, :], ACT.Copy).then_inc(s.kc_hi, 1)
                e.wait_ge(s.q_nrm, 3 * j + 3)
                e.activation(r.Q[0][:, :], qr[:, :], ACT.Copy).then_inc(s.qk2_hi, 1)
                e.wait_ge(s.k_nrm, 3 * j + 3)
                e.activation(r.K[0][:, :], kr[:, :], ACT.Copy).then_inc(s.qk2_hi, 1)
                for c in range(3):
                    e.wait_ge(s.bc_done, cnt.bc + 1)
                    bank = 6 if c == 1 else 7
                    nb = 3 if c < 2 else 2
                    e.activation(r.V[0][:, 3 * c:3 * c + nb], PS[:, bank, 0:nb * P].rearrange("p (b n) -> p b n", n=P),
                                 ACT.Copy).then_inc(s.v_hi, 1)
                    if c == 2:
                        e.activation(r.V[0][0:64, 8], PS[0:64, bank, 256:384], ACT.Copy).then_inc(s.v_hi, 1)
                    cnt.bc += 1

            def exps(n):
                _, cols, _ = keys(n)
                for h in range(2):
                    e.wait_ge(s.ttr_done, 2 * n + h + 1)
                    if n >= 2:
                        e.wait_ge(s.rec_done, n - 1)
                    m = 2 * (n % 2) + h
                    e.activation(SS[n % 2][:, h, 0:cols], SS[n % 2][:, h, 0:cols], ACT.Exp, bias=MIN[:, m:m + 1],
                                 scale=-1.0, accum_out=SUM[:, m:m + 1]).then_inc(s.exp_done, 1)

            def o_out(n):
                j, b = divmod(n, 9)
                e.wait_ge(s.pv_done, n + 1)
                for h in range(2):
                    rows = slice(64 * h, 64 * h + 64)
                    q0, c0_, w = (P * b, h * P, P) if b < 8 else (SEQ, h * P + 64, 64)
                    e.activation(y(2 + j)[rows, q0:q0 + w], PS[rows, 7, c0_:c0_ + w], ACT.Copy).then_inc(s.o_used, 1)

            def pt_hi(n):
                for p in range(pieces(n)):
                    rows, w = piece(n, p)
                    if p == 0:
                        e.wait_ge(s.t_done, n + 1)
                        if n >= 1:
                            e.wait_ge(s.pv_done, n)
                            e.wait_ge(s.pt_lo, CUM[n])
                    e.activation(PT[0][:, :, :].rearrange("p a b -> p (a b)")[0:rows, 512 * p:512 * p + w],
                                 PS[0:rows, 4 + p, 0:w], ACT.Copy).then_inc(s.pt_hi, 1)

            prep(0)
            exps(0)
            for n in range(N_U):
                if n + 1 < N_U:
                    exps(n + 1)
                if n:
                    o_out(n - 1)
                pt_hi(n)
                if n % 9 == 5 and n < 27:
                    prep(n // 9 + 1)
            o_out(N_U - 1)

            for i in range(4):
                e.wait_ge(s.pad_ready, 9)
                e.wait_ge(s.o_used, 2 * N_U)
                e.activation(OS[i][:, :], y(2 + i), ACT.Square).then_inc(s.o_sq, 1)
            act_split(e, S_OUT, 0, None)
            act_split(e, S_OUT + 1, 1, None)
            e.wait_ge(s.o_sum, 3)
            e.activation(TH[:, :], OS[0][:, :], ACT.Copy).then_inc(s.q_hi, 1)

            def b_hi(k):
                if k == 0:
                    e.wait_ge(s.kv_out, 128)
                    e.wait_ge(s.v_hi, 16)
                e.activation(B[0][:, k * T:(k + 1) * T], y(k), ACT.Copy).then_inc(s.b_hi, 1)
            for k in (0, 1, 6, 7):
                b_hi(k)
            cnt.other = 36
            act_root(e, cnt, 512)
            act_bcast(e, cnt, RSTD)
            for i in range(4):
                e.wait_ge(s.o_nrm, i + 1)
                b_hi(2 + i)

            def residual(t0, i, par, norm, acc0):
                m = i * 2 + par
                e.wait_ge(s.tile_read, m + (t0 + 1))
                e.wait_ge(s.acc_done, m + acc0)
                act_split(e, m + (t0 + 2), par, m + (t0 + 1))
                e.activation(A[0][:, bass.ds(m * T, T)], Y[:, bass.ds(m * T, T)], ACT.Copy,
                             scale=PAR[:, bass.ds(m + _cols[norm], 1)]).then_inc(s.a_hi, 1)
                e.activation(TT[:, :], Y[:, bass.ds(m * T, T)], ACT.Square).then_inc(s.sq_done, 1)

            with e.Fori(0, 4) as i:
                for par in range(2):
                    residual(S_OUT, i, par, "norm_x", 8)
            e.wait_ge(s.acc_done, 16)
            e.activation(TH[:, :], ACC[:, :], ACT.Copy).then_inc(s.q_hi, 1)

            act_root(e, cnt, D)
            act_bcast(e, cnt, RSTD)
            for i in range(8):
                if i < 6:
                    act_split(e, S_XQ + i + 2, i % 2, S_XQ + i + 1)
                h = i // 2
                if i % 2:
                    for k in range(2):
                        e.wait_ge(s.tile_read, S_XQ + 2 * h + k + 1)
                        if h:
                            e.wait_ge(s.q_lo, 3 + h)
                        e.activation(XSQ[k][:, :], y(2 * h + k), ACT.Square).then_inc(s.xs_sq, 1)
                    e.wait_ge(s.xs_sum, h + 1)
                    if h:
                        e.wait_ge(s.stat_done, cnt.stat)
                    e.activation(XQH[:, :], XSQ[0][:, :], ACT.Copy).then_inc(s.q_hi, 1)
                if i % 2 == 0 and i:
                    act_root(e, cnt, 256)
            act_root(e, cnt, 256)

            def xprep(h):
                r = CX[h % 2]
                if h >= 2:
                    e.wait_ge(s.x_pv, 3 * (h - 1))
                else:
                    e.wait_ge(s.tile_done, S_XO)
                e.wait_ge(s.bc_used, cnt.used(N_BC_X + 3 * h))
                e.activation(r.Q[0][:, :], Y[:, 2 * h * T:(2 * h + 2) * T], ACT.Copy).then_inc(s.xq_hi, 1)
                e.wait_ge(s.xkv_in, 64 * (h + 1))
                e.activation(r.KV[0][:, :, :], XR[:, :, :], ACT.Copy).then_inc(s.xkv_hi, 1)

            def xexp(u):
                e.wait_ge(s.x_min, u + 1)
                if u >= 2:
                    e.wait_ge(s.x_t, u - 1)
                    e.wait_ge(s.x_rec, u - 1)
                for b in range(xblocks(u)):
                    m = 2 * (u % 2) + b
                    e.activation(XS[:, u % 2, b], PS[:, u % 2, b * NMEM:(b + 1) * NMEM], ACT.Exp, bias=MIN[:, m:m + 1],
                                 scale=-1.0, accum_out=SUM[:, m:m + 1]).then_inc(s.x_exp, 1)

            def xpt_hi(q):
                h, g = divmod(q, 3)
                w = 512 if g < 2 else P
                e.wait_ge(s.x_t, 5 * h + (2 * g + 2 if g < 2 else 5))
                if q:
                    e.wait_ge(s.x_pv, q)
                    e.wait_ge(s.x_ptlo, q)
                k = 2 + 2 * (q % 2)
                e.activation(XPT[0][:, :, 0:w], PS[:, k:k + 2, 0:w], ACT.Copy).then_inc(s.x_pthi, 1)

            def xo_hi(q):
                h, g = divmod(q, 3)
                e.wait_ge(s.x_pv, q + 1)
                for d in range(2):
                    lo, c, w = (512 * g, 0, 512) if g < 2 else (SEQ, 64, 64)
                    col = (2 * h + d) * T + lo
                    e.activation(B[0][:, col:col + w], PS[:, 6 + d, c:c + w], ACT.Copy).then_inc(s.x_ohi, 1)

            N_BC_X = cnt.bc + 3
            xprep(0)
            xexp(0)
            done = None
            for u in range(N_XU):
                if u + 1 < N_XU:
                    xexp(u + 1)
                if done is not None:
                    xo_hi(done)
                    done = None
                q, last = xgroup(u)
                if last:
                    xpt_hi(q)
                    done = q
                if u % 5 == 1 and u < 15:
                    xprep(u // 5 + 1)
            xo_hi(done)
            cnt.bc += 12

            e.wait_ge(s.x_pv, N_XQ)
            act_split(e, S_XO, 0, None)
            act_split(e, S_XO + 1, 1, None)
            with e.Fori(0, 4) as i:
                for par in range(2):
                    residual(S_XO, i, par, "norm_ff", 16)
            e.wait_ge(s.acc_done, 24)
            e.activation(TH[:, :], ACC[:, :], ACT.Copy).then_inc(s.q_hi, 1)

            def hidden(t, h0, j, slot):
                e.wait_ge(s.tile_read, t + (j + 1))
                e.activation(HID[:, :], HID[:, :], ACT.Square).then_inc(s.h_sq, 1)
                e.wait_ge(s.h_sq, h0 + (j + 1))
                e.activation(B[0][:, (slot + j) * T:(slot + j + 1) * T], HID[:, :], ACT.Copy).then_inc(s.h_hi, 1)

            def mlp_group(g, half):
                if not isinstance(g, int) or g < N_G - 1:
                    for j in range(4):
                        act_split(e, su(g) + (j + 2), j % 2, tu(g) + (j + 1))
                        hidden(tu(g), g * 4 + 4, j, 4 * (1 - half))
                for j in range(4 if not isinstance(g, int) or g < N_G - 1 else 2):
                    act_split(e, sd(g) + (j + 2), j % 2, td(g) + (2 * j + 2))

            act_root(e, cnt, D)
            act_bcast(e, cnt, RSTD)
            for j in range(4):
                act_split(e, S_UP + j + 2, j % 2, S_UP + j + 1)
                hidden(S_UP, 0, j, 0)
            with e.Fori(0, 3) as i:
                mlp_group(i * 2, 0)
                mlp_group(i * 2 + 1, 1)
            mlp_group(6, 0)
            mlp_group(7, 1)

        @block.vector
        def _(e):
            cnt = Count()
            dve_split(e, 0, 0)
            dve_split(e, 1, 1)
            e.wait_ge(s.params_in, 16)
            for k in range(KT):
                e.wait_ge(s.mem_hi, k + 1)
                sl = slice(k * NMEM, (k + 1) * NMEM)
                e.scalar_tensor_tensor(MX[1][:, sl], MR[:, k], par_col("norm_mem", k), MX[0][:, sl].bitcast(F32),
                                       ALU.mult, ALU.subtract).then_inc(s.mem_lo, 1)
            e.wait_ge(s.mem_sq, 1)
            e.tensor_reduce(MSUM[:, :], MSQ[:, :, :].rearrange("p k n -> p n k"), AX.X, ALU.add).then_inc(s.mem_sum, 1)
            e.wait_ge(s.mem_qhi, 1)
            e.tensor_tensor(MQL[:, :], MSUM[:, :], MQH[:, :].bitcast(F32), ALU.subtract).then_inc(s.mem_qlo, 1)

            def x_lo(k):
                e.wait_ge(s.a_hi, k + 1)
                e.scalar_tensor_tensor(A[1][:, bass.ds(k * T, T)], Y[:, bass.ds(k * T, T)],
                                       PAR[:, bass.ds(k + _cols["norm_mix"], 1)],
                                       A[0][:, bass.ds(k * T, T)].bitcast(F32), ALU.mult, ALU.subtract)\
                    .then_inc(s.a_lo, 1)

            def add_sq(n):
                e.wait_ge(s.sq_done, n + 1)
                e.tensor_tensor(ACC[:, :], ACC[:, :], TT[:, :], ALU.add).then_inc(s.acc_done, 1)

            def mem_evac(t, par):
                e.wait_ge(s.tile_done, t + 1)
                e.tensor_tensor(KV[:, bass.ds(t, 1)].rearrange("p o n -> p (o n)"), PS[:, 3 * par, 0:NMEM],
                                RM[:, :], ALU.mult).then_inc(s.tile_read, 1)

            dve_split(e, 2, 0)
            e.wait_ge(s.stat_read, 1)
            e.reciprocal(CKC[:, 0:2], CKR[:, 0:2]).then_inc(s.ck_rc, 1)
            cnt.stat += 1
            e.wait_ge(s.bc_used, 1)
            cnt.bc += 1
            mem_evac(0, 0)
            x_lo(0)
            dve_split(e, 3, 1)
            mem_evac(1, 1)
            e.wait_ge(s.const_ready, 6)
            add_sq(0)
            with e.Fori(1, 8) as i:
                dve_split(e, i * 2 + 2, 0)
                mem_evac(i * 2, 0)
                x_lo(i)
                dve_split(e, i * 2 + 3, 1)
                mem_evac(i * 2 + 1, 1)
                e.wait_ge(s.acc_done, i)
                add_sq(i)
            e.wait_ge(s.q_hi, 1)
            e.wait_ge(s.acc_done, 8)
            e.tensor_tensor(RL[:, :], ACC[:, :], TH[:, :].bitcast(F32), ALU.subtract).then_inc(s.q_lo, 1)
            e.wait_ge(s.kq_hi, 1)
            e.tensor_tensor(KQL[:, :, :], MSQ[:, :, :], KQH[:, :, :].bitcast(F32), ALU.subtract).then_inc(s.kq_lo, 1)

            def win_split(i):
                if i < 20:
                    dve_split(e, S_IN + i + 2, i % 2)

            def evac(i, dst):
                e.wait_ge(s.tile_done, S_IN + i + 1)
                e.wait_ge(s.bc_used, 4)
                e.tensor_tensor(chunks(dst), ps_tile(i % 2), chunks(RSTD[:, :]), ALU.mult).then_inc(s.tile_read, 1)

            dve_recip(e, cnt)
            cnt.bc += 3
            win_split(0)
            e.wait_ge(s.sq_done, 8)
            e.wait_ge(s.a_lo, 8)
            for i in (6, 7):
                e.memset(y(i)[:, TOK:T], 0.0).then_inc(s.pad_ready, 1)
            for i in (0, 1):
                e.memset(y(i)[:, 0:CC], 0.0).then_inc(s.pad_ready, 1)
            evac(0, y(2))
            e.wait_ge(s.stat_read, cnt.stat + 1)
            e.reciprocal(CKC[:, :], CKR[:, :]).then_inc(s.ck_rc, 1)
            cnt.stat += 1
            e.memset(UE[:, :, 0:CA], 0.0).then_inc(s.pad_ready, 1)
            win_split(1)
            evac(1, y(3))
            e.wait_ge(s.tile_read, S_MEM + 8)
            for k in range(KT):
                h = k // 2
                e.wait_ge(s.mk_bc, h // 2 + 1)
                e.scalar_tensor_tensor(KV[:, k], KV[:, k], par_col("xk_norm", k % 2),
                                       PS[:, 6 + h // 2, (h % 2) * NMEM:(h % 2) * NMEM + NMEM],
                                       ALU.mult, ALU.mult).then_inc(s.mk_norm, 1)

            def glu(i):
                e.wait_ge(s.sig_done, i + 1)
                e.wait_ge(s.tile_read, S_IN + 1 + 2 * i)
                if i == 0:
                    e.wait_ge(s.stat_done, 3)
                e.tensor_tensor(UE[:, i, CA:CA + SEQ], y(2)[:, 0:SEQ], y(3)[:, 0:SEQ], ALU.mult).then_inc(s.ue_done, 1)
                e.tensor_tensor(UE[:, i, 2 * CA + SEQ:UEW], y(2)[:, SEQ:TOK], y(3)[:, SEQ:TOK], ALU.mult)\
                    .then_inc(s.ue_done, 1)

            glu(0)
            win_split(2)
            e.wait_ge(s.ue_done, 2)
            evac(2, y(2))
            win_split(3)
            evac(3, y(3))
            glu(1)

            tap = [0]

            def conv_taps(n):
                for _ in range(n):
                    j, h = divmod(tap[0], 2)
                    w = par_col("conv_a_w", 2 * j + h)
                    if tap[0] == 0:
                        e.wait_ge(s.ue_done, 4)
                        e.wait_ge(s.ctx_in, 48)
                        e.wait_ge(s.pad_ready, 5)
                    if j == 0:
                        e.tensor_scalar(CAV[:, h], UE[:, h, j:j + CAW], w, par_col("conv_a_b", h), ALU.mult, ALU.add)\
                            .then_inc(s.conv_step, 1)
                    elif j < CA:
                        e.wait_ge(s.conv_step, tap[0] - 1)
                        e.scalar_tensor_tensor(CAV[:, h], UE[:, h, j:j + CAW], w, CAV[:, h], ALU.mult, ALU.add)\
                            .then_inc(s.conv_step, 1)
                    else:
                        e.wait_ge(s.conv_step, tap[0] - 1 if h == 0 else tap[0])
                        if h == 0:
                            e.wait_ge(s.state_out, 16 * 6)
                            e.wait_ge(s.c3_done, 6)
                        for lo, n_, src in ((0, SEQ, 0), (SEQ, DEC, SEQ + CA)):
                            e.scalar_tensor_tensor(y(h)[:, lo:lo + n_], UE[:, h, j + src:j + src + n_], w,
                                                   CAV[:, h, src:src + n_], ALU.mult, ALU.add)\
                                .then_inc(s.conv_step, 1)
                    tap[0] += 1

            def conv_c(i, gate, h3, out):
                for j in range(3):
                    w = par_col("conv_c_w", 2 * j + i)
                    src = y(i)[:, j:j + T - CC]
                    if j == 0:
                        e.wait_ge(s.uc_done, 2 * i + 2)
                        e.wait_ge(s.ctx_in, 48)
                        e.wait_ge(s.pad_ready, 5)
                        e.tensor_scalar(gate[:, 0:T - CC], src, w, None, ALU.mult).then_inc(s.c3_done, 1)
                    else:
                        e.wait_ge(s.c3_done, 3 * i + j)
                        e.scalar_tensor_tensor(gate[:, 0:T - CC], src, w, gate[:, 0:T - CC], ALU.mult, ALU.add)\
                            .then_inc(s.c3_done, 1)

            def group_sum(n):
                e.wait_ge(s.g_sq, 2 * n + 2)
                e.tensor_tensor(TT[:, :], TT[:, :], Y4, ALU.add).then_inc(s.g_sum, 1)
                e.wait_ge(s.g_hi, n + 1)
                e.wait_ge(s.g_sum, n + 1)
                e.tensor_tensor(TH[:, :], TT[:, :], Y5R[:, :].bitcast(F32), ALU.subtract).then_inc(s.g_lo, 1)

            for i in range(4, 22):
                win_split(i)
                if i in (4, 7):
                    c = (i - 4) // 3
                    e.wait_ge(s.ue_done, 4)
                    evac(i, y(4) if c == 0 else y(2))
                elif i in (5, 8):
                    c = (i - 5) // 3
                    a, b = (y(4), y(5)) if c == 0 else (y(2), y(3))
                    evac(i, b)
                    e.wait_ge(s.tile_read, S_IN + i + 1)
                    e.tensor_tensor(y(c)[:, CC:CC + SEQ], a[:, 0:SEQ], b[:, 0:SEQ], ALU.mult).then_inc(s.uc_done, 1)
                    e.tensor_tensor(y(c)[:, 2 * CC + SEQ:T], a[:, SEQ:TOK], b[:, SEQ:TOK], ALU.mult)\
                        .then_inc(s.uc_done, 1)
                    conv_c(c, a, b, None)
                elif i in (6, 9):
                    c = (i - 6) // 3
                    a, b = (y(4), y(5)) if c == 0 else (y(2), y(3))
                    e.wait_ge(s.uc_done, 2 * c + 2)
                    evac(i, b)
                    e.wait_ge(s.tile_read, S_IN + i + 1)
                    e.wait_ge(s.c3_done, 3 * c + 3)
                    e.tensor_tensor(y(6 + c)[:, 0:SEQ], b[:, 0:SEQ], a[:, 0:SEQ], ALU.mult).then_inc(s.yc_done, 1)
                    e.tensor_tensor(y(6 + c)[:, SEQ:TOK], b[:, SEQ:TOK], a[:, SEQ + CC:T - CC], ALU.mult)\
                        .then_inc(s.yc_done, 1)
                else:
                    if i == 10:
                        e.wait_ge(s.mem_stored, 32)
                    evac(i, QKV[i - 10][:, :])
                if i == 10:
                    e.wait_ge(s.yc_done, 4)
                    group_sum(0)
                if i == 11:
                    dve_recip(e, cnt)
                if i == 12:
                    cnt.bc += 3
                    for c in range(2):
                        e.wait_ge(s.bc_used, cnt.bc)
                        e.scalar_tensor_tensor(y(6 + c), y(6 + c), par_col("out_norm", 6 + c), BCC[:, :],
                                               ALU.mult, ALU.mult).then_inc(s.gn_done, 1)
                if 11 <= i <= 18:
                    j = i - 11
                    e.wait_ge(s.qk_hi, j + 1)
                    e.tensor_tensor(TH[:, :], TT[:, :], Y5R[:, :].bitcast(F32), ALU.subtract).then_inc(s.qk_lo, 1)
                    cnt.stat += 1
                conv_taps(TAPS.get(i, 0))
                if i == 18:
                    for h in range(2):
                        e.wait_ge(s.xa_hi, h + 1)
                        e.tensor_tensor(XL[h][:, :], y(h), XH[h][:, :].bitcast(F32), ALU.subtract).then_inc(s.xa_lo, 1)
                if i == 19:
                    cnt.stat += 1
                    cnt.bc += 3
                    for h in range(2):
                        e.wait_ge(s.bc_used, cnt.bc)
                        e.tensor_tensor(y(h), y(h), BCM[:, :], ALU.subtract).then_inc(s.xa_sub, 1)
                    group_sum(1)
                if i == 20:
                    dve_recip(e, cnt)
                    cnt.bc += 3
                    for h in range(2):
                        e.wait_ge(s.bc_used, cnt.bc)
                        e.wait_ge(s.xa_sub, 2)
                        e.scalar_tensor_tensor(y(h), y(h), par_col("ln_a_g", h), BCV[:, :], ALU.mult, ALU.mult)\
                            .then_inc(s.xa_nrm, 1)
                    for h in range(2):
                        e.wait_ge(s.ya_sig, h + 1)
                        e.scalar_tensor_tensor(y(h), y(h), par_col("ln_a_b", h), SGM[h][:, :], ALU.add, ALU.mult)\
                            .then_inc(s.ya_done, 1)
                    group_sum(2)
                if i == 21:
                    dve_recip(e, cnt)
                    cnt.bc += 3
                    for h in range(2):
                        e.wait_ge(s.bc_used, cnt.bc)
                        e.wait_ge(s.ya_done, 2)
                        e.scalar_tensor_tensor(y(h), y(h), par_col("out_norm", h), BCN[:, :], ALU.mult, ALU.mult)\
                            .then_inc(s.gn_done, 1)

            def heads_nrm(dst, gain, done):
                for c, (lo, hi, _) in enumerate(BC):
                    e.wait_ge(s.bc_done, cnt.bc + 1)
                    e.scalar_tensor_tensor(dst[:, lo:hi], dst[:, lo:hi], gain, PS[:, 6 if c == 1 else 7, 0:hi - lo],
                                           ALU.mult, ALU.mult).then_inc(done, 1)
                    cnt.bc += 1

            def prep(j):
                r = AT[j % 2]
                qr, kr = QKV[j], QKV[4 + j]
                heads_nrm(qr, GQ[:, 0:1], s.q_nrm)
                heads_nrm(kr, par_col("k_norm"), s.k_nrm)
                for n, (dst, src) in enumerate(((r.KC, RKC[:, :]), (r.VC, RVC[:, :, :]))):
                    e.wait_ge(s.kc_hi, 2 * j + n + 1)
                    full = (slice(None),) * len(dst[0].shape)
                    e.tensor_tensor(dst[1][full], src, dst[0][full].bitcast(F32), ALU.subtract).then_inc(s.kc_lo, 1)
                for n, (dst, src) in enumerate(((r.Q, qr), (r.K, kr))):
                    e.wait_ge(s.qk2_hi, 2 * j + n + 1)
                    e.tensor_tensor(dst[1][:, :], src[:, :], dst[0][:, :].bitcast(F32), ALU.subtract)\
                        .then_inc(s.qk2_lo, 1)
                for c in range(3):
                    bank = 6 if c == 1 else 7
                    nb = 3 if c < 2 else 2
                    e.wait_ge(s.v_hi, 4 * j + c + (2 if c == 2 else 1))
                    e.tensor_tensor(r.V[1][:, 3 * c:3 * c + nb], PS[:, bank, 0:nb * P].rearrange("p (b n) -> p b n", n=P),
                                    r.V[0][:, 3 * c:3 * c + nb].bitcast(F32), ALU.subtract).then_inc(s.v_lo, 1)
                    if c == 2:
                        e.tensor_tensor(r.V[1][0:64, 8], PS[0:64, bank, 256:384], r.V[0][0:64, 8].bitcast(F32),
                                        ALU.subtract).then_inc(s.v_lo, 1)
                    cnt.bc += 1

            def biased(n):
                _, cols, off = keys(n)
                j = n // 9
                e.wait_ge(s.bias_ready, 2 * j + 2)
                e.wait_ge(s.s_done, n + 1)
                if n >= 2:
                    e.wait_ge(s.t_done, n - 1)
                for h in range(2):
                    m = 2 * (n % 2) + h
                    e.tensor_tensor_reduce(
                        out=SS[n % 2][:, h, 0:cols], in0=PS[:, 2 * h:2 * h + 2].rearrange("p a b -> p (a b)")[:, 0:cols],
                        in1=BIAS[j % 2][:, h, off:off + cols], scale=1.0, scalar=3e38, op0=ALU.add, op1=ALU.min,
                        accum_out=MIN[:, m:m + 1]).then_inc(s.ttr_done, 1)

            def normalise(n):
                _, cols, _ = keys(n)
                m = 2 * (n % 2)
                e.wait_ge(s.exp_done, 2 * n + 2)
                if n >= 2:
                    e.wait_ge(s.p_ready, 2 * n - 2)
                e.reciprocal(REC[:, m:m + 2], SUM[:, m:m + 2]).then_inc(s.rec_done, 1)
                e.wait_ge(s.rec_done, n + 1)
                for h in range(2):
                    e.tensor_scalar(SS[n % 2][:, h, 0:cols], SS[n % 2][:, h, 0:cols], REC[:, m + h:m + h + 1], None,
                                    ALU.mult).then_inc(s.p_ready, 1)

            def pt_lo(n):
                for p in range(pieces(n)):
                    rows, w = piece(n, p)
                    e.wait_ge(s.pt_hi, CUM[n] + p + 1)
                    flat = [x[:, :, :].rearrange("p a b -> p (a b)")[0:rows, 512 * p:512 * p + w] for x in PT]
                    e.tensor_tensor(flat[1], PS[0:rows, 4 + p, 0:w], flat[0].bitcast(F32), ALU.subtract)\
                        .then_inc(s.pt_lo, 1)

            e.wait_ge(s.stat_read, 13)
            e.reciprocal(CQC[:, :, :, :].rearrange("p j b e -> p (j b e)"),
                         CQR[:, :, :, :].rearrange("p j b e -> p (j b e)")).then_inc(s.cq_rc, 1)
            e.tensor_scalar(GQ[:, 0:1], par_col("q_norm"), -0.125, None, ALU.mult).then_inc(s.gq_ready, 1)
            e.tensor_scalar(GQ[:, 1:3], PAR[:, _cols["xq_norm"]:_cols["xq_norm"] + 2], -0.0625, None, ALU.mult)\
                .then_inc(s.gq_ready, 1)
            e.wait_ge(s.g_lo, 3)
            e.wait_ge(s.stat_done, 14)
            for i in range(2, 6):
                e.memset(y(i)[:, TOK:T], 0.0).then_inc(s.pad_ready, 1)
            e.wait_ge(s.gq_ready, 2)
            prep(0)
            biased(0)
            normalise(0)
            for n in range(N_U):
                if n + 1 < N_U:
                    biased(n + 1)
                    normalise(n + 1)
                pt_lo(n)
                if n % 9 == 5 and n < 27:
                    prep(n // 9 + 1)

            e.wait_ge(s.o_sq, 4)
            e.tensor_tensor(OS[0][:, :], OS[0][:, :], OS[1][:, :], ALU.add).then_inc(s.o_sum, 1)
            e.tensor_tensor(OS[2][:, :], OS[2][:, :], OS[3][:, :], ALU.add).then_inc(s.o_sum, 1)
            e.wait_ge(s.o_sum, 2)
            e.tensor_tensor(OS[0][:, :], OS[0][:, :], OS[2][:, :], ALU.add).then_inc(s.o_sum, 1)
            dve_split(e, S_OUT, 0)
            dve_split(e, S_OUT + 1, 1)
            e.wait_ge(s.o_sum, 3)
            e.wait_ge(s.q_hi, 2)
            e.tensor_tensor(RL[:, :], OS[0][:, :], TH[:, :].bitcast(F32), ALU.subtract).then_inc(s.q_lo, 1)

            def b_lo(n, k):
                e.wait_ge(s.b_hi, n + 1)
                sl = slice(k * T, (k + 1) * T)
                e.tensor_tensor(B[1][:, sl], y(k), B[0][:, sl].bitcast(F32), ALU.subtract).then_inc(s.b_lo, 1)
            b_lo(0, 0)
            dve_recip(e, cnt)
            cnt.bc += 3
            cnt.other = 36
            for n, k in enumerate((1, 6, 7)):
                b_lo(n + 1, k)
            e.wait_ge(s.bc_used, cnt.used(cnt.bc))
            for i in range(4):
                e.scalar_tensor_tensor(y(2 + i), y(2 + i), par_col("out_norm", 2 + i), RSTD[:, :],
                                       ALU.mult, ALU.mult).then_inc(s.o_nrm, 1)
            for i in range(4):
                e.wait_ge(s.o_nrm, i + 1)
                b_lo(4 + i, 2 + i)
            e.wait_ge(s.o_nrm, 4)
            e.memset(ACC[:, :], 0.0).then_inc(s.acc_zero, 1)

            def residual(t0, i, par, norm, src_in, acc0, src0=0):
                m = i * 2 + par
                e.wait_ge(s.tile_done, m + (t0 + 1))
                e.wait_ge(src_in, m * 16 + (16 + src0))
                ym = Y[:, bass.ds(m * T, T)]
                e.tensor_tensor(chunks(ym), ps_tile(par), chunks(ym), ALU.add).then_inc(s.tile_read, 1)
                e.wait_ge(s.a_hi, m + (acc0 + 1))
                e.wait_ge(s.tile_read, m + (t0 + 1))
                e.scalar_tensor_tensor(A[1][:, bass.ds(m * T, T)], ym, PAR[:, bass.ds(m + _cols[norm], 1)],
                                       A[0][:, bass.ds(m * T, T)].bitcast(F32), ALU.mult, ALU.subtract)\
                    .then_inc(s.a_lo, 1)
                e.wait_ge(s.sq_done, m + (acc0 + 1))
                e.wait_ge(s.acc_done, m + acc0)
                e.tensor_tensor(ACC[:, :], ACC[:, :], TT[:, :], ALU.add).then_inc(s.acc_done, 1)

            e.wait_ge(s.acc_zero, 1)
            with e.Fori(0, 4) as i:
                for par in range(2):
                    residual(S_OUT, i, par, "norm_x", s.x2_in, 8)
                    dve_split(e, i * 2 + (S_OUT + 2 + par), par)
            e.wait_ge(s.q_hi, 3)
            e.wait_ge(s.acc_done, 16)
            e.tensor_tensor(RL[:, :], ACC[:, :], TH[:, :].bitcast(F32), ALU.subtract).then_inc(s.q_lo, 1)

            def xevac(i):
                e.wait_ge(s.tile_done, S_XQ + i + 1)
                e.wait_ge(s.y1_out, 16 * (i + 1))
                e.wait_ge(s.sq_done, 16)
                e.wait_ge(s.a_lo, 16)
                e.tensor_tensor(chunks(y(i)), ps_tile(i % 2), chunks(RSTD[:, :]), ALU.mult).then_inc(s.tile_read, 1)

            def xq_nrm(h):
                e.wait_ge(s.xs_sq, 2 * h + 2)
                for c, (lo, hi, _) in enumerate(BC):
                    e.wait_ge(s.bc_done, cnt.bc + 1)
                    if c == 0:
                        e.wait_ge(s.tile_read, S_XQ + 2 * h + 2)
                    for k in range(2):
                        ins = e.scalar_tensor_tensor(y(2 * h + k)[:, lo:hi], y(2 * h + k)[:, lo:hi],
                                                     GQ[:, 1 + k:2 + k], PS[:, 6 if c == 1 else 7, 0:hi - lo],
                                                     ALU.mult, ALU.mult)
                    ins.then_inc(s.bc_used, 1)
                    cnt.bc += 1

            dve_recip(e, cnt)
            cnt.bc += 3
            e.wait_ge(s.bc_used, cnt.used(cnt.bc))
            for i in range(8):
                if i < 6:
                    dve_split(e, S_XQ + i + 2, i % 2)
                xevac(i)
                h = i // 2
                if i % 2:
                    if h:
                        xq_nrm(h - 1)
                    e.wait_ge(s.xs_sq, 2 * h + 2)
                    e.tensor_tensor(XSQ[0][:, :], XSQ[0][:, :], XSQ[1][:, :], ALU.add).then_inc(s.xs_sum, 1)
                    e.wait_ge(s.q_hi, 4 + h)
                    e.wait_ge(s.xs_sum, h + 1)
                    e.tensor_tensor(XQL[:, :], XSQ[0][:, :], XQH[:, :].bitcast(F32), ALU.subtract).then_inc(s.q_lo, 1)
                if i % 2 == 0 and i:
                    dve_recip(e, cnt)
            dve_recip(e, cnt)
            xq_nrm(3)

            def xprep(h):
                r = CX[h % 2]
                e.wait_ge(s.xq_hi, h + 1)
                e.tensor_tensor(r.Q[1][:, :], Y[:, 2 * h * T:(2 * h + 2) * T], r.Q[0][:, :].bitcast(F32),
                                ALU.subtract).then_inc(s.xq_lo, 1)
                e.wait_ge(s.xkv_hi, h + 1)
                e.tensor_tensor(r.KV[1][:, :, :], XR[:, :, :], r.KV[0][:, :, :].bitcast(F32),
                                ALU.subtract).then_inc(s.xkv_lo, 1)

            def xmin(u):
                nb = xblocks(u)
                m = 2 * (u % 2)
                e.wait_ge(s.x_s, u + 1)
                if u >= 2:
                    e.wait_ge(s.x_exp, xexps(u - 1))
                e.tensor_reduce(MIN[:, m:m + nb], PS[:, u % 2, 0:nb * NMEM].rearrange("p (b k) -> p b k", k=NMEM),
                                AX.X, ALU.min).then_inc(s.x_min, 1)

            def xnorm(u):
                nb = xblocks(u)
                m = 2 * (u % 2)
                e.wait_ge(s.x_exp, xexps(u + 1))
                if u >= 2:
                    e.wait_ge(s.x_p, u - 1)
                e.reciprocal(REC[:, m:m + nb], SUM[:, m:m + nb]).then_inc(s.x_rec, 1)
                e.wait_ge(s.x_rec, u + 1)
                e.tensor_tensor(XS[:, u % 2, 0:nb], XS[:, u % 2, 0:nb],
                                REC[:, m:m + nb].unsqueeze(2).to_broadcast([P, nb, NMEM]), ALU.mult)\
                    .then_inc(s.x_p, 1)

            def xpt_lo(q):
                w = 512 if q % 3 < 2 else P
                k = 2 + 2 * (q % 2)
                e.wait_ge(s.x_pthi, q + 1)
                e.tensor_tensor(XPT[1][:, :, 0:w], PS[:, k:k + 2, 0:w], XPT[0][:, :, 0:w].bitcast(F32),
                                ALU.subtract).then_inc(s.x_ptlo, 1)

            def xo_lo(q):
                h, g = divmod(q, 3)
                for d in range(2):
                    lo, c, w = (512 * g, 0, 512) if g < 2 else (SEQ, 64, 64)
                    col = (2 * h + d) * T + lo
                    e.wait_ge(s.x_ohi, 2 * q + d + 1)
                    e.tensor_tensor(B[1][:, col:col + w], PS[:, 6 + d, c:c + w], B[0][:, col:col + w].bitcast(F32),
                                    ALU.subtract).then_inc(s.x_olo, 1)

            for X in B:
                e.wait_ge(s.tile_done, S_XQ)
                e.wait_ge(s.stat_done, N_STAT_X + 4)
                e.wait_ge(s.q_lo, 7)
                e.memset(X[:, :].bitcast(F32).rearrange("p (k t) -> p k t", t=T)[:, :, TOK:T], 0.0).then_inc(s.o_pad, 1)
            xprep(0)
            xmin(0)
            xnorm(0)
            done = None
            for u in range(N_XU):
                if u + 1 < N_XU:
                    xmin(u + 1)
                    xnorm(u + 1)
                if done is not None:
                    xo_lo(done)
                    done = None
                q, last = xgroup(u)
                if last:
                    xpt_lo(q)
                    done = q
                if u % 5 == 1 and u < 15:
                    xprep(u // 5 + 1)
            xo_lo(done)

            dve_split(e, S_XO, 0)
            e.wait_ge(s.xkv_lo, 4)
            e.memset(ACC[:, :], 0.0).then_inc(s.acc_zero, 1)
            dve_split(e, S_XO + 1, 1)
            e.wait_ge(s.acc_zero, 2)
            with e.Fori(0, 4) as i:
                for par in range(2):
                    residual(S_XO, i, par, "norm_ff", s.y1_in, 16)
                    dve_split(e, i * 2 + (S_XO + 2 + par), par)
            e.wait_ge(s.q_hi, 8)
            e.wait_ge(s.acc_done, 24)
            e.tensor_tensor(RL[:, :], ACC[:, :], TH[:, :].bitcast(F32), ALU.subtract).then_inc(s.q_lo, 1)

            def relu(t, j, h0):
                e.wait_ge(s.tile_done, t + 1)
                e.wait_ge(s.h_lo, h0 + j)
                e.wait_ge(s.tile_read, t)
                e.scalar_tensor_tensor(chunks(HID[:, :]), ps_tile(j % 2), 0.0, chunks(RSTD[:, :]),
                                       ALU.max, ALU.mult).then_inc(s.tile_read, 1)

            def hidden_lo(h0, j, slot):
                e.wait_ge(s.h_hi, h0 + (j + 1))
                col = (slot + j) * T
                e.tensor_tensor(B[1][:, col:col + T], HID[:, :], B[0][:, col:col + T].bitcast(F32), ALU.subtract)\
                    .then_inc(s.h_lo, 1)

            def down(g, j):
                for k in range(2):
                    m = 2 * j + k
                    e.wait_ge(s.tile_done, td(g) + (m + 1))
                    e.wait_ge(s.tile_read, td(g) + m)
                    e.tensor_tensor(chunks(y(m)), ps_tile(k), chunks(y(m)), ALU.add).then_inc(s.tile_read, 1)
                    if k == 0:
                        continue
                    if not isinstance(g, int) or g < N_G - 1 or j < 2:
                        dve_split(e, sd(g) + (j + 2), j % 2)

            def mlp_group(g, half):
                if not isinstance(g, int) or g < N_G - 1:
                    for j in range(4):
                        relu(tu(g) + j, j, g * 4 + 4)
                        dve_split(e, su(g) + (j + 2), j % 2)
                        hidden_lo(g * 4 + 4, j, 4 * (1 - half))
                for j in range(4):
                    down(g, j)

            dve_recip(e, cnt)
            cnt.bc += 3
            e.wait_ge(s.bc_used, cnt.used(cnt.bc))
            for j in range(4):
                relu(S_UP + j, j, 0)
                dve_split(e, S_UP + j + 2, j % 2)
                hidden_lo(0, j, 0)
            with e.Fori(0, 3) as i:
                mlp_group(i * 2, 0)
                mlp_group(i * 2 + 1, 1)
            mlp_group(6, 0)
            mlp_group(7, 1)

        @block.tensor
        def _(e):
            cnt = Count()
            e.wait_ge(s.const_ready, 6)

            def mem_tile(par):
                for k in range(KT):
                    for m, (wt, xt) in enumerate(((WH, MX[0]), (WH, MX[1]), (WL, MX[0]))):
                        ins = e.matmul(PS[:, 3 * par, 0:NMEM], wt[:, par, k * P:(k + 1) * P],
                                       xt[:, k * NMEM:(k + 1) * NMEM],
                                       start=(k == 0 and m == 0), stop=(k == KT - 1 and m == 2))
                ins.then_inc(s.tile_done, 1)

            e.wait_ge(s.mem_lo, 8)
            e.wait_ge(s.w_lo, 1)
            mem_tile(0)
            e.wait_ge(s.mem_qlo, 1)
            for b in range(2):
                for n, src in enumerate((MQH, MQL)):
                    ins = e.matmul(PS[:, 6, 2 * b:2 * b + 2], src[:, b * P:(b + 1) * P], ONE[:, :],
                                   start=(n == 0), stop=(n == 1))
            ins.then_inc(s.stat_done, 1)
            cnt.stat += 1
            e.wait_ge(s.ck_rc, 1)
            for b in range(2):
                ins = e.transpose(PS[:, 7, b * P:(b + 1) * P], CKC[:, b:b + 1].to_broadcast([P, P]), ID[:, :])
            ins.then_inc(s.bc_done, 1)
            cnt.bc += 1
            e.wait_ge(s.w_lo, 2)
            mem_tile(1)
            with e.Fori(1, 8) as i:
                for par in range(2):
                    e.wait_ge(s.w_lo, i * 2 + par + 1)
                    e.wait_ge(s.tile_read, i * 2 + par - 1)
                    mem_tile(par)

            def win_tile(i):
                e.wait_ge(s.w_lo, S_IN + i + 1)
                e.wait_ge(s.tile_read, S_IN + i - 1)
                if i == 0:
                    e.wait_ge(s.a_lo, 8)
                pe_tile(e, i % 2, i % 2, A)

            def rc_wait(n):
                return lambda: e.wait_ge(s.rc_done, n)

            def crc(b):
                return CRC[:, b:b + 1].to_broadcast([P, P])

            win_tile(0)
            e.wait_ge(s.q_lo, 1)
            pe_stat(e, cnt, (TH, RL), ONE, cnt.bc)
            pe_bcast(e, cnt, crc, rc_wait(1))
            e.wait_ge(s.kq_lo, 1)
            e.wait_ge(s.bc_used, cnt.bc)
            for h in range(4):
                for b in range(2):
                    c = 2 * (2 * h + b)
                    for n, (src, k) in enumerate(((KQH, 0), (KQL, 0), (KQH, 1), (KQL, 1))):
                        ins = e.matmul(PS[:, 6, c:c + 2], src[:, 2 * h + k, b * P:(b + 1) * P], ONE[:, :],
                                       start=(n == 0), stop=(n == 3))
            ins.then_inc(s.stat_done, 1)
            cnt.stat += 1
            win_tile(1)
            e.wait_ge(s.ck_rc, 2)
            e.wait_ge(s.stat_read, cnt.stat)
            for h in range(4):
                for b in range(2):
                    c = 2 * h + b
                    ins = e.transpose(PS[:, 6 + h // 2, (c % 4) * P:(c % 4 + 1) * P],
                                      CKC[:, c:c + 1].to_broadcast([P, P]), ID[:, :])
                if h % 2:
                    ins.then_inc(s.mk_bc, 1)
            win_tile(2)
            for n in range(4):
                if n < 2:
                    e.wait_ge(s.mk_norm, 4 * n + 4)
                else:
                    e.wait_ge(s.mv_cp, n - 1)
                for f in range(4):
                    ins = e.transpose(PS[:, 6 + n % 2, f * P:(f + 1) * P],
                                      KV[:, 8 + 4 * (n % 2) + f, (n // 2) * P:(n // 2 + 1) * P], ID[:, :])
                ins.then_inc(s.mv_tr, 1)
            n_rc = 1
            for i in range(3, 22):
                win_tile(i)
                if i == 4:
                    e.wait_ge(s.mv_cp, 4)
                if i == 11:
                    e.wait_ge(s.g_lo, 1)
                    pe_stat(e, cnt, (Y5R, TH), ONE, cnt.bc)
                if 12 <= i <= 19:
                    j = i - 12
                    e.wait_ge(s.qk_lo, j + 1)
                    pe_stat(e, cnt, (Y5R, TH), SEL, cnt.bc)
                if i == 12:
                    n_rc += 1
                    pe_bcast(e, cnt, crc, rc_wait(n_rc))
                if i == 19:
                    e.wait_ge(s.xa_lo, 2)
                    pe_stat(e, cnt, (XH[0], XL[0], XH[1], XL[1]), ONE, cnt.bc)
                    st = cnt.stat
                    pe_bcast(e, cnt, lambda b: CRT[:, b:b + 1].to_broadcast([P, P]), lambda: e.wait_ge(s.stat_read, st))
                if i == 20:
                    e.wait_ge(s.g_lo, 2)
                    pe_stat(e, cnt, (Y5R, TH), ONE, cnt.bc)
                    n_rc += 1
                    pe_bcast(e, cnt, crc, rc_wait(n_rc))
                if i == 21:
                    e.wait_ge(s.g_lo, 3)
                    pe_stat(e, cnt, (Y5R, TH), ONE, cnt.bc)
                    n_rc += 1
                    pe_bcast(e, cnt, crc, rc_wait(n_rc))

            def prep(j):
                r = AT[j % 2]
                for which in range(2):
                    n = 2 * j + which + 1
                    pe_bcast(e, cnt, lambda b: RX[:, b].rearrange("p e d -> p (e d)"), lambda: e.wait_ge(s.rx_ready, n),
                             used)
                for c in range(3):
                    n = cnt.bc
                    used(n if c == 0 else n - 1)
                    for b in range(3 * c, 3 * c + 3):
                        w = P if b < 8 else 64
                        ins = e.transpose(PS[0:w, 6 if c == 1 else 7, (b % 3) * P:(b % 3 + 1) * P],
                                          QKV[8 + j][:, b * P:b * P + w], ID[:, :])
                    ins.then_inc(s.bc_done, 1)
                    cnt.bc += 1

            def scores(n):
                j, b = divmod(n, 9)
                r = AT[j % 2]
                tiles, cols, _ = keys(n)
                if b == 0:
                    e.wait_ge(s.qk2_lo, 2 * j + 2)
                    e.wait_ge(s.kc_lo, 2 * j + 2)
                if n:
                    e.wait_ge(s.ttr_done, 2 * n)
                q0 = P * b if b < 8 else TOK - P
                if b < 8:
                    k0 = P * max(0, b - 4)
                    parts = [(r.K, k0, min(512, cols), 0)] + ([(r.K, k0 + 512, cols - 512, 1)] if cols > 512 else [])
                else:
                    parts = [(r.KC, 0, 512, 0), (r.K, SEQ, 64, 1)]
                for K, k0, w, bank in parts:
                    for m, (qx, kx) in enumerate(((0, 0), (1, 0), (0, 1))):
                        for h in range(2):
                            rows = slice(64 * h, 64 * h + 64)
                            ins = e.matmul(PS[:, 2 * h + bank, 0:w], r.Q[qx][rows, q0:q0 + P], K[kx][rows, k0:k0 + w],
                                           start=(m == 0), stop=(m == 2))
                ins.then_inc(s.s_done, 1)

            def transposes(n):
                tiles, cols, _ = keys(n)
                e.wait_ge(s.p_ready, 2 * n + 2)
                if n:
                    e.wait_ge(s.pt_lo, CUM[n])
                for kt in range(tiles):
                    w = min(P, cols - kt * P)
                    for h in range(2):
                        ins = e.transpose(PS[0:w, 4 + kt // 2, (kt % 2) * 256 + h * P:(kt % 2) * 256 + h * P + P],
                                          SS[n % 2][:, h, kt * P:kt * P + w], ID[:, :])
                ins.then_inc(s.t_done, 1)

            def values(n):
                j, b = divmod(n, 9)
                r = AT[j % 2]
                tiles, cols, _ = keys(n)
                if b == 0:
                    e.wait_ge(s.v_lo, 4 * j + 4)
                if b == 5 and j < 3:
                    e.wait_ge(s.v_lo, 4 * j + 8)
                if n:
                    e.wait_ge(s.o_used, 2 * n)
                for kt in range(tiles):
                    if kt % 2 == 0:
                        e.wait_ge(s.pt_lo, CUM[n] + kt // 2 + 1)
                    w = min(P, cols - kt * P)
                    for m, (vx, px) in enumerate(((0, 0), (0, 1), (1, 0))):
                        if b < 8:
                            lhs = r.V[vx][:, max(0, b - 4) + kt]
                        else:
                            lhs = r.VC[vx][:, kt] if kt < 4 else r.V[vx][0:w, 8]
                        ins = e.matmul(PS[:, 7, 0:256], lhs, PT[px][0:w, kt],
                                       start=(kt == 0 and m == 0), stop=(kt == tiles - 1 and m == 2))
                ins.then_inc(s.pv_done, 1)

            def used(n):
                k = n - N_ACT_BC
                if k <= 0:
                    e.wait_ge(s.bc_used, n)
                    return
                j, k = divmod(k, 9)
                if k == 0:
                    j, k = j - 1, 9
                if k <= 3:
                    e.wait_ge(s.q_nrm, 3 * j + k)
                elif k <= 6:
                    e.wait_ge(s.k_nrm, 3 * j + k - 3)
                else:
                    e.wait_ge(s.v_lo, 4 * j + k - 6 + (k == 9))
            N_ACT_BC = cnt.bc
            e.wait_ge(s.tile_read, S_OUT)
            prep(0)
            scores(0)
            for n in range(N_U):
                if n + 1 < N_U:
                    scores(n + 1)
                if n:
                    values(n - 1)
                transposes(n)
                if n % 9 == 5 and n < 27:
                    e.wait_ge(s.o_used, 2 * n)
                    e.wait_ge(s.pt_lo, CUM[n + 1])
                    prep(n // 9 + 1)
            values(N_U - 1)

            e.wait_ge(s.q_lo, 2)
            pe_stat(e, cnt, (TH, RL), ONE, 0)
            n_rc += 1
            e.wait_ge(s.o_used, 2 * N_U)
            cnt.other = 36
            pe_bcast(e, cnt, crc, rc_wait(n_rc))
            e.wait_ge(s.w_lo, S_OUT + 1)
            pe_tile(e, 0, 0, B, order=KORD, kwait=lambda k: e.wait_ge(s.b_lo, KORD.index(k) + 1))
            e.wait_ge(s.w_lo, S_OUT + 2)
            pe_tile(e, 1, 1, B)
            with e.Fori(1, 4) as i:
                for par in range(2):
                    e.wait_ge(s.w_lo, i * 2 + (S_OUT + par + 1))
                    e.wait_ge(s.tile_read, i * 2 + (S_OUT + par - 1))
                    pe_tile(e, par, par, B)

            def xq_tile(i):
                e.wait_ge(s.w_lo, S_XQ + i + 1)
                e.wait_ge(s.tile_read, S_XQ + i - 1)
                pe_tile(e, i % 2, i % 2, A)

            def xq_stat(h):
                e.wait_ge(s.q_lo, 4 + h)
                pe_stat(e, cnt, (XQH, XQL), ONE, cnt.used(cnt.bc))

            e.wait_ge(s.a_lo, 16)
            xq_tile(0)
            e.wait_ge(s.q_lo, 3)
            pe_stat(e, cnt, (TH, RL), ONE, cnt.used(cnt.bc))
            assert cnt.stat == N_STAT_X, cnt.stat
            n_rc += 1
            pe_bcast(e, cnt, crc, rc_wait(n_rc))
            xq_tile(1)
            for h in range(3):
                xq_tile(2 * h + 2)
                xq_stat(h)
                xq_tile(2 * h + 3)
                n_rc += 1
                pe_bcast(e, cnt, crc, rc_wait(n_rc))
            xq_stat(3)
            n_rc += 1
            pe_bcast(e, cnt, crc, rc_wait(n_rc))

            def xscores(u):
                h, p = divmod(u, 5)
                r = CX[h % 2]
                kk = 0 if p < 4 else 2
                if p == 0:
                    e.wait_ge(s.xq_lo, h + 1)
                    e.wait_ge(s.xkv_lo, h + 1)
                if u >= 2:
                    e.wait_ge(s.x_exp, xexps(u - 1))
                for b in range(xblocks(u)):
                    q0 = P * (2 * p + b) if p < 4 else TOK - P
                    for n, (k, qx, kx) in enumerate((k, qx, kx) for k in range(2) for qx, kx in ((0, 0), (1, 0), (0, 1))):
                        ins = e.matmul(PS[:, u % 2, b * NMEM:(b + 1) * NMEM], r.Q[qx][:, k * T + q0:k * T + q0 + P],
                                       r.KV[kx][:, kk, k * NMEM:(k + 1) * NMEM], start=(n == 0), stop=(n == 5))
                ins.then_inc(s.x_s, 1)

            def xtransposes(u):
                q, _ = xgroup(u)
                e.wait_ge(s.x_p, u + 1)
                if q >= 2:
                    e.wait_ge(s.x_ptlo, q - 1)
                for b in range(xblocks(u)):
                    c = (u % 5 % 2) * 2 + b if u % 5 < 4 else 0
                    for k in range(2):
                        ins = e.transpose(PS[:, 2 + 2 * (q % 2) + k, c * P:(c + 1) * P],
                                          XS[:, u % 2, b, k * P:(k + 1) * P], ID[:, :])
                ins.then_inc(s.x_t, 1)

            def xvalues(q):
                h, g = divmod(q, 3)
                r = CX[h % 2]
                vv = 1 if g < 2 else 3
                w = 512 if g < 2 else P
                e.wait_ge(s.x_ptlo, q + 1)
                if q:
                    e.wait_ge(s.x_olo, 2 * q)
                else:
                    e.wait_ge(s.bc_used, cnt.used(cnt.bc))
                for d in range(2):
                    for n, (k, vx, px) in enumerate((k, vx, px) for k in range(2) for vx, px in ((0, 0), (0, 1), (1, 0))):
                        v0 = k * NMEM + d * P
                        ins = e.matmul(PS[:, 6 + d, 0:w], r.KV[vx][:, vv, v0:v0 + P], XPT[px][:, k, 0:w],
                                       start=(n == 0), stop=(n == 5))
                ins.then_inc(s.x_pv, 1)

            e.wait_ge(s.tile_read, S_XO)
            xscores(0)
            done = None
            for u in range(N_XU):
                if u + 1 < N_XU:
                    xscores(u + 1)
                if done is not None:
                    xvalues(done)
                    done = None
                q, last = xgroup(u)
                xtransposes(u)
                if last:
                    done = q
            xvalues(done)

            e.wait_ge(s.x_olo, 2 * N_XQ)
            e.wait_ge(s.o_pad, 2)
            with e.Fori(0, 4) as i:
                for par in range(2):
                    e.wait_ge(s.w_lo, i * 2 + (S_XO + par + 1))
                    e.wait_ge(s.tile_read, i * 2 + (S_XO + par - 1))
                    pe_tile(e, par, par, B)

            def up(t, sl, j):
                e.wait_ge(s.w_lo, sl + (j + 1))
                e.wait_ge(s.tile_read, t + (j - 1))
                pe_tile(e, j % 2, j % 2, A)

            def mlp_group(g, half):
                if not isinstance(g, int) or g < N_G - 1:
                    for j in range(4):
                        up(tu(g), su(g), j)
                e.wait_ge(s.h_lo, g * 4 + 4)
                for j in range(4):
                    for k in range(2):
                        e.wait_ge(s.w_lo, sd(g) + (j + 1))
                        e.wait_ge(s.tile_read, td(g) + (2 * j + k - 1))
                        pe_tile(e, k, j % 2, B, nk=4, k0=4 * half, woff=512 * k)

            e.wait_ge(s.a_lo, 24)
            up(S_UP, S_UP, 0)
            e.wait_ge(s.q_lo, 8)
            pe_stat(e, cnt, (TH, RL), ONE, cnt.used(cnt.bc))
            n_rc += 1
            pe_bcast(e, cnt, crc, rc_wait(n_rc))
            for j in range(1, 4):
                up(S_UP, S_UP, j)
            with e.Fori(0, 3) as i:
                mlp_group(i * 2, 0)
                mlp_group(i * 2 + 1, 1)
            mlp_group(6, 0)
            mlp_group(7, 1)


_INS = ["xT", "memT", "slabs", "par", "rbrev", "ctxa", "ctxc", "kcT", "vc", "mkcT", "mvc"]
_OUTS = {"o_y": (KT, P, T), "o_ca": (2, 2, P, CA), "o_cc": (2, 2, P, CC), "o_k": (4, P, 576), "o_v": (4, P, 576),
         "o_kc": (4, P, 448), "o_vc": (448, 512), "o_mk": (KT, P, NMEM), "o_mv": (2, P, D)}


def layout(inp):
    f = lambda n: np.asarray(inp[n])
    xT = np.zeros((D, T), np.float32)
    xT[:, :SEQ] = f("x_prompt")[0].T
    xT[:, SEQ:TOK] = f("x_sample")[0].T

    def k1024(w):
        return w.reshape(KT, P, -1, P).transpose(2, 1, 0, 3).reshape(-1, P, D)

    up = k1024(f("w_up")[0])
    down = f("w_down")[0].reshape(N_G, 4, P, 4, 2, P).transpose(0, 3, 2, 4, 1, 5).reshape(N_G, 4, P, D)
    mlp = [up[0:4]]
    for g in range(N_G):
        if g + 1 < N_G:
            mlp.append(up[4 * g + 4:4 * g + 8])
        mlp.append(down[g])
    slabs = np.concatenate([k1024(f("w_xk")[0]), k1024(f("w_xv")[0]), k1024(f("w_in")[0])[IN_ORDER],
                            k1024(f("w_out")[0]), k1024(f("w_xq")[0]), k1024(f("w_xo")[0])] + mlp)

    def cols(v):
        return v.reshape(-1, P).T
    par = np.concatenate([
        cols(f("norm_mix")[0]), cols(f("norm_x")[0]), cols(f("norm_ff")[0]), cols(f("norm_mem")[0]),
        cols(f("out_norm")[0]), cols(f("ln_a_g")[0]), cols(f("ln_a_b")[0]), cols(f("conv_a_b")[0]),
        cols(f("conv_a_w")[0]), cols(f("conv_c_w")[0]), cols(np.tile(f("q_norm")[0], 2)),
        cols(np.tile(f("k_norm")[0], 2)), cols(f("xq_norm")[0]), cols(f("xk_norm")[0])], axis=1)
    a = {
        "xT": xT.reshape(KT, P, T), "memT": f("mem_prompt")[0].T.reshape(KT, P, NMEM), "slabs": slabs, "par": par,
        "rbrev": f("rel_bias")[0][:, ::-1],
        "ctxa": f("cache_conv_a")[0, 0].T.reshape(2, P, CA), "ctxc": f("cache_conv_c")[0, 0].T.reshape(2, P, CC),
        "kcT": f("cache_band_k")[0, 0].reshape(512, 512).T.reshape(4, P, 512),
        "vc": f("cache_band_v")[0, 0].reshape(4, P, 512),
        "mkcT": f("cache_mem_k")[0, 0].reshape(NMEM, D).T.reshape(KT, P, NMEM),
        "mvc": f("cache_mem_v")[0, 0].reshape(2, P, D)}
    return {n: np.ascontiguousarray(v) for n, v in a.items()}


def returned(o):
    yT = o["o_y"].reshape(D, T)
    ca = o["o_ca"].reshape(2, 256, CA).transpose(0, 2, 1)
    cc = o["o_cc"].reshape(2, 256, CC).transpose(0, 2, 1)
    kn, vn = (o[n].reshape(512, 576).T for n in ("o_k", "o_v"))
    kc, vc = o["o_kc"].reshape(512, 448).T, o["o_vc"]
    band = lambda a: a.reshape(1, 1, -1, 8, 64)
    c = np.ascontiguousarray
    return tuple(c(x) for x in (
        yT[:, :SEQ].T[None], yT[:, SEQ:TOK].T[None], ca[0][None, None], band(kn[:512]), band(vn[:512]), cc[0][None, None],
        o["o_mk"].reshape(D, NMEM).T.reshape(1, 1, NMEM, 4, 256), o["o_mv"].reshape(1, 1, NMEM, 4, 256),
        ca[1][None, None], band(np.concatenate([kc, kn[512:]])), band(np.concatenate([vc, vn[512:]])), cc[1][None, None]))


def kernel(**inputs):
    import concourse.bacc as bacc
    from concourse.bass_utils import run_bass_kernel_spmd

    nc = bacc.Bacc("TRN2", target_bir_lowering=False, num_devices=1)
    arrays = layout(inputs)
    args = [nc.dram_tensor(n, arrays[n].shape, F32, kind="ExternalInput").ap() for n in _INS]
    args += [nc.dram_tensor(n, shape, F32, kind="ExternalOutput").ap() for n, shape in _OUTS.items()]
    build(nc, *args)
    r = run_bass_kernel_spmd(nc, [arrays], core_ids=[0])
    return returned({n: np.asarray(r.results[0][n]) for n in _OUTS})
```

```python
from contextlib import ExitStack

import numpy as np

import concourse.bass as bass
from concourse import mybir

F32 = mybir.dt.float32
F32R = mybir.dt.float32r
ACT = mybir.ActivationFunctionType
ALU = mybir.AluOpType
AX = mybir.AxisListType

P = 128
D = 1024
KT = D // P
SEQ, DEC = 1024, 64
NCH = 3
CH = 364
T = NCH * CH
TOK = SEQ + DEC
NMEM = 256
CA = 30
CC = 2
EPS = 1e-6
BIG = 1e30
BLK = [128 * b for b in range(8)] + [T - 128]
BC = [(0, 384, (0, 1, 2)), (384, 768, (3, 4, 5)), (768, T, (6, 7, 8))]

_cols = {}
_n = 0
for _name, _w in (("norm_mix", 8), ("norm_x", 8), ("norm_ff", 8), ("norm_mem", 8), ("out_norm", 8),
                  ("ln_a_g", 2), ("ln_a_b", 2), ("conv_a_b", 2), ("conv_a_w", 62), ("conv_c_w", 6),
                  ("q_norm", 1), ("k_norm", 1), ("xq_norm", 2), ("xk_norm", 2)):
    _cols[_name] = _n
    _n += _w
NPAR = _n

S_MEM, S_IN, S_OUT, S_XQ, S_XO, S_UP = 0, 16, 38, 46, 54, 62
N_SLABS = 126
N_G = 8

IN_ORDER = [0, 2, 1, 3, 18, 20, 16, 19, 21, 17] + list(range(4, 16))
TAPS = {4: 4, 5: 3, 6: 3, 7: 5, 8: 3, 9: 3, 10: 6, 11: 5, 12: 4, 13: 5, 14: 6, 15: 5, 16: 5, 17: 5}


class Semaphores:

    def __init__(self, sem):
        self.params_in = sem("params_in")
        self.mem_in0 = sem("mem_in0")
        self.mem_in1 = sem("mem_in1")
        self.x_in = sem("x_in")
        self.w_in0 = sem("w_in0")
        self.w_in1 = sem("w_in1")
        self.w_in_mem0 = sem("w_in_mem0")
        self.w_in_mem1 = sem("w_in_mem1")
        self.w_hi = sem("w_hi")
        self.w_lo = sem("w_lo")
        self.zero_ready = sem("zero_ready")
        self.const_ready = sem("const_ready")
        self.pad_ready = sem("pad_ready")
        self.tile_done = sem("tile_done")
        self.tile_read = sem("tile_read")
        self.stat_done = sem("stat_done")
        self.stat_read = sem("stat_read")
        self.rc_done = sem("rc_done")
        self.bc_done = sem("bc_done")
        self.bc_used = sem("bc_used")
        self.a_hi = sem("a_hi")
        self.a_lo = sem("a_lo")
        self.sq_done = sem("sq_done")
        self.acc_done = sem("acc_done")
        self.acc_zero = sem("acc_zero")
        self.mem_hi = sem("mem_hi")
        self.mem_lo = sem("mem_lo")
        self.mem_sq = sem("mem_sq")
        self.mem_sum = sem("mem_sum")
        self.kq_sq = sem("kq_sq")
        self.ck_rc = sem("ck_rc")
        self.mk_bc = sem("mk_bc")
        self.mk_norm = sem("mk_norm")
        self.mv_tr = sem("mv_tr")
        self.mv_cp = sem("mv_cp")
        self.mem_stored = sem("mem_stored")
        self.sig_done = sem("sig_done")
        self.ue_done = sem("ue_done")
        self.ctx_in = sem("ctx_in")
        self.state_out = sem("state_out")
        self.conv_step = sem("conv_step")
        self.uc_done = sem("uc_done")
        self.c3_done = sem("c3_done")
        self.yc_done = sem("yc_done")
        self.g_sq = sem("g_sq")
        self.g_sum = sem("g_sum")
        self.xa_sub = sem("xa_sub")
        self.xa_nrm = sem("xa_nrm")
        self.ya_sig = sem("ya_sig")
        self.ya_done = sem("ya_done")
        self.gn_done = sem("gn_done")
        self.qk_sq = sem("qk_sq")
        self.bx_in = sem("bx_in")
        self.bx_done = sem("bx_done")
        self.ext_out = sem("ext_out")
        self.rep_out = sem("rep_out")
        self.bias_in = sem("bias_in")
        self.bias_ready = sem("bias_ready")
        self.cache_in = sem("cache_in")
        self.cache_out = sem("cache_out")
        self.kv_out = sem("kv_out")
        self.cq_rc = sem("cq_rc")
        self.gq_ready = sem("gq_ready")
        self.rx_ready = sem("rx_ready")
        self.q_nrm = sem("q_nrm")
        self.k_nrm = sem("k_nrm")
        self.qk2_hi = sem("qk2_hi")
        self.qk2_lo = sem("qk2_lo")
        self.kc_hi = sem("kc_hi")
        self.kc_lo = sem("kc_lo")
        self.v_hi = sem("v_hi")
        self.v_lo = sem("v_lo")
        self.s_done = sem("s_done")
        self.ttr_done = sem("ttr_done")
        self.exp_done = sem("exp_done")
        self.rec_done = sem("rec_done")
        self.p_ready = sem("p_ready")
        self.t_done = sem("t_done")
        self.pt_hi = sem("pt_hi")
        self.pt_lo = sem("pt_lo")
        self.pv_done = sem("pv_done")
        self.o_used = sem("o_used")
        self.o_sq = sem("o_sq")
        self.o_sum = sem("o_sum")
        self.o_nrm = sem("o_nrm")
        self.b_hi = sem("b_hi")
        self.b_lo = sem("b_lo")
        self.x2_in = sem("x2_in")
        self.y1_out = sem("y1_out")
        self.xs_sq = sem("xs_sq")
        self.xs_sum = sem("xs_sum")
        self.xkv_in0 = sem("xkv_in0")
        self.xkv_in1 = sem("xkv_in1")
        self.xkv_hi = sem("xkv_hi")
        self.xkv_lo = sem("xkv_lo")
        self.xq_hi = sem("xq_hi")
        self.xq_lo = sem("xq_lo")
        self.x_s = sem("x_s")
        self.x_min = sem("x_min")
        self.x_exp = sem("x_exp")
        self.x_rec = sem("x_rec")
        self.x_p = sem("x_p")
        self.x_t = sem("x_t")
        self.x_pthi = sem("x_pthi")
        self.x_ptlo = sem("x_ptlo")
        self.x_pv = sem("x_pv")
        self.x_ohi = sem("x_ohi")
        self.x_olo = sem("x_olo")
        self.o_pad = sem("o_pad")
        self.y1_in = sem("y1_in")
        self.h_sq = sem("h_sq")
        self.h_hi = sem("h_hi")
        self.h_lo = sem("h_lo")
        self.stored = sem("stored")


class BandOperands:

    def __init__(self, Q, K, V, KC, VC):
        self.Q, self.K, self.V, self.KC, self.VC = Q, K, V, KC, VC


class CrossOperands:

    def __init__(self, Q, KV):
        self.Q, self.KV = Q, KV


def build(nc, xT, memT, slabs, params, rbrev, ctxa, ctxc, kcT, vc, mkcT, mvc,
          o_y, o_ca, o_cc, o_k, o_v, o_kc, o_vc, o_mk, o_mv):
    ctx = ExitStack()
    with ctx:
        base = (nc.sbuf_base + 31) // 32 * 32
        TB = 4 * T
        A0, B0, Y0, W0 = base, base + 16 * TB, base + 32 * TB, base + 40 * TB
        R0 = W0 + 3 * 8192

        def at(name, shape, dt, off):
            return nc.alloc_sbuf_tensor_at(name, shape, dt, offset=off, align_bytes=16)

        def sem(name):
            return ctx.enter_context(nc.semaphore(name))

        A = [at("A_hi", [P, KT * T], F32R, A0), at("A_lo", [P, KT * T], F32R, A0 + 8 * TB)]
        B = [at("B_hi", [P, KT * T], F32R, B0), at("B_lo", [P, KT * T], F32R, B0 + 8 * TB)]
        Y = at("Y", [P, KT * T], F32, Y0)
        RAW = at("w_raw", [P, 2, D], F32, W0)
        WH = at("w_hi", [P, 2, D], F32R, W0 + 8192)
        WL = at("w_lo", [P, 2, D], F32R, W0 + 16384)
        TT = at("square", [P, T], F32, R0)
        RSTD = at("rstd", [P, T], F32, R0 + TB)
        ACC = RSTD
        c0 = R0 + 2 * TB
        ID = at("ident", [P, P], F32, c0)
        ONE = at("ones", [P, 2], F32, c0 + 512)
        SEL = at("half_sel", [P, 2], F32, c0 + 544)
        PAR = at("params", [P, NPAR], F32, c0 + 576)
        c1 = c0 + 576 + (NPAR * 4 + 31) // 32 * 32
        CRT = at("c_root", [P, 9], F32, c1)
        CRC = at("c_rstd", [P, 9], F32, c1 + 64)
        CKR = at("ck_root", [P, 8], F32, c1 + 128)
        CKC = at("ck_rstd", [P, 8], F32, c1 + 160)
        CQR = at("cq_root", [P, 8, 9, 2], F32, c1 + 192)
        CQC = at("cq_rstd", [P, 8, 9, 2], F32, c1 + 192 + 576)
        EPSC = at("eps", [P, 1], F32, c1 + 192 + 1152)
        GQ = at("gq_scaled", [P, 3], F32, c1 + 192 + 1184)
        MIN = at("neg_max", [P, 4], F32, c1 + 192 + 1216)
        SUM = at("exp_sum", [P, 4], F32, c1 + 192 + 1248)
        REC = at("exp_rec", [P, 4], F32, c1 + 192 + 1280)
        assert c1 + 192 + 1312 <= nc.sbuf_usable_end

        MR = at("mem_raw", [P, 8, NMEM], F32, B0)
        MX = [at("mem_hi", [P, 8 * NMEM], F32R, B0 + 8192), at("mem_lo", [P, 8 * NMEM], F32R, B0 + 16384)]
        MSQ = at("mem_sq", [P, 8, NMEM], F32, B0 + 24576)
        KV = at("mem_kv", [P, 16, NMEM], F32, B0 + 32768)
        VMN = at("mem_v", [P, 2, D], F32, B0 + 49152)
        MSUM = at("mem_sum", [P, NMEM], F32, B0 + 57344)
        RM = at("mem_rstd", [P, NMEM], F32, B0 + 60416)
        RAWM = at("w_raw_mem", [P, 2, D], F32, B0 + 61440)

        def slot(name, i, dt=F32):
            return at(name, [P, T], dt, B0 + i * TB)

        UEW = CA + SEQ + CA + DEC
        UE = at("ua_ext", [P, 2, UEW], F32, B0)
        CAW = UEW - CA
        CAV = at("conv_acc", [P, 2, CAW], F32, B0 + 9216)
        QKV = [slot(f"q_raw{j}", 12 + j) for j in range(4)] + [slot(f"k_raw{j}", 8 + j) for j in range(4)] \
            + [slot(f"v_raw{j}", 7 - j) for j in range(4)]
        BCC, BCM, BCV = slot("bc_c", 6), slot("bc_mean", 4), slot("bc_var", 0)
        SGM = [slot("sig0", 2), slot("sig1", 3)]

        AT = []
        for r in range(2):
            o = A0 + 8 * r * TB
            AT.append(BandOperands(
                Q=[at(f"q_hi{r}", [P, T], F32R, o), at(f"q_lo{r}", [P, T], F32R, o + TB)],
                K=[at(f"k_hi{r}", [P, T], F32R, o + 2 * TB), at(f"k_lo{r}", [P, T], F32R, o + 3 * TB)],
                V=[at(f"v_hi{r}", [P, 9, P], F32R, o + 4 * TB), at(f"v_lo{r}", [P, 9, P], F32R, o + 4 * TB + 4608)],
                KC=[at(f"kc_hi{r}", [P, 512], F32R, o + 4 * TB + 9216),
                    at(f"kc_lo{r}", [P, 512], F32R, o + 4 * TB + 11264)],
                VC=[at(f"vc_hi{r}", [P, 4, P], F32R, o + 4 * TB + 13312),
                    at(f"vc_lo{r}", [P, 4, P], F32R, o + 4 * TB + 15360)]))
        SS = [at(f"scores{r}", [P, 2, 640], F32, B0 + 5120 * r) for r in range(2)]
        BIAS = [at("bias0", [P, 2, 640], F32, B0 + 10240), at("bias1", [P, 2, 640], F32, W0 + 18432)]
        PT = [[at(f"pt_{n}{r}", [P, 4, 256], F32R, W0 + 4096 * (2 * r + x)) for x, n in enumerate(("hi", "lo"))]
              for r in range(2)]
        PT5 = [[at("pt5_hi0", [P, 256], F32R, W0 + 16384), at("pt5_lo0", [P, 256], F32R, W0 + 17408)],
               [at("pt5_hi1", [P, 256], F32R, W0 + 23552), at("pt5_lo1", [P, 256], F32R, B0 + 15360)]]
        RX = at("rstd_heads", [P, 9, 2, 64], F32, R0)
        RX0 = at("rstd_heads_q0", [P, 9, 2, 64], F32, B0 + 4128)
        RKC = at("kc_raw", [P, 512], F32, R0 + 4608)
        RVC = at("vc_raw", [P, 4, P], F32, R0 + 6656)
        BX = at("bias_ext", [8, 768], F32, B0 + 5 * TB)
        ext_d = nc.dram_tensor("bias_ext_d", [8, 768], F32, kind="Internal").ap()
        rep_d = nc.dram_tensor("bias_rep_d", [P, 8 * 768], F32, kind="Internal").ap()
        y1_d = nc.dram_tensor("y1_d", [KT, P, T], F32, kind="Internal").ap()
        OS = [at(f"o_sq{i}", [P, T], F32, A0 + i * TB) for i in range(2)]
        RAW2 = at("w_raw_b", [P, 2, D], F32, A0 + 2 * TB)
        W2 = [at("w_hi_b", [P, 2, D], F32R, A0 + 2 * TB + 8192), at("w_lo_b", [P, 2, D], F32R, A0 + 2 * TB + 16384)]

        XSQ = [at(f"xq_sq{i}", [P, T], F32, B0 + (6 + i) * TB) for i in range(2)]
        CX, XR = [], []
        for h, (q0, kv0) in enumerate(((B0 + 2 * TB, B0 + 10 * TB), (A0 + 8 * TB, A0 + 12 * TB), (A0, A0 + 4 * TB))):
            CX.append(CrossOperands(
                Q=[at(f"xq_hi{h}", [P, 2 * T], F32R, q0), at(f"xq_lo{h}", [P, 2 * T], F32R, q0 + 2 * TB)],
                KV=[at(f"xkv_hi{h}", [P, 4, 512], F32R, kv0), at(f"xkv_lo{h}", [P, 4, 512], F32R, kv0 + 8192)]))
            XR.append(at(f"xkv_raw{h}", [P, 4, 512], F32, kv0 + 8192))
        CX, XR = CX + CX[1:2], XR + XR[1:2]
        XPT = [at("xpt_hi", [P, 2, 512], F32R, W0 + 8192), at("xpt_lo", [P, 2, 512], F32R, W0 + 8192 + 4096)]
        XS = at("x_scores", [P, 2, 2, NMEM], F32, W0 + 16384)
        HID = TT

        def y(i):
            return Y[:, i * T:(i + 1) * T]
        Y4, Y5 = y(4), y(5)

        PS = ctx.enter_context(nc.psum_tensor("ps", [P, 8, 512], F32))

        s = Semaphores(sem)
        w_in = [s.w_in0, s.w_in1]
        w_in_mem = [s.w_in_mem0, s.w_in_mem1]
        mem_in = [s.mem_in0, s.mem_in1]
        xkv_in = [s.xkv_in0, s.xkv_in1]

        def par_col(name, i=0):
            return PAR[:, _cols[name] + i:_cols[name] + i + 1]

        def ps_tile(par):
            return PS[:, 3 * par:3 * par + 3, 0:CH]

        def chunks(ap):
            return ap.rearrange("p (c n) -> p c n", n=CH)

        def act_split(e, sl, par, tile_needed):
            e.wait_ge(w_in[par], sl * 8 + (16 - 8 * par - 8 * S_IN // 2))
            e.wait_ge(s.tile_done, tile_needed)
            e.activation(WH[:, par], RAW[:, par], ACT.Copy).then_inc(s.w_hi, 1)

        def dve_split(e, sl, par):
            e.wait_ge(s.w_hi, sl + 1)
            e.tensor_tensor(WL[:, par], RAW[:, par], WH[:, par].bitcast(F32), ALU.subtract).then_inc(s.w_lo, 1)

        def act_split_mem(e, i, q):
            e.wait_ge((w_in if q < 2 else w_in_mem)[q % 2], i * 16 + 16)
            e.wait_ge(s.tile_done, i * 4 + (q - 1))
            e.activation(WH[:, q % 2], (RAW if q < 2 else RAWM)[:, q % 2], ACT.Copy).then_inc(s.w_hi, 1)

        def dve_split_mem(e, i, q):
            e.wait_ge(s.w_hi, i * 4 + (q + 1))
            e.tensor_tensor(WL[:, q % 2], (RAW if q < 2 else RAWM)[:, q % 2], WH[:, q % 2].bitcast(F32), ALU.subtract)\
                .then_inc(s.w_lo, 1)

        def act_split2(e, sl, par):
            e.wait_ge(w_in[par], 8 * (sl - par) + 16 - 8 * S_IN // 2)
            e.activation(W2[0][:, par], RAW2[:, par], ACT.Copy).then_inc(s.w_hi, 1)

        def dve_split2(e, sl, par):
            e.wait_ge(s.w_hi, sl + 1)
            e.tensor_tensor(W2[1][:, par], RAW2[:, par], W2[0][:, par].bitcast(F32), ALU.subtract).then_inc(s.w_lo, 1)

        def cache_lo(e, j):
            r = AT[j % 2]
            for n, (dst, src) in enumerate(((r.KC, RKC[:, :]), (r.VC, RVC[:, :, :]))):
                e.wait_ge(s.kc_hi, 2 * j + n + 1)
                full = (slice(None),) * len(dst[0].shape)
                e.tensor_tensor(dst[1][full], src, dst[0][full].bitcast(F32), ALU.subtract).then_inc(s.kc_lo, 1)

        def qk_lo(e, j, n):
            dst, src = ((AT[j % 2].Q, QKV[j]), (AT[j % 2].K, QKV[4 + j]))[n]
            e.wait_ge(s.qk2_hi, 2 * j + n + 1)
            e.tensor_tensor(dst[1][:, :], src[:, :], dst[0][:, :].bitcast(F32), ALU.subtract).then_inc(s.qk2_lo, 1)

        def x_lo_part(e, h, part):
            if part < 2:
                sl = slice(part * T, (part + 1) * T)
                e.wait_ge(s.xq_hi, 2 * h + part + 1)
                e.tensor_tensor(CX[h].Q[1][:, sl], y(2 * h + part), CX[h].Q[0][:, sl].bitcast(F32), ALU.subtract)\
                    .then_inc(s.xq_lo, 1)
            else:
                a = 2 * (part - 2)
                e.wait_ge(s.xkv_hi, 2 * h + part - 1)
                e.tensor_tensor(CX[h].KV[1][:, a:a + 2], XR[h][:, a:a + 2], CX[h].KV[0][:, a:a + 2].bitcast(F32),
                                ALU.subtract).then_inc(s.xkv_lo, 1)

        def pe_part(e, par, wpar, X, ks, W=None, k0=0, woff=0, first=True, last=True, kwait=None):
            wh, wl = W or (WH, WL)
            for n, k in enumerate(ks):
                if kwait is not None:
                    kwait(k)
                w = slice(woff + k * P, woff + (k + 1) * P)
                for m, (wt, xt) in enumerate(((wh, X[0]), (wh, X[1]), (wl, X[0]))):
                    for c in range(NCH):
                        col = (k0 + k) * T + c * CH
                        ins = e.matmul(PS[:, 3 * par + c, 0:CH], wt[:, wpar, w], xt[:, col:col + CH],
                                       start=(first and n == 0 and m == 0), stop=(last and n == len(ks) - 1 and m == 2))
            if last:
                ins.then_inc(s.tile_done, 1)

        def pe_tile(e, par, wpar, X, nk=KT, **more):
            pe_part(e, par, wpar, X, range(nk), **more)

        class Count:
            def __init__(self):
                self.stat = 0
                self.rc = 0
                self.bc = 0
                self.other = 0

            def used(self, n):
                return n - self.other

        def pe_stat(e, cnt, pairs, rhs, bc_seen):
            if cnt.stat:
                e.wait_ge(s.stat_read, cnt.stat)
            if bc_seen:
                e.wait_ge(s.bc_used, bc_seen)
            for b, t0 in enumerate(BLK):
                for n, src in enumerate(pairs):
                    ins = e.matmul(PS[:, 6, 2 * b:2 * b + 2], src[:, t0:t0 + P], rhs[:, :],
                                   start=(n == 0), stop=(n == len(pairs) - 1))
            ins.then_inc(s.stat_done, 1)
            cnt.stat += 1

        def pe_bcast(e, cnt, src, first_wait=None, chunks=(0, 1, 2)):
            def used(n):
                e.wait_ge(s.bc_used, cnt.used(n))
            if first_wait is not None:
                first_wait()
            for c in chunks:
                lo, hi, blocks = BC[c]
                n = cnt.bc
                if c == 0:
                    used(n)
                if c == 1:
                    e.wait_ge(s.stat_read, cnt.stat)
                if c == 2:
                    used(n - 1)
                bank = 6 if c == 1 else 7
                for b in blocks:
                    ins = e.transpose(PS[:, bank, BLK[b] - lo:BLK[b] - lo + P], src(b), ID[:, :])
                ins.then_inc(s.bc_done, 1)
                cnt.bc += 1

        def act_bcast(e, cnt, dst):
            for c, (lo, hi, blocks) in enumerate(BC):
                bank = 6 if c == 1 else 7
                e.wait_ge(s.bc_done, cnt.bc + 1)
                e.activation(dst[:, lo:hi], PS[:, bank, 0:hi - lo], ACT.Copy).then_inc(s.bc_used, 1)
                cnt.bc += 1

        def act_root(e, cnt, dim):
            e.wait_ge(s.stat_done, cnt.stat + 1)
            if cnt.rc:
                e.wait_ge(s.rc_done, cnt.rc)
            e.activation(CRT[:, :], PS[:, 6, 0:18:2], ACT.Sqrt, bias=EPSC[:, :], scale=1.0 / dim)\
                .then_inc(s.stat_read, 1)
            cnt.stat += 1
            cnt.rc += 1

        def dve_recip(e, cnt):
            e.wait_ge(s.stat_read, cnt.stat + 1)
            if cnt.bc:
                e.wait_ge(s.bc_done, cnt.bc)
            e.reciprocal(CRC[:, :], CRT[:, :]).then_inc(s.rc_done, 1)
            cnt.stat += 1
            cnt.rc += 1

        N_U = 36

        def keys(n):
            b = n % 9
            tiles = min(b + 1, 5)
            cols = 576 if b == 8 else 128 * tiles
            return tiles, cols, 640 - cols

        def pieces(n):
            return (keys(n)[0] + 1) // 2
        CUM = [0]
        for n in range(N_U):
            CUM.append(CUM[-1] + pieces(n))

        def piece(n, p):
            tiles = keys(n)[0]
            w = 256 * min(2, tiles - 2 * p)
            return (64 if n % 9 == 8 and p == 2 else P), w

        def pt_piece(x, n, p):
            rows, w = piece(n, p)
            if p == 2:
                return PT5[n % 2][x][0:rows, 0:w]
            return PT[n % 2][x][:, :, :].rearrange("p a b -> p (a b)")[0:rows, 512 * p:512 * p + w]

        CHUNKS = {1: (0, 1), 2: (2,), 3: (3, 4), 4: (5,), 5: (6, 7), 6: (8,)}

        N_XU, N_XQ = 20, 12

        def xblocks(u):
            return 1 if u % 5 == 4 else 2

        def xexps(u):
            return 9 * (u // 5) + 2 * (u % 5)

        def xgroup(u):
            return 3 * (u // 5) + (u % 5) // 2, u % 5 in (1, 3, 4)

        X_SPLIT = {0: ((1, 0), (1, 1)), 1: ((1, 2),), 2: ((1, 3),), 3: ((2, 0),), 4: ((2, 1),), 5: ((2, 2),), 6: ((2, 3),),
                   10: ((3, 0), (3, 1)), 11: ((3, 2),), 12: ((3, 3),)}

        def su(g):
            return g * 8 + (S_UP + 4)

        def sd(g):
            return g * 8 + (S_UP + (8 if not isinstance(g, int) or g < N_G - 1 else 4))

        def tu(g):
            return g * 12 + (S_UP + 4)

        def td(g):
            return g * 12 + (S_UP + (8 if not isinstance(g, int) or g < N_G - 1 else 4))

        K_AC, K_O = (6, 7, 0, 1), (2, 3, 4, 5)

        block = ctx.enter_context(nc.Block())

        N_STAT_X = 17

        @block.sync
        def _(sp):
            sp.dma_start(PAR[:, :], params).then_inc(s.params_in, 16)
            for par in range(2):
                sp.dma_start(MR[:, 4 * par:4 * par + 4], memT[4 * par:4 * par + 4].rearrange("k p n -> p k n"))\
                    .then_inc(mem_in[par], 16)
                sp.dma_start(RAW[:, par], slabs[par]).then_inc(w_in[par], 16)
            for par in range(2):
                sp.dma_start(RAWM[:, par], slabs[2 + par]).then_inc(w_in_mem[par], 16)
            with sp.Fori(1, S_IN // 4) as i:
                for q in range(4):
                    sp.wait_ge(s.w_lo, i * 4 + q - 3)
                    sp.dma_start((RAW if q < 2 else RAWM)[:, q % 2],
                                 slabs[bass.ds(i * 4 + q, 1)].rearrange("o p c -> p (o c)"))\
                        .then_inc((w_in if q < 2 else w_in_mem)[q % 2], 16)
            for par in range(2):
                sp.wait_ge(s.w_lo, S_IN + par - 3)
                sp.dma_start(RAW[:, par], slabs[S_IN + par]).then_inc(w_in[par], 16)

            def load(i, buf):
                for par in range(2):
                    sp.wait_ge(s.w_lo, i * 2 + par - 1)
                    sp.dma_start(buf[:, par], slabs[bass.ds(i * 2 + par, 1)].rearrange("o p c -> p (o c)"))\
                        .then_inc(w_in[par], 16)

            with sp.Fori(S_IN // 2 + 1, S_OUT // 2) as i:
                load(i, RAW)
            sp.wait_ge(s.pv_done, 27)
            load(S_OUT // 2, RAW2)
            sp.wait_ge(s.pv_done, N_U)
            load(S_OUT // 2 + 1, RAW)

            def load_kv(h):
                for n, src in enumerate((o_mk[2 * h:2 * h + 2].rearrange("k p n -> p k n"),
                                         o_mv[:, :, h * 256:(h + 1) * 256].rearrange("a p n -> p a n"),
                                         mkcT[2 * h:2 * h + 2].rearrange("k p n -> p k n"),
                                         mvc[:, :, h * 256:(h + 1) * 256].rearrange("a p n -> p a n"))):
                    sp.dma_start(XR[h][:, n].rearrange("p (k n) -> p k n", k=2), src).then_inc(xkv_in[h % 2], 16)

            with sp.Fori(S_OUT // 2 + 2, S_XQ // 2 + 1) as i:
                load(i, RAW)
            sp.wait_ge(s.mem_stored, 32)
            sp.wait_ge(s.tile_done, S_XQ)
            load_kv(0)
            with sp.Fori(S_XQ // 2 + 1, S_XO // 2) as i:
                load(i, RAW)
            sp.wait_ge(s.tile_done, S_XO)
            load_kv(1)
            sp.wait_ge(s.xkv_hi, 2)
            load_kv(2)
            sp.wait_ge(s.xkv_hi, 4)
            sp.wait_ge(s.x_pv, 6)
            load_kv(3)
            sp.wait_ge(s.x_pv, 9)
            load(S_XO // 2, RAW2)
            with sp.Fori(S_XO // 2 + 1, N_SLABS // 2) as i:
                load(i, RAW)

        @block.gpsimd
        def _(g):
            for k in range(KT):
                if k:
                    g.wait_ge(s.x_in, 16 * k)
                g.dma_start(y(k), xT[k]).then_inc(s.x_in, 16)
                if k == 0:
                    g.memset(ID[:, :], 0.0).then_inc(s.zero_ready, 1)
                    g.wait_ge(s.zero_ready, 1)
                    g.affine_select(out=ID[:, :], in_=ID[:, :], compare_op=ALU.not_equal, fill=1.0, base=0,
                                    pattern=[[-1, P]], channel_multiplier=1).then_inc(s.const_ready, 1)
                    g.memset(SEL[:, :], 0.0).then_inc(s.zero_ready, 1)
                    g.wait_ge(s.zero_ready, 2)
                    for n, (ap, value) in enumerate((
                            (ONE[:, :], 1.0), (SEL[0:64, 0:1], 1.0),
                            (SEL[64:128, 1:2], 1.0), (EPSC[:, :], EPS), (ACC[:, :], 0.0))):
                        g.wait_ge(s.const_ready, n + 1)
                        g.memset(ap, value).then_inc(s.const_ready, 1)
            g.wait_ge(s.mk_norm, 8)
            g.dma_start(o_mk.rearrange("k p n -> p k n"), KV[:, 0:8]).then_inc(s.mem_stored, 16)
            g.wait_ge(s.mv_cp, 4)
            g.dma_start(o_mv.rearrange("a p n -> p a n"), VMN[:, :, :]).then_inc(s.mem_stored, 16)
            g.wait_ge(s.stat_done, 3)
            g.dma_start(UE[:, :, CA + SEQ:2 * CA + SEQ], ctxa.rearrange("i p n -> p i n")).then_inc(s.ctx_in, 16)
            for i in range(2):
                g.wait_ge(s.sq_done, 8)
                g.wait_ge(s.a_lo, 8)
                g.dma_start(y(i)[:, CC + SEQ:2 * CC + SEQ], ctxc[i]).then_inc(s.ctx_in, 16)
            g.dma_start(BX[:, 511:768], rbrev).then_inc(s.bx_in, 16)
            g.wait_ge(s.bx_in, 16)
            g.tensor_copy(BX[:, 0:511], BX[:, 511:512].to_broadcast([8, 511])).then_inc(s.bx_done, 1)
            g.wait_ge(s.bx_done, 1)
            g.tensor_scalar(BX[:, :], BX[:, :], -1.0, 0.0, ALU.mult, ALU.add).then_inc(s.bx_done, 1)
            g.wait_ge(s.bx_done, 2)
            g.dma_start(ext_d, BX[:, :]).then_inc(s.ext_out, 16)
            g.wait_ge(s.ext_out, 16)
            g.dma_start(rep_d, bass.AP(ext_d.tensor, 0, [[0, P], [1, 8 * 768]])).then_inc(s.rep_out, 16)
            g.dma_start(o_kc, kcT[:, :, 64:512]).then_inc(s.cache_out, 16)
            g.dma_start(o_vc, vc.rearrange("a p n -> (a p) n")[64:512, :]).then_inc(s.cache_out, 16)
            g.wait_ge(s.ue_done, 4)
            g.wait_ge(s.ctx_in, 48)
            g.dma_start(o_ca[0].rearrange("i p n -> p i n"), UE[:, :, SEQ:SEQ + CA]).then_inc(s.state_out, 16)
            g.dma_start(o_ca[1].rearrange("i p n -> p i n"), UE[:, :, UEW - CA:UEW]).then_inc(s.state_out, 16)
            for i in range(2):
                g.wait_ge(s.uc_done, 2 * i + 2)
                g.dma_start(o_cc[0, i], y(i)[:, SEQ:SEQ + CC]).then_inc(s.state_out, 16)
                g.dma_start(o_cc[1, i], y(i)[:, T - CC:T]).then_inc(s.state_out, 16)
            def load_bias(j):
                if j >= 2:
                    g.wait_ge(s.ttr_done, 18 * (j - 1))
                else:
                    g.wait_ge(s.ya_done, 2)
                    g.wait_ge(s.w_lo, S_OUT)
                    g.wait_ge(s.tile_done, S_OUT)
                if j >= 1:
                    g.wait_ge(s.bias_in, 16 * j)
                g.dma_start(BIAS[j % 2][:, :, :], bass.AP(rep_d.tensor, 2 * j * 768 + 127,
                                                          [[8 * 768 - 1, P], [768, 2], [1, 640]])).then_inc(s.bias_in, 16)
                g.wait_ge(s.bias_in, 16 * (j + 1))
                if j >= 2:
                    g.wait_ge(s.qk2_lo, 2 * j)
                g.memset(BIAS[j % 2][0:64, :, 576:640], BIG).then_inc(s.bias_ready, 1)
                g.wait_ge(s.bias_ready, 2 * j + 1)
                g.memset(BIAS[j % 2][64:128, :, 0:64], BIG).then_inc(s.bias_ready, 1)

            def load_cache(j):
                if j == 0:
                    g.wait_ge(s.stat_done, 14)
                else:
                    g.wait_ge(s.kc_lo, 2 * j)
                g.dma_start(RKC[:, :], kcT[j]).then_inc(s.cache_in, 16)
                g.dma_start(RVC[:, :, :], vc[:, :, j * P:(j + 1) * P].rearrange("a p n -> p a n")).then_inc(s.cache_in, 16)

            g.wait_ge(s.tile_read, S_IN + 22)
            for j in range(4):
                g.dma_start(o_v[j], QKV[8 + j][:, 512:TOK]).then_inc(s.kv_out, 16)
            g.wait_ge(s.rep_out, 16)
            for j in range(4):
                load_cache(j)
                load_bias(j)
                if j:
                    g.wait_ge(s.bias_ready, 2 * j + 2)
                    cache_lo(g, j)
                    g.wait_ge(s.kc_lo, 2 * j + 2)
                    g.wait_ge(s.qk2_lo, 2 * j)
                    qk_lo(g, j, 0)
                g.wait_ge(s.k_nrm, 3 * j + 3)
                g.dma_start(o_k[j], QKV[4 + j][:, 512:TOK]).then_inc(s.kv_out, 16)
                if j:
                    qk_lo(g, j, 1)
            g.wait_ge(s.b_lo, 8)
            for k in range(KT):
                if k:
                    g.wait_ge(s.x2_in, 16 * k)
                g.dma_start(y(k), xT[k]).then_inc(s.x2_in, 16)
            for k in range(KT):
                g.wait_ge(s.tile_read, S_OUT + k + 1)
                if k:
                    g.wait_ge(s.y1_out, 16 * k)
                g.dma_start(y1_d[k], y(k)).then_inc(s.y1_out, 16)
            g.wait_ge(s.xkv_lo, 2)
            g.wait_ge(s.xq_lo, 2)
            for u in sorted(X_SPLIT):
                for h, part in X_SPLIT[u]:
                    x_lo_part(g, h, part)
            g.wait_ge(s.xq_lo, 8)
            g.wait_ge(s.y1_out, 128)
            for k in range(KT):
                if k:
                    g.wait_ge(s.y1_in, 16 * k)
                g.dma_start(y(k), y1_d[k]).then_inc(s.y1_in, 16)
            for m in range(KT):
                g.wait_ge(s.tile_read, td(N_G - 1) + m + 1)
                g.dma_start(o_y[m], y(m)).then_inc(s.stored, 16)
            g.wait_ge(s.stored, 128)
            for q, v in ((s.state_out, 96), (s.mem_stored, 32), (s.cache_out, 32), (s.kv_out, 128)):
                g.wait_ge(q, v)

        @block.scalar
        def _(e):
            cnt = Count()
            e.wait_ge(s.params_in, 16)
            for half in range(2):
                e.wait_ge(mem_in[half], 16)
                for k in range(4 * half, 4 * half + 4):
                    e.activation(MX[0][:, k * NMEM:(k + 1) * NMEM], MR[:, k], ACT.Copy,
                                 scale=par_col("norm_mem", k)).then_inc(s.mem_hi, 1)
                e.wait_ge(w_in[half], 16)
                e.activation(WH[:, half], RAW[:, half], ACT.Copy).then_inc(s.w_hi, 1)
            e.activation(MSQ[:, :, :], MR[:, :, :], ACT.Square).then_inc(s.mem_sq, 1)

            def x_hi(k):
                e.wait_ge(s.x_in, k * 16 + 16)
                e.wait_ge(s.params_in, 16)
                e.activation(A[0][:, bass.ds(k * T, T)], Y[:, bass.ds(k * T, T)], ACT.Copy,
                             scale=PAR[:, bass.ds(k + _cols["norm_mix"], 1)]).then_inc(s.a_hi, 1)

            act_split_mem(e, 0, 2)
            e.wait_ge(s.stat_done, 1)
            e.wait_ge(s.const_ready, 6)
            e.activation(CKR[:, 0:2], PS[:, 6, 0:4:2], ACT.Sqrt, bias=EPSC[:, :], scale=1.0 / D)\
                .then_inc(s.stat_read, 1)
            cnt.stat += 1
            e.wait_ge(s.bc_done, 1)
            e.activation(RM[:, :], PS[:, 7, 0:NMEM], ACT.Copy).then_inc(s.bc_used, 1)
            cnt.bc += 1
            x_hi(0)
            act_split_mem(e, 0, 3)
            e.activation(TT[:, :], y(0), ACT.Square).then_inc(s.sq_done, 1)

            def mem_pair(i, ii, q):
                act_split_mem(e, ii, q)
                x_hi(i)
                e.wait_ge(s.acc_done, i)
                act_split_mem(e, ii, q + 1)
                e.activation(TT[:, :], Y[:, bass.ds(i * T, T)], ACT.Square).then_inc(s.sq_done, 1)

            mem_pair(1, 1, 0)
            with e.Fori(1, 4) as ii:
                mem_pair(ii * 2, ii, 2)
                mem_pair(ii * 2 + 1, ii + 1, 0)
            e.wait_ge(s.tile_read, 8)
            e.activation(MSQ[:, :, :], KV[:, 0:8], ACT.Square).then_inc(s.kq_sq, 1)

            def win_split(i):
                if i < 20:
                    act_split(e, S_IN + i + 2, i % 2, S_IN + i + 1)

            act_root(e, cnt, D)
            act_bcast(e, cnt, RSTD)
            win_split(0)
            e.wait_ge(s.stat_done, cnt.stat + 1)
            e.activation(CKR[:, :], PS[:, 6, 0:16:2], ACT.Sqrt, bias=EPSC[:, :], scale=1.0 / 256)\
                .then_inc(s.stat_read, 1)
            cnt.stat += 1
            win_split(1)

            def sigmoid(i):
                e.wait_ge(s.tile_read, S_IN + 2 + 2 * i)
                e.activation(y(3), y(3), ACT.Sigmoid).then_inc(s.sig_done, 1)

            sigmoid(0)
            for n in range(4):
                e.wait_ge(s.mv_tr, n + 1)
                e.activation(VMN[:, n // 2, (n % 2) * 512:(n % 2) * 512 + 512], PS[:, 6 + n % 2, :], ACT.Copy)\
                    .then_inc(s.mv_cp, 1)
            win_split(2)
            win_split(3)
            sigmoid(1)
            def group_sq(tiles, ready, cnt_ready):
                e.wait_ge(ready, cnt_ready)
                e.wait_ge(s.stat_done, cnt.stat)
                e.activation(TT[:, :], tiles[0], ACT.Square).then_inc(s.g_sq, 1)
                e.activation(Y4, tiles[1], ACT.Square).then_inc(s.g_sq, 1)

            def rstd_heads(j, which):
                if j == 0 and which == 0:
                    e.wait_ge(s.cq_rc, 1)
                    e.wait_ge(s.xa_nrm, 2)
                elif j == 0:
                    e.wait_ge(s.stat_done, 14)
                    e.wait_ge(s.tile_read, S_OUT)
                else:
                    e.wait_ge(s.bc_done, N_ACT_BC + 9 * j + 3 * which)
                e.activation((RX0 if j == which == 0 else RX)[:, :, :, :],
                             CQC[:, j + 4 * which].unsqueeze(3).to_broadcast([P, 9, 2, 64]), ACT.Copy)\
                    .then_inc(s.rx_ready, 1)

            for i in range(4, 22):
                win_split(i)
                if i == 10:
                    group_sq((y(6), y(7)), s.yc_done, 4)
                if i == 11:
                    act_root(e, cnt, 256)
                if i == 12:
                    act_bcast(e, cnt, BCC)
                if 11 <= i <= 18:
                    j = i - 11
                    e.wait_ge(s.tile_read, S_IN + 10 + j + 1)
                    e.wait_ge(s.stat_done, cnt.stat)
                    e.activation(TT[:, :], QKV[j][:, :], ACT.Square).then_inc(s.qk_sq, 1)
                    e.wait_ge(s.stat_done, cnt.stat + 1)
                    e.activation(CQR[:, j].rearrange("p b e -> p (b e)"), PS[:, 6, 0:18], ACT.Sqrt,
                                 bias=EPSC[:, :], scale=1.0 / 64).then_inc(s.stat_read, 1)
                    cnt.stat += 1
                if i == 19:
                    e.wait_ge(s.stat_done, cnt.stat + 1)
                    e.activation(CRT[:, :], PS[:, 6, 0:18:2], ACT.Copy, scale=1.0 / 256).then_inc(s.stat_read, 1)
                    cnt.stat += 1
                    act_bcast(e, cnt, BCM)
                    group_sq((y(0), y(1)), s.xa_sub, 2)
                if i == 20:
                    act_root(e, cnt, 256)
                    act_bcast(e, cnt, BCV)
                    for h in range(2):
                        e.wait_ge(s.xa_nrm, h + 1)
                        e.activation(SGM[h][:, :], y(h), ACT.Sigmoid, bias=par_col("ln_a_b", h)).then_inc(s.ya_sig, 1)
                    group_sq((y(0), y(1)), s.ya_done, 2)
                if i == 21:
                    rstd_heads(0, 0)
                    act_root(e, cnt, 256)

            def cache_hi(j):
                r = AT[j % 2]
                e.wait_ge(s.cache_in, 32 * (j + 1))
                if j >= 2:
                    e.wait_ge(s.pv_done, 9 * (j - 1))
                e.activation(r.KC[0][:, :], RKC[:, :], ACT.Copy).then_inc(s.kc_hi, 1)
                e.activation(r.VC[0][:, :, :], RVC[:, :, :], ACT.Copy).then_inc(s.kc_hi, 1)

            def q_hi(j):
                e.wait_ge(s.q_nrm, 3 * j + 3)
                e.activation(AT[j % 2].Q[0][:, :], QKV[j][:, :], ACT.Copy).then_inc(s.qk2_hi, 1)

            def k_hi(j):
                e.wait_ge(s.k_nrm, 3 * j + 3)
                e.activation(AT[j % 2].K[0][:, :], QKV[4 + j][:, :], ACT.Copy).then_inc(s.qk2_hi, 1)

            def v_hi(j, c):
                r = AT[j % 2]
                e.wait_ge(s.bc_done, N_ACT_BC + 9 * j + 7 + c)
                bank = 6 if c == 1 else 7
                nb = 3 if c < 2 else 2
                e.activation(r.V[0][:, 3 * c:3 * c + nb], PS[:, bank, 0:nb * P].rearrange("p (b n) -> p b n", n=P),
                             ACT.Copy).then_inc(s.v_hi, 1)
                if c == 2:
                    e.activation(r.V[0][0:64, 8], PS[0:64, bank, 256:384], ACT.Copy).then_inc(s.v_hi, 1)

            def prepare(j, i):
                if i == 0:
                    rstd_heads(j, 0)
                if i == 2 and j:
                    cache_hi(j)
                if i == 3:
                    if j:
                        rstd_heads(j, 1)
                    q_hi(j)
                if i == 5:
                    k_hi(j)
                for x in CHUNKS.get(i, ()):
                    if x >= 6:
                        v_hi(j, x - 6)

            def exps(n):
                _, cols, _ = keys(n)
                for h in range(2):
                    e.wait_ge(s.ttr_done, 2 * n + h + 1)
                    if n >= 2:
                        e.wait_ge(s.rec_done, n - 1)
                    m = 2 * (n % 2) + h
                    e.activation(SS[n % 2][:, h, 0:cols], SS[n % 2][:, h, 0:cols], ACT.Exp, bias=MIN[:, m:m + 1],
                                 scale=-1.0, accum_out=SUM[:, m:m + 1]).then_inc(s.exp_done, 1)

            def o_out(n):
                j, b = divmod(n, 9)
                e.wait_ge(s.pv_done, n + 1)
                for h in range(2):
                    rows = slice(64 * h, 64 * h + 64)
                    q0, c0_, w = (P * b, h * P, P) if b < 8 else (SEQ, h * P + 64, 64)
                    e.activation(y(2 + j)[rows, q0:q0 + w], PS[rows, 7, c0_:c0_ + w], ACT.Copy).then_inc(s.o_used, 1)

            def pt_hi(n):
                for p in range(pieces(n)):
                    rows, w = piece(n, p)
                    e.wait_ge(s.t_done, CUM[n] + p + 1)
                    if n >= 2:
                        e.wait_ge(s.pv_done, n - 1)
                        e.wait_ge(s.pt_lo, CUM[n - 1])
                    e.activation(pt_piece(0, n, p), PS[0:rows, 4 + p, 0:w], ACT.Copy).then_inc(s.pt_hi, 1)

            def o_square(i):
                e.wait_ge(s.pad_ready, 9)
                e.wait_ge(s.o_used, 18 * (i + 1))
                if i >= 2:
                    e.wait_ge(s.o_sum, i - 1)
                e.activation(OS[min(i, 1)][:, :], y(2 + i), ACT.Square).then_inc(s.o_sq, 1)

            def b_hi(k):
                e.wait_ge(s.kv_out, 128)
                e.wait_ge(s.v_lo, 16)
                if k >= 6:
                    e.wait_ge(s.gn_done, 2)
                elif k < 2:
                    e.wait_ge(s.bc_used, N_ACT_BC + 3)
                e.activation(B[0][:, k * T:(k + 1) * T], y(k), ACT.Copy).then_inc(s.b_hi, 1)

            N_ACT_BC = cnt.bc
            cnt.bc += 39
            rstd_heads(0, 1)
            for i in range(1, 7):
                prepare(0, i)
            exps(0)
            for n in range(N_U):
                pt_hi(n)
                if n + 1 < N_U:
                    exps(n + 1)
                if n:
                    o_out(n - 1)
                if n == 0:
                    cache_hi(0)
                if n < 27:
                    prepare(n // 9 + 1, n % 9)
                if n == 28:
                    o_square(0)
                    o_square(1)
                if n == 29:
                    b_hi(6)
                if n == 30:
                    b_hi(7)
                if n == 31:
                    o_square(2)
                if n in (32, 33):
                    act_split2(e, S_OUT + n - 32, n - 32)
            for k in (0, 1):
                e.wait_ge(s.t_done, CUM[N_U])
                b_hi(k)
            o_out(N_U - 1)
            o_square(3)
            cnt.other = 36
            act_root(e, cnt, 512)
            act_bcast(e, cnt, RSTD)
            for i in range(4):
                e.wait_ge(s.o_nrm, i + 1)
                b_hi(2 + i)
            e.wait_ge(s.pv_done, N_U)
            for par in range(2):
                act_split(e, S_OUT + 2 + par, par, S_OUT)

            def residual(t0, i, par, norm, acc0):
                m = i * 2 + par
                e.wait_ge(s.tile_read, m + (t0 + 1))
                e.wait_ge(s.acc_done, m + acc0)
                if not isinstance(i, int):
                    act_split(e, m + (t0 + 2), par, m + (t0 + 1))
                e.activation(A[0][:, bass.ds(m * T, T)], Y[:, bass.ds(m * T, T)], ACT.Copy,
                             scale=PAR[:, bass.ds(m + _cols[norm], 1)]).then_inc(s.a_hi, 1)
                e.activation(TT[:, :], Y[:, bass.ds(m * T, T)], ACT.Square).then_inc(s.sq_done, 1)

            for par in range(2):
                residual(S_OUT, 0, par, "norm_x", 8)
            with e.Fori(1, 4) as i:
                for par in range(2):
                    residual(S_OUT, i, par, "norm_x", 8)

            act_root(e, cnt, D)
            act_bcast(e, cnt, RSTD)
            N_BC_X = cnt.used(cnt.bc)

            def x_place(h):
                if h == 3:
                    e.wait_ge(s.x_pv, 6)
                else:
                    e.wait_ge(s.tile_done, S_XQ if h == 0 else S_XO)

            def x_hi_part(h, part):
                x_place(h)
                if part < 2:
                    e.wait_ge(s.bc_used, N_BC_X + 3 * h + 3)
                    e.activation(CX[h].Q[0][:, part * T:(part + 1) * T], y(2 * h + part), ACT.Copy).then_inc(s.xq_hi, 1)
                else:
                    a = 2 * (part - 2)
                    e.wait_ge(xkv_in[h % 2], 64 * (h // 2 + 1))
                    e.activation(CX[h].KV[0][:, a:a + 2], XR[h][:, a:a + 2], ACT.Copy).then_inc(s.xkv_hi, 1)

            def xexp(u):
                e.wait_ge(s.x_min, u + 1)
                if u >= 2:
                    e.wait_ge(s.x_t, u - 1)
                    e.wait_ge(s.x_rec, u - 1)
                for b in range(xblocks(u)):
                    m = 2 * (u % 2) + b
                    e.activation(XS[:, u % 2, b], PS[:, u % 2, b * NMEM:(b + 1) * NMEM], ACT.Exp, bias=MIN[:, m:m + 1],
                                 scale=-1.0, accum_out=SUM[:, m:m + 1]).then_inc(s.x_exp, 1)

            for i in range(8):
                if i < 6:
                    act_split(e, S_XQ + i + 2, i % 2, S_XQ + i + 1)
                h = i // 2
                if i == 7:
                    xexp(0)
                    xexp(1)
                if i % 2:
                    for k in range(2):
                        e.wait_ge(s.tile_read, S_XQ + 2 * h + k + 1)
                        if h:
                            e.wait_ge(s.stat_done, cnt.stat)
                        e.activation(XSQ[k][:, :], y(2 * h + k), ACT.Square).then_inc(s.xs_sq, 1)
                if i in (5, 6):
                    x_hi_part(0, 2 * i - 10)
                    x_hi_part(0, 2 * i - 9)
                if i % 2 == 0 and i:
                    act_root(e, cnt, 256)

            def xpt_hi(q):
                h, g = divmod(q, 3)
                w = 512 if g < 2 else P
                e.wait_ge(s.x_t, 5 * h + (2 * g + 2 if g < 2 else 5))
                if q:
                    e.wait_ge(s.x_pv, q)
                    e.wait_ge(s.x_ptlo, q)
                k = 2 + 2 * (q % 2)
                e.activation(XPT[0][:, :, 0:w], PS[:, k:k + 2, 0:w], ACT.Copy).then_inc(s.x_pthi, 1)

            def xo_hi(q):
                h, g = divmod(q, 3)
                e.wait_ge(s.x_pv, q + 1)
                for d in range(2):
                    lo, c, w = (512 * g, 0, 512) if g < 2 else (SEQ, 64, 64)
                    col = (2 * h + d) * T + lo
                    e.activation(B[0][:, col:col + w], PS[:, 6 + d, c:c + w], ACT.Copy).then_inc(s.x_ohi, 1)

            done = None
            for u in range(N_XU):
                q, last = xgroup(u)
                if last:
                    xpt_hi(q)
                if u + 2 < N_XU:
                    xexp(u + 2)
                if u == 1:
                    act_root(e, cnt, 256)
                if done is not None:
                    xo_hi(done)
                done = q if last else None
                for h, part in X_SPLIT.get(u, ()):
                    x_hi_part(h, part)
                if u in (17, 18):
                    act_split2(e, S_XO + u - 17, u - 17)
            xo_hi(done)
            cnt.bc += 12

            e.wait_ge(s.x_pv, N_XQ)
            for par in range(2):
                act_split(e, S_XO + 2 + par, par, S_XO)
            for par in range(2):
                residual(S_XO, 0, par, "norm_ff", 16)
            with e.Fori(1, 4) as i:
                for par in range(2):
                    residual(S_XO, i, par, "norm_ff", 16)

            def hidden(t, h0, j, slot):
                e.wait_ge(s.tile_read, t + (j + 1))
                e.activation(HID[:, :], HID[:, :], ACT.Square).then_inc(s.h_sq, 1)
                e.wait_ge(s.h_sq, h0 + (j + 1))
                e.activation(B[0][:, (slot + j) * T:(slot + j + 1) * T], HID[:, :], ACT.Copy).then_inc(s.h_hi, 1)

            def mlp_group(g, half):
                if not isinstance(g, int) or g < N_G - 1:
                    for j in range(4):
                        act_split(e, su(g) + (j + 2), j % 2, tu(g) + (j + 1))
                        hidden(tu(g), g * 4 + 4, j, 4 * (1 - half))
                for j in range(4 if not isinstance(g, int) or g < N_G - 1 else 2):
                    act_split(e, sd(g) + (j + 2), j % 2, td(g) + (2 * j + 2))

            act_root(e, cnt, D)
            act_bcast(e, cnt, RSTD)
            for j in range(4):
                act_split(e, S_UP + j + 2, j % 2, S_UP + j + 1)
                hidden(S_UP, 0, j, 0)
            with e.Fori(0, 3) as i:
                mlp_group(i * 2, 0)
                mlp_group(i * 2 + 1, 1)
            mlp_group(6, 0)
            mlp_group(7, 1)

        @block.vector
        def _(e):
            cnt = Count()
            e.wait_ge(s.params_in, 16)
            for half in range(2):
                for k in range(4 * half, 4 * half + 4):
                    e.wait_ge(s.mem_hi, k + 1)
                    sl = slice(k * NMEM, (k + 1) * NMEM)
                    e.scalar_tensor_tensor(MX[1][:, sl], MR[:, k], par_col("norm_mem", k), MX[0][:, sl].bitcast(F32),
                                           ALU.mult, ALU.subtract).then_inc(s.mem_lo, 1)
                dve_split(e, half, half)
            e.wait_ge(s.mem_sq, 1)
            e.tensor_reduce(MSUM[:, :], MSQ[:, :, :].rearrange("p k n -> p n k"), AX.X, ALU.add).then_inc(s.mem_sum, 1)

            def x_lo(k):
                e.wait_ge(s.a_hi, k + 1)
                e.scalar_tensor_tensor(A[1][:, bass.ds(k * T, T)], Y[:, bass.ds(k * T, T)],
                                       PAR[:, bass.ds(k + _cols["norm_mix"], 1)],
                                       A[0][:, bass.ds(k * T, T)].bitcast(F32), ALU.mult, ALU.subtract)\
                    .then_inc(s.a_lo, 1)

            def add_sq(n):
                e.wait_ge(s.sq_done, n + 1)
                e.tensor_tensor(ACC[:, :], ACC[:, :], TT[:, :], ALU.add).then_inc(s.acc_done, 1)

            def mem_evac(t, par):
                e.wait_ge(s.tile_done, t + 1)
                e.tensor_tensor(KV[:, bass.ds(t, 1)].rearrange("p o n -> p (o n)"), PS[:, 3 * par, 0:NMEM],
                                RM[:, :], ALU.mult).then_inc(s.tile_read, 1)

            dve_split_mem(e, 0, 2)
            e.wait_ge(s.stat_read, 1)
            e.reciprocal(CKC[:, 0:2], CKR[:, 0:2]).then_inc(s.ck_rc, 1)
            cnt.stat += 1
            e.wait_ge(s.bc_used, 1)
            cnt.bc += 1
            mem_evac(0, 0)
            x_lo(0)
            dve_split_mem(e, 0, 3)
            mem_evac(1, 1)
            e.wait_ge(s.const_ready, 6)
            add_sq(0)

            def mem_pair(i, ii, q):
                dve_split_mem(e, ii, q)
                mem_evac(i * 2, 0)
                x_lo(i)
                dve_split_mem(e, ii, q + 1)
                mem_evac(i * 2 + 1, 1)
                e.wait_ge(s.acc_done, i)
                add_sq(i)

            mem_pair(1, 1, 0)
            with e.Fori(1, 4) as ii:
                mem_pair(ii * 2, ii, 2)
                mem_pair(ii * 2 + 1, ii + 1, 0)

            def win_split(i):
                if i < 20:
                    dve_split(e, S_IN + i + 2, i % 2)

            def evac(i, dst):
                e.wait_ge(s.tile_done, S_IN + i + 1)
                e.wait_ge(s.bc_used, 4)
                e.tensor_tensor(chunks(dst), ps_tile(i % 2), chunks(RSTD[:, :]), ALU.mult).then_inc(s.tile_read, 1)

            dve_recip(e, cnt)
            cnt.bc += 3
            win_split(0)
            e.wait_ge(s.sq_done, 8)
            e.wait_ge(s.a_lo, 8)
            for i in (6, 7):
                e.memset(y(i)[:, TOK:T], 0.0).then_inc(s.pad_ready, 1)
            for i in (0, 1):
                e.memset(y(i)[:, 0:CC], 0.0).then_inc(s.pad_ready, 1)
            evac(0, y(2))
            e.wait_ge(s.stat_read, cnt.stat + 1)
            e.reciprocal(CKC[:, :], CKR[:, :]).then_inc(s.ck_rc, 1)
            cnt.stat += 1
            e.memset(UE[:, :, 0:CA], 0.0).then_inc(s.pad_ready, 1)
            win_split(1)
            evac(1, y(3))
            e.wait_ge(s.tile_read, S_MEM + 8)
            for k in range(KT):
                h = k // 2
                e.wait_ge(s.mk_bc, h // 2 + 1)
                e.scalar_tensor_tensor(KV[:, k], KV[:, k], par_col("xk_norm", k % 2),
                                       PS[:, 6 + h // 2, (h % 2) * NMEM:(h % 2) * NMEM + NMEM],
                                       ALU.mult, ALU.mult).then_inc(s.mk_norm, 1)

            def glu(i):
                e.wait_ge(s.sig_done, i + 1)
                e.wait_ge(s.tile_read, S_IN + 1 + 2 * i)
                if i == 0:
                    e.wait_ge(s.stat_done, 3)
                e.tensor_tensor(UE[:, i, CA:CA + SEQ], y(2)[:, 0:SEQ], y(3)[:, 0:SEQ], ALU.mult).then_inc(s.ue_done, 1)
                e.tensor_tensor(UE[:, i, 2 * CA + SEQ:UEW], y(2)[:, SEQ:TOK], y(3)[:, SEQ:TOK], ALU.mult)\
                    .then_inc(s.ue_done, 1)

            glu(0)
            win_split(2)
            e.wait_ge(s.ue_done, 2)
            evac(2, y(2))
            win_split(3)
            evac(3, y(3))
            glu(1)

            tap = [0]

            def conv_taps(n):
                for _ in range(n):
                    j, h = divmod(tap[0], 2)
                    w = par_col("conv_a_w", 2 * j + h)
                    if tap[0] == 0:
                        e.wait_ge(s.ue_done, 4)
                        e.wait_ge(s.ctx_in, 48)
                        e.wait_ge(s.pad_ready, 5)
                    if j == 0:
                        e.tensor_scalar(CAV[:, h], UE[:, h, j:j + CAW], w, par_col("conv_a_b", h), ALU.mult, ALU.add)\
                            .then_inc(s.conv_step, 1)
                    elif j < CA:
                        e.wait_ge(s.conv_step, tap[0] - 1)
                        e.scalar_tensor_tensor(CAV[:, h], UE[:, h, j:j + CAW], w, CAV[:, h], ALU.mult, ALU.add)\
                            .then_inc(s.conv_step, 1)
                    else:
                        e.wait_ge(s.conv_step, tap[0] - 1 if h == 0 else tap[0])
                        if h == 0:
                            e.wait_ge(s.state_out, 16 * 6)
                            e.wait_ge(s.c3_done, 6)
                        for lo, n_, src in ((0, SEQ, 0), (SEQ, DEC, SEQ + CA)):
                            e.scalar_tensor_tensor(y(h)[:, lo:lo + n_], UE[:, h, j + src:j + src + n_], w,
                                                   CAV[:, h, src:src + n_], ALU.mult, ALU.add)\
                                .then_inc(s.conv_step, 1)
                    tap[0] += 1

            def conv_c(i, out):
                for j in range(3):
                    w = par_col("conv_c_w", 2 * j + i)
                    src = y(i)[:, j:j + T - CC]
                    if j == 0:
                        e.wait_ge(s.uc_done, 2 * i + 2)
                        e.wait_ge(s.ctx_in, 48)
                        e.wait_ge(s.pad_ready, 5)
                        e.tensor_scalar(out[:, 0:T - CC], src, w, None, ALU.mult).then_inc(s.c3_done, 1)
                    else:
                        e.wait_ge(s.c3_done, 3 * i + j)
                        e.scalar_tensor_tensor(out[:, 0:T - CC], src, w, out[:, 0:T - CC], ALU.mult, ALU.add)\
                            .then_inc(s.c3_done, 1)

            def group_sum(n):
                e.wait_ge(s.g_sq, 2 * n + 2)
                e.tensor_tensor(TT[:, :], TT[:, :], Y4, ALU.add).then_inc(s.g_sum, 1)

            for i in range(4, 22):
                win_split(i)
                if i == 21:
                    e.wait_ge(s.stat_read, 13)
                    e.reciprocal(CQC[:, :, :, :].rearrange("p j b e -> p (j b e)"),
                                 CQR[:, :, :, :].rearrange("p j b e -> p (j b e)")).then_inc(s.cq_rc, 1)
                    e.tensor_scalar(GQ[:, 0:1], par_col("q_norm"), -0.125, None, ALU.mult).then_inc(s.gq_ready, 1)
                    e.tensor_scalar(GQ[:, 1:3], PAR[:, _cols["xq_norm"]:_cols["xq_norm"] + 2], -0.0625, None, ALU.mult)\
                        .then_inc(s.gq_ready, 1)
                if i in (4, 7):
                    c = (i - 4) // 3
                    e.wait_ge(s.ue_done, 4)
                    evac(i, y(4) if c == 0 else y(2))
                elif i in (5, 8):
                    c = (i - 5) // 3
                    a, b = (y(4), y(5)) if c == 0 else (y(2), y(3))
                    evac(i, b)
                    e.wait_ge(s.tile_read, S_IN + i + 1)
                    e.tensor_tensor(y(c)[:, CC:CC + SEQ], a[:, 0:SEQ], b[:, 0:SEQ], ALU.mult).then_inc(s.uc_done, 1)
                    e.tensor_tensor(y(c)[:, 2 * CC + SEQ:T], a[:, SEQ:TOK], b[:, SEQ:TOK], ALU.mult)\
                        .then_inc(s.uc_done, 1)
                    conv_c(c, a)
                elif i in (6, 9):
                    c = (i - 6) // 3
                    a, b = (y(4), y(5)) if c == 0 else (y(2), y(3))
                    e.wait_ge(s.uc_done, 2 * c + 2)
                    evac(i, b)
                    e.wait_ge(s.tile_read, S_IN + i + 1)
                    e.wait_ge(s.c3_done, 3 * c + 3)
                    e.tensor_tensor(y(6 + c)[:, 0:SEQ], b[:, 0:SEQ], a[:, 0:SEQ], ALU.mult).then_inc(s.yc_done, 1)
                    e.tensor_tensor(y(6 + c)[:, SEQ:TOK], b[:, SEQ:TOK], a[:, SEQ + CC:T - CC], ALU.mult)\
                        .then_inc(s.yc_done, 1)
                else:
                    if i == 10:
                        e.wait_ge(s.mem_stored, 32)
                    evac(i, QKV[i - 10][:, :])
                if i == 10:
                    e.wait_ge(s.yc_done, 4)
                    group_sum(0)
                if i == 11:
                    dve_recip(e, cnt)
                if i == 12:
                    cnt.bc += 3
                    for c in range(2):
                        e.wait_ge(s.bc_used, cnt.bc)
                        e.scalar_tensor_tensor(y(6 + c), y(6 + c), par_col("out_norm", 6 + c), BCC[:, :],
                                               ALU.mult, ALU.mult).then_inc(s.gn_done, 1)
                if 11 <= i <= 18:
                    cnt.stat += 1
                conv_taps(TAPS.get(i, 0))
                if i == 19:
                    cnt.stat += 1
                    cnt.bc += 3
                    for h in range(2):
                        e.wait_ge(s.bc_used, cnt.bc)
                        e.tensor_tensor(y(h), y(h), BCM[:, :], ALU.subtract).then_inc(s.xa_sub, 1)
                    group_sum(1)
                if i == 20:
                    dve_recip(e, cnt)
                    cnt.bc += 3
                    for h in range(2):
                        e.wait_ge(s.bc_used, cnt.bc)
                        e.wait_ge(s.xa_sub, 2)
                        e.scalar_tensor_tensor(y(h), y(h), par_col("ln_a_g", h), BCV[:, :], ALU.mult, ALU.mult)\
                            .then_inc(s.xa_nrm, 1)
                    for h in range(2):
                        e.wait_ge(s.ya_sig, h + 1)
                        e.scalar_tensor_tensor(y(h), y(h), par_col("ln_a_b", h), SGM[h][:, :], ALU.add, ALU.mult)\
                            .then_inc(s.ya_done, 1)
                    group_sum(2)
                if i == 21:
                    dve_recip(e, cnt)

            def heads_nrm(dst, gain, done, c):
                lo, hi, _ = BC[c]
                e.wait_ge(s.bc_done, cnt.bc + 1)
                e.scalar_tensor_tensor(dst[:, lo:hi], dst[:, lo:hi], gain, PS[:, 6 if c == 1 else 7, 0:hi - lo],
                                       ALU.mult, ALU.mult).then_inc(done, 1)

            def v_lo(j, c):
                r = AT[j % 2]
                bank = 6 if c == 1 else 7
                nb = 3 if c < 2 else 2
                e.wait_ge(s.v_hi, 4 * j + c + (2 if c == 2 else 1))
                e.tensor_tensor(r.V[1][:, 3 * c:3 * c + nb], PS[:, bank, 0:nb * P].rearrange("p (b n) -> p b n", n=P),
                                r.V[0][:, 3 * c:3 * c + nb].bitcast(F32), ALU.subtract).then_inc(s.v_lo, 1)
                if c == 2:
                    e.tensor_tensor(r.V[1][0:64, 8], PS[0:64, bank, 256:384], r.V[0][0:64, 8].bitcast(F32),
                                    ALU.subtract).then_inc(s.v_lo, 1)

            def prepare(j, i):
                for x in CHUNKS.get(i, ()):
                    if x < 3:
                        heads_nrm(QKV[j], GQ[:, 0:1], s.q_nrm, x)
                    elif x < 6:
                        heads_nrm(QKV[4 + j], par_col("k_norm"), s.k_nrm, x - 3)
                    else:
                        v_lo(j, x - 6)
                    cnt.bc += 1
                if j == 0:
                    if i in (4, 6):
                        qk_lo(e, j, (i - 4) // 2)

            def biased(n):
                _, cols, off = keys(n)
                j = n // 9
                e.wait_ge(s.bias_ready, 2 * j + 2)
                e.wait_ge(s.s_done, n + 1)
                if n >= 2:
                    e.wait_ge(s.t_done, CUM[n - 1])
                for h in range(2):
                    m = 2 * (n % 2) + h
                    e.tensor_tensor_reduce(
                        out=SS[n % 2][:, h, 0:cols], in0=PS[:, 2 * h:2 * h + 2].rearrange("p a b -> p (a b)")[:, 0:cols],
                        in1=BIAS[j % 2][:, h, off:off + cols], scale=1.0, scalar=3e38, op0=ALU.add, op1=ALU.min,
                        accum_out=MIN[:, m:m + 1]).then_inc(s.ttr_done, 1)

            def normalise(n):
                _, cols, _ = keys(n)
                m = 2 * (n % 2)
                e.wait_ge(s.exp_done, 2 * n + 2)
                if n >= 2:
                    e.wait_ge(s.p_ready, 2 * n - 2)
                e.reciprocal(REC[:, m:m + 2], SUM[:, m:m + 2]).then_inc(s.rec_done, 1)
                e.wait_ge(s.rec_done, n + 1)
                for h in range(2):
                    e.tensor_scalar(SS[n % 2][:, h, 0:cols], SS[n % 2][:, h, 0:cols], REC[:, m + h:m + h + 1], None,
                                    ALU.mult).then_inc(s.p_ready, 1)

            def pt_lo(n):
                for p in range(pieces(n)):
                    rows, w = piece(n, p)
                    e.wait_ge(s.pt_hi, CUM[n] + p + 1)
                    e.tensor_tensor(pt_piece(1, n, p), PS[0:rows, 4 + p, 0:w], pt_piece(0, n, p).bitcast(F32),
                                    ALU.subtract).then_inc(s.pt_lo, 1)

            e.wait_ge(s.g_sum, 3)
            e.wait_ge(s.stat_done, 14)
            for i in range(2, 6):
                e.memset(y(i)[:, TOK:T], 0.0).then_inc(s.pad_ready, 1)
            e.wait_ge(s.gq_ready, 2)
            def o_add(i):
                e.wait_ge(s.o_sq, i + 1)
                e.wait_ge(s.o_sum, i - 1)
                e.tensor_tensor(OS[0][:, :], OS[0][:, :], OS[1][:, :], ALU.add).then_inc(s.o_sum, 1)

            def b_lo(n, k):
                e.wait_ge(s.b_hi, n + 1)
                sl = slice(k * T, (k + 1) * T)
                e.tensor_tensor(B[1][:, sl], y(k), B[0][:, sl].bitcast(F32), ALU.subtract).then_inc(s.b_lo, 1)

            def o_norm(i):
                e.scalar_tensor_tensor(y(2 + i), y(2 + i), par_col("out_norm", 2 + i), RSTD[:, :],
                                       ALU.mult, ALU.mult).then_inc(s.o_nrm, 1)

            def ya_norm(chunks):
                for c in chunks:
                    lo, hi, _ = BC[c]
                    e.wait_ge(s.bc_done, cnt.bc + 1)
                    for h in range(2):
                        ins = e.scalar_tensor_tensor(y(h)[:, lo:hi], y(h)[:, lo:hi], par_col("out_norm", h),
                                                     PS[:, 6 if c == 1 else 7, 0:hi - lo], ALU.mult, ALU.mult)
                    ins.then_inc(s.bc_used, 1)
                    cnt.bc += 1

            for i in range(7):
                prepare(0, i)
            e.wait_ge(s.ya_done, 2)
            biased(0)
            normalise(0)
            for n in range(N_U):
                if n + 1 < N_U:
                    biased(n + 1)
                pt_lo(n)
                if n + 1 < N_U:
                    normalise(n + 1)
                if n == 1:
                    cache_lo(e, 0)
                if n < 27:
                    prepare(n // 9 + 1, n % 9)
                if n == 27:
                    ya_norm((0, 1))
                if n == 28:
                    ya_norm((2,))
                if n == 29:
                    o_add(1)
                if n == 30:
                    b_lo(0, 6)
                if n == 31:
                    b_lo(1, 7)
                if n == 32:
                    o_add(2)
                if n in (33, 34):
                    dve_split2(e, S_OUT + n - 33, n - 33)

            b_lo(2, 0)
            b_lo(3, 1)
            o_add(3)
            cnt.other = 36
            dve_recip(e, cnt)
            cnt.bc += 3
            e.wait_ge(s.bc_used, cnt.used(cnt.bc))
            o_norm(0)
            for i in range(4):
                if i < 3:
                    o_norm(i + 1)
                e.wait_ge(s.o_nrm, i + 1)
                b_lo(4 + i, 2 + i)
            for par in range(2):
                dve_split(e, S_OUT + 2 + par, par)
            e.wait_ge(s.o_nrm, 4)
            e.memset(ACC[:, :], 0.0).then_inc(s.acc_zero, 1)

            def residual(t0, i, par, norm, src_in, acc0):
                m = i * 2 + par
                e.wait_ge(s.tile_done, m + (t0 + 1))
                e.wait_ge(src_in, m * 16 + 16)
                ym = Y[:, bass.ds(m * T, T)]
                e.tensor_tensor(chunks(ym), ps_tile(par), chunks(ym), ALU.add).then_inc(s.tile_read, 1)
                e.wait_ge(s.a_hi, m + (acc0 + 1))
                e.wait_ge(s.tile_read, m + (t0 + 1))
                e.scalar_tensor_tensor(A[1][:, bass.ds(m * T, T)], ym, PAR[:, bass.ds(m + _cols[norm], 1)],
                                       A[0][:, bass.ds(m * T, T)].bitcast(F32), ALU.mult, ALU.subtract)\
                    .then_inc(s.a_lo, 1)
                e.wait_ge(s.sq_done, m + (acc0 + 1))
                e.wait_ge(s.acc_done, m + acc0)
                e.tensor_tensor(ACC[:, :], ACC[:, :], TT[:, :], ALU.add).then_inc(s.acc_done, 1)

            e.wait_ge(s.acc_zero, 1)
            for par in range(2):
                residual(S_OUT, 0, par, "norm_x", s.x2_in, 8)
            with e.Fori(1, 4) as i:
                for par in range(2):
                    residual(S_OUT, i, par, "norm_x", s.x2_in, 8)
                    dve_split(e, i * 2 + (S_OUT + 2 + par), par)

            def xevac(i):
                e.wait_ge(s.tile_done, S_XQ + i + 1)
                e.wait_ge(s.y1_out, 16 * (i + 1))
                e.wait_ge(s.sq_done, 16)
                e.wait_ge(s.a_lo, 16)
                e.tensor_tensor(chunks(y(i)), ps_tile(i % 2), chunks(RSTD[:, :]), ALU.mult).then_inc(s.tile_read, 1)

            def xq_nrm(h, chunks):
                e.wait_ge(s.xs_sq, 2 * h + 2)
                for c in chunks:
                    lo, hi, _ = BC[c]
                    e.wait_ge(s.bc_done, cnt.bc + 1)
                    if c == 0:
                        e.wait_ge(s.tile_read, S_XQ + 2 * h + 2)
                    for k in range(2):
                        ins = e.scalar_tensor_tensor(y(2 * h + k)[:, lo:hi], y(2 * h + k)[:, lo:hi],
                                                     GQ[:, 1 + k:2 + k], PS[:, 6 if c == 1 else 7, 0:hi - lo],
                                                     ALU.mult, ALU.mult)
                    ins.then_inc(s.bc_used, 1)
                    cnt.bc += 1

            def xmin(u):
                nb = xblocks(u)
                m = 2 * (u % 2)
                e.wait_ge(s.x_s, u + 1)
                if u >= 2:
                    e.wait_ge(s.x_exp, xexps(u - 1))
                e.tensor_reduce(MIN[:, m:m + nb], PS[:, u % 2, 0:nb * NMEM].rearrange("p (b k) -> p b k", k=NMEM),
                                AX.X, ALU.min).then_inc(s.x_min, 1)

            def xnorm(u):
                nb = xblocks(u)
                m = 2 * (u % 2)
                e.wait_ge(s.x_exp, xexps(u + 1))
                if u >= 2:
                    e.wait_ge(s.x_p, u - 1)
                e.reciprocal(REC[:, m:m + nb], SUM[:, m:m + nb]).then_inc(s.x_rec, 1)
                e.wait_ge(s.x_rec, u + 1)
                e.tensor_tensor(XS[:, u % 2, 0:nb], XS[:, u % 2, 0:nb],
                                REC[:, m:m + nb].unsqueeze(2).to_broadcast([P, nb, NMEM]), ALU.mult)\
                    .then_inc(s.x_p, 1)

            dve_recip(e, cnt)
            cnt.bc += 3
            e.wait_ge(s.bc_used, cnt.used(cnt.bc))
            for i in range(8):
                if i < 6:
                    dve_split(e, S_XQ + i + 2, i % 2)
                xevac(i)
                h = i // 2
                if i % 2:
                    if h == 3:
                        xmin(0)
                        xmin(1)
                        xnorm(0)
                    if h:
                        xq_nrm(h - 1, (0, 1))
                    e.wait_ge(s.xs_sq, 2 * h + 2)
                    e.tensor_tensor(XSQ[0][:, :], XSQ[0][:, :], XSQ[1][:, :], ALU.add).then_inc(s.xs_sum, 1)
                if i % 2 == 0 and i:
                    if i > 2:
                        xq_nrm(i // 2 - 2, (2,))
                    dve_recip(e, cnt)
                if i in (5, 6):
                    x_lo_part(e, 0, 2 * i - 10)
                    x_lo_part(e, 0, 2 * i - 9)

            def xpt_lo(q):
                w = 512 if q % 3 < 2 else P
                k = 2 + 2 * (q % 2)
                e.wait_ge(s.x_pthi, q + 1)
                e.tensor_tensor(XPT[1][:, :, 0:w], PS[:, k:k + 2, 0:w], XPT[0][:, :, 0:w].bitcast(F32),
                                ALU.subtract).then_inc(s.x_ptlo, 1)

            def xo_lo(q):
                h, g = divmod(q, 3)
                for d in range(2):
                    lo, c, w = (512 * g, 0, 512) if g < 2 else (SEQ, 64, 64)
                    col = (2 * h + d) * T + lo
                    e.wait_ge(s.x_ohi, 2 * q + d + 1)
                    e.tensor_tensor(B[1][:, col:col + w], PS[:, 6 + d, c:c + w], B[0][:, col:col + w].bitcast(F32),
                                    ALU.subtract).then_inc(s.x_olo, 1)

            xq_nrm(2, (2,))
            done = None
            for u in range(N_XU):
                if u + 1 < N_XU:
                    xnorm(u + 1)
                if u + 2 < N_XU:
                    xmin(u + 2)
                q, last = xgroup(u)
                if last:
                    xpt_lo(q)
                if done is not None:
                    xo_lo(done)
                done = q if last else None
                if u == 3:
                    dve_recip(e, cnt)
                    xq_nrm(3, (0, 1, 2))
                if u == 8:
                    for X in B:
                        e.wait_ge(s.stat_done, N_STAT_X + 4)
                        e.wait_ge(s.xs_sum, 4)
                        e.wait_ge(s.x_pv, 3)
                        e.memset(X[:, :].bitcast(F32).rearrange("p (k t) -> p k t", t=T)[:, :, TOK:T], 0.0)\
                            .then_inc(s.o_pad, 1)
                if u in (18, 19):
                    dve_split2(e, S_XO + u - 18, u - 18)
            xo_lo(done)

            for par in range(2):
                dve_split(e, S_XO + 2 + par, par)
            e.wait_ge(s.tile_read, S_XO)
            e.memset(ACC[:, :], 0.0).then_inc(s.acc_zero, 1)
            e.wait_ge(s.acc_zero, 2)
            for par in range(2):
                residual(S_XO, 0, par, "norm_ff", s.y1_in, 16)
            with e.Fori(1, 4) as i:
                for par in range(2):
                    residual(S_XO, i, par, "norm_ff", s.y1_in, 16)
                    dve_split(e, i * 2 + (S_XO + 2 + par), par)

            def relu(t, j, h0):
                e.wait_ge(s.tile_done, t + 1)
                e.wait_ge(s.h_lo, h0 + j)
                e.wait_ge(s.tile_read, t)
                e.scalar_tensor_tensor(chunks(HID[:, :]), ps_tile(j % 2), 0.0, chunks(RSTD[:, :]),
                                       ALU.max, ALU.mult).then_inc(s.tile_read, 1)

            def hidden_lo(h0, j, slot):
                e.wait_ge(s.h_hi, h0 + (j + 1))
                col = (slot + j) * T
                e.tensor_tensor(B[1][:, col:col + T], HID[:, :], B[0][:, col:col + T].bitcast(F32), ALU.subtract)\
                    .then_inc(s.h_lo, 1)

            def down(g, j):
                for k in range(2):
                    m = 2 * j + k
                    e.wait_ge(s.tile_done, td(g) + (m + 1))
                    e.wait_ge(s.tile_read, td(g) + m)
                    e.tensor_tensor(chunks(y(m)), ps_tile(k), chunks(y(m)), ALU.add).then_inc(s.tile_read, 1)
                    if k == 0:
                        continue
                    if not isinstance(g, int) or g < N_G - 1 or j < 2:
                        dve_split(e, sd(g) + (j + 2), j % 2)

            def mlp_group(g, half):
                if not isinstance(g, int) or g < N_G - 1:
                    for j in range(4):
                        relu(tu(g) + j, j, g * 4 + 4)
                        dve_split(e, su(g) + (j + 2), j % 2)
                        hidden_lo(g * 4 + 4, j, 4 * (1 - half))
                for j in range(4):
                    down(g, j)

            dve_recip(e, cnt)
            cnt.bc += 3
            e.wait_ge(s.bc_used, cnt.used(cnt.bc))
            for j in range(4):
                relu(S_UP + j, j, 0)
                dve_split(e, S_UP + j + 2, j % 2)
                hidden_lo(0, j, 0)
            with e.Fori(0, 3) as i:
                mlp_group(i * 2, 0)
                mlp_group(i * 2 + 1, 1)
            mlp_group(6, 0)
            mlp_group(7, 1)

        @block.tensor
        def _(e):
            cnt = Count()
            e.wait_ge(s.const_ready, 6)

            def mem_tile(par, first=False):
                for k in range(KT):
                    if first:
                        e.wait_ge(s.mem_lo, k + 1)
                    for m, (wt, xt) in enumerate(((WH, MX[0]), (WH, MX[1]), (WL, MX[0]))):
                        ins = e.matmul(PS[:, 3 * par, 0:NMEM], wt[:, par, k * P:(k + 1) * P],
                                       xt[:, k * NMEM:(k + 1) * NMEM],
                                       start=(k == 0 and m == 0), stop=(k == KT - 1 and m == 2))
                ins.then_inc(s.tile_done, 1)

            e.wait_ge(s.w_lo, 1)
            mem_tile(0, first=True)
            e.wait_ge(s.mem_sum, 1)
            for b in range(2):
                ins = e.matmul(PS[:, 6, 2 * b:2 * b + 2], MSUM[:, b * P:(b + 1) * P], ONE[:, :], start=True, stop=True)
            ins.then_inc(s.stat_done, 1)
            cnt.stat += 1
            e.wait_ge(s.ck_rc, 1)
            for b in range(2):
                ins = e.transpose(PS[:, 7, b * P:(b + 1) * P], CKC[:, b:b + 1].to_broadcast([P, P]), ID[:, :])
            ins.then_inc(s.bc_done, 1)
            cnt.bc += 1
            e.wait_ge(s.w_lo, 2)
            mem_tile(1)
            with e.Fori(1, 8) as i:
                for par in range(2):
                    e.wait_ge(s.w_lo, i * 2 + par + 1)
                    e.wait_ge(s.tile_read, i * 2 + par - 1)
                    mem_tile(par)

            def win_tile(i):
                e.wait_ge(s.w_lo, S_IN + i + 1)
                e.wait_ge(s.tile_read, S_IN + i - 1)
                pe_tile(e, i % 2, i % 2, A, kwait=(lambda k: e.wait_ge(s.a_lo, k + 1)) if i == 0 else None)

            def rc_wait(n):
                return lambda: e.wait_ge(s.rc_done, n)

            def crc(b):
                return CRC[:, b:b + 1].to_broadcast([P, P])

            win_tile(0)
            e.wait_ge(s.acc_done, 8)
            pe_stat(e, cnt, (ACC[:, :],), ONE, cnt.bc)
            pe_bcast(e, cnt, crc, rc_wait(1))
            e.wait_ge(s.kq_sq, 1)
            e.wait_ge(s.bc_used, cnt.bc)
            for h in range(4):
                for b in range(2):
                    c = 2 * (2 * h + b)
                    for k in range(2):
                        ins = e.matmul(PS[:, 6, c:c + 2], MSQ[:, 2 * h + k, b * P:(b + 1) * P], ONE[:, :],
                                       start=(k == 0), stop=(k == 1))
            ins.then_inc(s.stat_done, 1)
            cnt.stat += 1
            win_tile(1)
            e.wait_ge(s.ck_rc, 2)
            e.wait_ge(s.stat_read, cnt.stat)
            for h in range(4):
                for b in range(2):
                    c = 2 * h + b
                    ins = e.transpose(PS[:, 6 + h // 2, (c % 4) * P:(c % 4 + 1) * P],
                                      CKC[:, c:c + 1].to_broadcast([P, P]), ID[:, :])
                if h % 2:
                    ins.then_inc(s.mk_bc, 1)
            win_tile(2)
            for n in range(4):
                if n < 2:
                    e.wait_ge(s.mk_norm, 4 * n + 4)
                else:
                    e.wait_ge(s.mv_cp, n - 1)
                for f in range(4):
                    ins = e.transpose(PS[:, 6 + n % 2, f * P:(f + 1) * P],
                                      KV[:, 8 + 4 * (n % 2) + f, (n // 2) * P:(n // 2 + 1) * P], ID[:, :])
                ins.then_inc(s.mv_tr, 1)
            n_rc = 1
            for i in range(3, 22):
                win_tile(i)
                if i == 4:
                    e.wait_ge(s.mv_cp, 4)
                if i == 11:
                    e.wait_ge(s.g_sum, 1)
                    pe_stat(e, cnt, (TT[:, :],), ONE, cnt.bc)
                if 12 <= i <= 19:
                    j = i - 12
                    e.wait_ge(s.qk_sq, j + 1)
                    pe_stat(e, cnt, (TT[:, :],), SEL, cnt.bc)
                if i == 12:
                    n_rc += 1
                    pe_bcast(e, cnt, crc, rc_wait(n_rc))
                if i == 19:
                    e.wait_ge(s.conv_step, 64)
                    pe_stat(e, cnt, (y(0), y(1)), ONE, cnt.bc)
                    st = cnt.stat
                    pe_bcast(e, cnt, lambda b: CRT[:, b:b + 1].to_broadcast([P, P]), lambda: e.wait_ge(s.stat_read, st))
                if i == 20:
                    e.wait_ge(s.g_sum, 2)
                    pe_stat(e, cnt, (TT[:, :],), ONE, cnt.bc)
                    n_rc += 1
                    pe_bcast(e, cnt, crc, rc_wait(n_rc))
                if i == 21:
                    e.wait_ge(s.g_sum, 3)
                    pe_stat(e, cnt, (TT[:, :],), ONE, cnt.bc)
                    n_rc += 1

            def prepare(j, x):
                which, c = divmod(x, 3)
                used(cnt.bc - (0, 2, 1)[c])
                if j == 0 and x == 1:
                    e.wait_ge(s.stat_read, cnt.stat)
                if which < 2:
                    e.wait_ge(s.rx_ready, 2 * j + which + 1)
                    for b in BC[c][2]:
                        t0 = BLK[b] - BC[c][0]
                        rx = RX0 if j == which == 0 else RX
                        ins = e.transpose(PS[:, 6 if c == 1 else 7, t0:t0 + P], rx[:, b].rearrange("p e d -> p (e d)"),
                                          ID[:, :])
                else:
                    for b in range(3 * c, 3 * c + 3):
                        w = P if b < 8 else 64
                        ins = e.transpose(PS[0:w, 6 if c == 1 else 7, (b % 3) * P:(b % 3 + 1) * P],
                                          QKV[8 + j][:, b * P:b * P + w], ID[:, :])
                ins.then_inc(s.bc_done, 1)
                cnt.bc += 1

            def scores(n):
                j, b = divmod(n, 9)
                r = AT[j % 2]
                tiles, cols, _ = keys(n)
                if b == 0:
                    e.wait_ge(s.qk2_lo, 2 * j + 2)
                if b == 8:
                    e.wait_ge(s.kc_lo, 2 * j + 2)
                if n:
                    e.wait_ge(s.ttr_done, 2 * n)
                q0 = P * b if b < 8 else TOK - P
                if b < 8:
                    k0 = P * max(0, b - 4)
                    parts = [(r.K, k0, min(512, cols), 0)] + ([(r.K, k0 + 512, cols - 512, 1)] if cols > 512 else [])
                else:
                    parts = [(r.KC, 0, 512, 0), (r.K, SEQ, 64, 1)]
                for K, k0, w, bank in parts:
                    for m, (qx, kx) in enumerate(((0, 0), (1, 0), (0, 1))):
                        for h in range(2):
                            rows = slice(64 * h, 64 * h + 64)
                            ins = e.matmul(PS[:, 2 * h + bank, 0:w], r.Q[qx][rows, q0:q0 + P], K[kx][rows, k0:k0 + w],
                                           start=(m == 0), stop=(m == 2))
                ins.then_inc(s.s_done, 1)

            def transposes(n):
                tiles, cols, _ = keys(n)
                if n:
                    e.wait_ge(s.pt_lo, CUM[n])
                for p in range(pieces(n)):
                    if p == 2 and CHUNKS.get((n - 1) % 9, (0,))[-1] % 3 == 1 and n - 1 < 27:
                        used(cnt.bc)
                    for h in range(2):
                        e.wait_ge(s.p_ready, 2 * n + h + 1)
                        for kt in range(2 * p, min(2 * p + 2, tiles)):
                            w = min(P, cols - kt * P)
                            t0 = (kt % 2) * 256 + h * P
                            ins = e.transpose(PS[0:w, 4 + p, t0:t0 + P], SS[n % 2][:, h, kt * P:kt * P + w], ID[:, :])
                    ins.then_inc(s.t_done, 1)

            def values(n):
                j, b = divmod(n, 9)
                r = AT[j % 2]
                tiles, cols, _ = keys(n)
                if b == 0:
                    e.wait_ge(s.v_lo, 4 * j + 4)
                if n:
                    e.wait_ge(s.o_used, 2 * n)
                for kt in range(tiles):
                    if kt % 2 == 0:
                        e.wait_ge(s.pt_lo, CUM[n] + kt // 2 + 1)
                    w = min(P, cols - kt * P)
                    for m, (vx, px) in enumerate(((0, 0), (0, 1), (1, 0))):
                        if b < 8:
                            lhs = r.V[vx][:, max(0, b - 4) + kt]
                        else:
                            lhs = r.VC[vx][:, kt] if kt < 4 else r.V[vx][0:w, 8]
                        rhs = PT[n % 2][px][0:w, kt] if kt < 4 else PT5[n % 2][px][0:w, :]
                        ins = e.matmul(PS[:, 7, 0:256], lhs, rhs,
                                       start=(kt == 0 and m == 0), stop=(kt == tiles - 1 and m == 2))
                ins.then_inc(s.pv_done, 1)

            def used(n):
                k = n - N_ACT_BC
                if k <= 0:
                    e.wait_ge(s.bc_used, n)
                    return
                j, k = divmod(k, 9)
                if k == 0:
                    j, k = j - 1, 9
                if k <= 3:
                    e.wait_ge(s.q_nrm, 3 * j + k)
                elif k <= 6:
                    e.wait_ge(s.k_nrm, 3 * j + k - 3)
                else:
                    e.wait_ge(s.v_lo, 4 * j + k - 6 + (k == 9))
            N_ACT_BC = cnt.bc
            for x in range(9):
                prepare(0, x)
            e.wait_ge(s.tile_read, S_OUT)
            scores(0)
            scores(1)
            for n in range(N_U):
                transposes(n)
                if n in (28, 29):
                    e.wait_ge(s.bc_used, cnt.used(cnt.bc))
                if n and n - 1 < 27 and (n - 1) % 9 in CHUNKS:
                    used(cnt.bc)
                if n:
                    values(n - 1)
                if n + 2 < N_U:
                    scores(n + 2)
                for x in CHUNKS.get(n % 9, ()) if n < 27 else ():
                    if x % 3 == 1:
                        e.wait_ge(s.pt_lo, CUM[n + 1])
                    else:
                        e.wait_ge(s.o_used, 2 * n)
                    prepare(n // 9 + 1, x)
                if n in (27, 28):
                    cnt.other = 36
                    e.wait_ge(s.o_used, 2 * n)
                    e.wait_ge(s.pt_lo, CUM[n + 1])
                    pe_bcast(e, cnt, crc, rc_wait(n_rc), chunks=(0, 1) if n == 27 else (2,))
            values(N_U - 1)

            order = K_AC + K_O

            def out_part(i, ks):
                e.wait_ge(s.w_lo, S_OUT + i + 1)
                pe_part(e, i, i, B, ks, W=W2, first=ks[0] == order[0], last=ks[-1] == order[-1],
                        kwait=lambda k: e.wait_ge(s.b_lo, order.index(k) + 1))

            out_part(0, K_AC)
            e.wait_ge(s.o_sum, 3)
            pe_stat(e, cnt, (OS[0][:, :],), ONE, 0)
            n_rc += 1
            out_part(1, K_AC[0:2])
            e.wait_ge(s.o_used, 2 * N_U)
            pe_bcast(e, cnt, crc, rc_wait(n_rc))
            out_part(1, K_AC[2:4])
            for k in K_O:
                out_part(0, (k,))
                out_part(1, (k,))
            with e.Fori(1, 4) as i:
                for par in range(2):
                    e.wait_ge(s.w_lo, i * 2 + (S_OUT + par + 1))
                    e.wait_ge(s.tile_read, i * 2 + (S_OUT + par - 1))
                    pe_tile(e, par, par, B)

            def xq_tile(i):
                e.wait_ge(s.w_lo, S_XQ + i + 1)
                e.wait_ge(s.tile_read, S_XQ + i - 1)
                pe_tile(e, i % 2, i % 2, A, kwait=(lambda k: e.wait_ge(s.a_lo, 9 + k)) if i == 0 else None)

            def xq_stat(h):
                e.wait_ge(s.xs_sum, h + 1)
                pe_stat(e, cnt, (XSQ[0][:, :],), ONE, cnt.used(cnt.bc - 1))

            xq_tile(0)
            e.wait_ge(s.acc_done, 16)
            pe_stat(e, cnt, (ACC[:, :],), ONE, cnt.used(cnt.bc))
            assert cnt.stat == N_STAT_X, cnt.stat
            n_rc += 1
            pe_bcast(e, cnt, crc, rc_wait(n_rc))
            xq_tile(1)
            for h in range(3):
                xq_tile(2 * h + 2)
                if h:
                    pe_bcast(e, cnt, crc, chunks=(2,))
                xq_stat(h)
                xq_tile(2 * h + 3)
                n_rc += 1
                pe_bcast(e, cnt, crc, rc_wait(n_rc), chunks=(0, 1))

            def xscores(u):
                h, p = divmod(u, 5)
                r = CX[h]
                kk = 0 if p < 4 else 2
                if p == 0:
                    e.wait_ge(s.xq_lo, 2 * h + 2)
                    e.wait_ge(s.xkv_lo, 2 * h + 1)
                if p == 4:
                    e.wait_ge(s.xkv_lo, 2 * h + 2)
                if u >= 2:
                    e.wait_ge(s.x_exp, xexps(u - 1))
                for b in range(xblocks(u)):
                    q0 = P * (2 * p + b) if p < 4 else TOK - P
                    steps = [(k, qx, kx) for k in range(2) for qx, kx in ((0, 0), (1, 0), (0, 1))]
                    for n, (k, qx, kx) in enumerate(steps):
                        ins = e.matmul(PS[:, u % 2, b * NMEM:(b + 1) * NMEM], r.Q[qx][:, k * T + q0:k * T + q0 + P],
                                       r.KV[kx][:, kk, k * NMEM:(k + 1) * NMEM], start=(n == 0), stop=(n == 5))
                ins.then_inc(s.x_s, 1)

            def xtransposes(u):
                q, _ = xgroup(u)
                e.wait_ge(s.x_p, u + 1)
                if q >= 2:
                    e.wait_ge(s.x_ptlo, q - 1)
                for b in range(xblocks(u)):
                    c = (u % 5 % 2) * 2 + b if u % 5 < 4 else 0
                    for k in range(2):
                        ins = e.transpose(PS[:, 2 + 2 * (q % 2) + k, c * P:(c + 1) * P],
                                          XS[:, u % 2, b, k * P:(k + 1) * P], ID[:, :])
                ins.then_inc(s.x_t, 1)

            def xvalues(q):
                h, g = divmod(q, 3)
                r = CX[h]
                vv = 1 if g < 2 else 3
                w = 512 if g < 2 else P
                e.wait_ge(s.x_ptlo, q + 1)
                if q:
                    e.wait_ge(s.x_olo, 2 * q)
                if q < 2:
                    e.wait_ge(s.bc_used, cnt.used(cnt.bc))
                    e.wait_ge(s.stat_read, cnt.stat)
                for d in range(2):
                    steps = [(k, vx, px) for k in range(2) for vx, px in ((0, 0), (0, 1), (1, 0))]
                    for n, (k, vx, px) in enumerate(steps):
                        v0 = k * NMEM + d * P
                        ins = e.matmul(PS[:, 6 + d, 0:w], r.KV[vx][:, vv, v0:v0 + P], XPT[px][:, k, 0:w],
                                       start=(n == 0), stop=(n == 5))
                ins.then_inc(s.x_pv, 1)

            e.wait_ge(s.tile_read, S_XO - 1)
            xscores(0)
            xscores(1)
            e.wait_ge(s.tile_read, S_XO)
            pe_bcast(e, cnt, crc, chunks=(2,))
            done = None
            for u in range(N_XU):
                xtransposes(u)
                if u + 2 < N_XU:
                    xscores(u + 2)
                if done is not None:
                    xvalues(done)
                if u == 0:
                    xq_stat(3)
                if u == 3:
                    e.wait_ge(s.x_olo, 2)
                    n_rc += 1
                    pe_bcast(e, cnt, crc, rc_wait(n_rc))
                q, last = xgroup(u)
                done = q if last else None
            xvalues(done)

            e.wait_ge(s.x_olo, 18)
            e.wait_ge(s.o_pad, 2)
            e.wait_ge(s.x_exp, xexps(N_XU))
            for i in range(2):
                if i:
                    e.wait_ge(s.x_ptlo, N_XQ)
                e.wait_ge(s.w_lo, S_XO + i + 1)
                pe_part(e, i, i, B, range(6), W=W2, last=False)
            e.wait_ge(s.x_olo, 2 * N_XQ)
            for i in range(2):
                pe_part(e, i, i, B, (6, 7), W=W2, first=False)
            with e.Fori(1, 4) as i:
                for par in range(2):
                    e.wait_ge(s.w_lo, i * 2 + (S_XO + par + 1))
                    e.wait_ge(s.tile_read, i * 2 + (S_XO + par - 1))
                    pe_tile(e, par, par, B)

            def up(t, sl, j, kwait=None):
                e.wait_ge(s.w_lo, sl + (j + 1))
                e.wait_ge(s.tile_read, t + (j - 1))
                pe_tile(e, j % 2, j % 2, A, kwait=kwait)

            def mlp_group(g, half):
                if not isinstance(g, int) or g < N_G - 1:
                    for j in range(4):
                        up(tu(g), su(g), j)
                e.wait_ge(s.h_lo, g * 4 + 4)
                for j in range(4):
                    for k in range(2):
                        e.wait_ge(s.w_lo, sd(g) + (j + 1))
                        e.wait_ge(s.tile_read, td(g) + (2 * j + k - 1))
                        pe_tile(e, k, j % 2, B, nk=4, k0=4 * half, woff=512 * k)

            up(S_UP, S_UP, 0, kwait=lambda k: e.wait_ge(s.a_lo, 17 + k))
            e.wait_ge(s.acc_done, 24)
            pe_stat(e, cnt, (ACC[:, :],), ONE, cnt.used(cnt.bc))
            n_rc += 1
            pe_bcast(e, cnt, crc, rc_wait(n_rc))
            for j in range(1, 4):
                up(S_UP, S_UP, j)
            with e.Fori(0, 3) as i:
                mlp_group(i * 2, 0)
                mlp_group(i * 2 + 1, 1)
            mlp_group(6, 0)
            mlp_group(7, 1)


_INS = ["xT", "memT", "slabs", "params", "rbrev", "ctxa", "ctxc", "kcT", "vc", "mkcT", "mvc"]
_OUTS = {"o_y": (KT, P, T), "o_ca": (2, 2, P, CA), "o_cc": (2, 2, P, CC), "o_k": (4, P, 576), "o_v": (4, P, 576),
         "o_kc": (4, P, 448), "o_vc": (448, 512), "o_mk": (KT, P, NMEM), "o_mv": (2, P, D)}


def layout(inp):
    f = lambda n: np.asarray(inp[n])
    xT = np.zeros((D, T), np.float32)
    xT[:, :SEQ] = f("x_prompt")[0].T
    xT[:, SEQ:TOK] = f("x_sample")[0].T

    def k1024(w):
        return w.reshape(KT, P, -1, P).transpose(2, 1, 0, 3).reshape(-1, P, D)

    up = k1024(f("w_up")[0])
    down = f("w_down")[0].reshape(N_G, 4, P, 4, 2, P).transpose(0, 3, 2, 4, 1, 5).reshape(N_G, 4, P, D)
    mlp = [up[0:4]]
    for g in range(N_G):
        if g + 1 < N_G:
            mlp.append(up[4 * g + 4:4 * g + 8])
        mlp.append(down[g])
    slabs = np.concatenate([k1024(f("w_xk")[0]), k1024(f("w_xv")[0]), k1024(f("w_in")[0])[IN_ORDER],
                            k1024(f("w_out")[0]), k1024(f("w_xq")[0]), k1024(f("w_xo")[0])] + mlp)

    def cols(v):
        return v.reshape(-1, P).T
    par = np.concatenate([
        cols(f("norm_mix")[0]), cols(f("norm_x")[0]), cols(f("norm_ff")[0]), cols(f("norm_mem")[0]),
        cols(f("out_norm")[0]), cols(f("ln_a_g")[0]), cols(f("ln_a_b")[0]), cols(f("conv_a_b")[0]),
        cols(f("conv_a_w")[0]), cols(f("conv_c_w")[0]), cols(np.tile(f("q_norm")[0], 2)),
        cols(np.tile(f("k_norm")[0], 2)), cols(f("xq_norm")[0]), cols(f("xk_norm")[0])], axis=1)
    a = {
        "xT": xT.reshape(KT, P, T), "memT": f("mem_prompt")[0].T.reshape(KT, P, NMEM), "slabs": slabs, "params": par,
        "rbrev": f("rel_bias")[0][:, ::-1],
        "ctxa": f("cache_conv_a")[0, 0].T.reshape(2, P, CA), "ctxc": f("cache_conv_c")[0, 0].T.reshape(2, P, CC),
        "kcT": f("cache_band_k")[0, 0].reshape(512, 512).T.reshape(4, P, 512),
        "vc": f("cache_band_v")[0, 0].reshape(4, P, 512),
        "mkcT": f("cache_mem_k")[0, 0].reshape(NMEM, D).T.reshape(KT, P, NMEM),
        "mvc": f("cache_mem_v")[0, 0].reshape(2, P, D)}
    return {n: np.ascontiguousarray(v) for n, v in a.items()}


def returned(o):
    yT = o["o_y"].reshape(D, T)
    ca = o["o_ca"].reshape(2, 256, CA).transpose(0, 2, 1)
    cc = o["o_cc"].reshape(2, 256, CC).transpose(0, 2, 1)
    kn, vn = (o[n].reshape(512, 576).T for n in ("o_k", "o_v"))
    kc, vc = o["o_kc"].reshape(512, 448).T, o["o_vc"]
    band = lambda a: a.reshape(1, 1, -1, 8, 64)
    c = np.ascontiguousarray
    return tuple(c(x) for x in (
        yT[:, :SEQ].T[None], yT[:, SEQ:TOK].T[None], ca[0][None, None], band(kn[:512]), band(vn[:512]), cc[0][None, None],
        o["o_mk"].reshape(D, NMEM).T.reshape(1, 1, NMEM, 4, 256), o["o_mv"].reshape(1, 1, NMEM, 4, 256),
        ca[1][None, None], band(np.concatenate([kc, kn[512:]])), band(np.concatenate([vc, vn[512:]])), cc[1][None, None]))


def kernel(**inputs):
    import concourse.bacc as bacc
    from concourse.bass_utils import run_bass_kernel_spmd

    nc = bacc.Bacc("TRN2", target_bir_lowering=False, num_devices=1)
    arrays = layout(inputs)
    args = [nc.dram_tensor(n, arrays[n].shape, F32, kind="ExternalInput").ap() for n in _INS]
    args += [nc.dram_tensor(n, shape, F32, kind="ExternalOutput").ap() for n, shape in _OUTS.items()]
    build(nc, *args)
    r = run_bass_kernel_spmd(nc, [arrays], core_ids=[0])
    return returned({n: np.asarray(r.results[0][n]) for n in _OUTS})
```
